# Optimizing a Trainium2 kernel written in Bass

```python
import jax, jax.numpy as jnp
from jax import lax
import numpy as np
import math

D_MODEL = 2048
BATCH = 1
SEQ = 256
DEPTH = 1

CHUNK = 64
D_BRANCH = D_MODEL // 2
HEAD_DIM = 64
RWKV_HEADS = D_BRANCH // HEAD_DIM
ATTN_HEADS = D_BRANCH // HEAD_DIM
LORA_DECAY = 64
LORA_ICLR = 64
DECAY_SCALE = 0.606531
PAST_CHUNKS = 8
PAST = PAST_CHUNKS * CHUNK
BAND = (PAST_CHUNKS + 1) * CHUNK
REL_CLIP = 256
N_BRANCH = 2
NORM_EPS = 1e-6
GN_EPS = 64e-5
IN_SIZES = (D_BRANCH,) * 8 + (D_MODEL,) * 2
D_IN = sum(IN_SIZES)


def _rms_norm(x, g):
    xf = x.astype(jnp.float32)
    y = xf * lax.rsqrt(jnp.mean(xf * xf, axis=-1, keepdims=True) + NORM_EPS)
    return (y * g.astype(jnp.float32)).astype(x.dtype)

def _shift(x):
    return jnp.pad(x, ((0, 0), (1, 0), (0, 0)))[:, :-1]

def _rwkv7_mixer(h, p_r, p_k, p_v, mu_rkv, mu_wa, w0, w1, w2, a0, a1, a2,
                 k_k, k_a, r_k, ln_x_g, ln_x_b):
    B, S, _ = h.shape
    H, N = RWKV_HEADS, HEAD_DIM
    f32 = jnp.float32
    r = p_r + (_shift(p_r) - p_r) * mu_rkv[0]
    k = p_k + (_shift(p_k) - p_k) * mu_rkv[1]
    v = p_v + (_shift(p_v) - p_v) * mu_rkv[2]
    dh = _shift(h) - h
    xw = h + dh * mu_wa[0]
    xa = h + dh * mu_wa[1]
    w = jnp.exp(-DECAY_SCALE * jax.nn.sigmoid((w0 + jnp.tanh(xw @ w1) @ w2).astype(f32)))
    a = jax.nn.sigmoid((a0 + (xa @ a1) @ a2).astype(f32))
    r = r.astype(f32)
    k = k.astype(f32)
    v = v.astype(f32)
    kk = (k * k_k.astype(f32)).reshape(B, S, H, N)
    kk = kk / jnp.maximum(jnp.sqrt(jnp.sum(kk * kk, axis=-1, keepdims=True)), 1e-12)
    k = k * (1.0 + (a - 1.0) * k_a.astype(f32))
    r4, k4, v4 = (t.reshape(B, S, H, N) for t in (r, k, v))
    w4, a4 = w.reshape(B, S, H, N), a.reshape(B, S, H, N)

    def step(state, inp):
        rt, wt, kt, vt, kkt, at = inp
        sa = jnp.einsum('bhvk,bhk->bhv', state, -kkt)
        state = (state * wt[:, :, None, :] + sa[..., None] * (kkt * at)[:, :, None, :]
                 + vt[..., :, None] * kt[..., None, :])
        yt = jnp.einsum('bhvk,bhk->bhv', state, rt)
        return state, yt

    seq_major = tuple(jnp.swapaxes(t, 0, 1) for t in (r4, w4, k4, v4, kk, a4))
    state0 = jnp.zeros((B, H, N, N), f32)
    _, y = lax.scan(step, state0, seq_major)
    y = jnp.swapaxes(y, 0, 1)
    mean = jnp.mean(y, axis=-1, keepdims=True)
    var = jnp.mean(jnp.square(y - mean), axis=-1, keepdims=True)
    y = ((y - mean) * lax.rsqrt(var + GN_EPS)).reshape(B, S, D_BRANCH)
    y = y * ln_x_g.astype(f32) + ln_x_b.astype(f32)
    bonus = jnp.sum(r4 * k4 * r_k.astype(f32), axis=-1, keepdims=True) * v4
    y = y + bonus.reshape(B, S, D_BRANCH)
    return y.astype(h.dtype)

def _chunk_band_attention(q, k, v, rel_bias):
    B, S, _ = q.shape
    H, Dh = ATTN_HEADS, HEAD_DIM
    n_chunks = S // CHUNK
    q = q.reshape(B, S, H, Dh) * (Dh ** -0.5)
    kp = jnp.pad(k.reshape(B, S, H, Dh), ((0, 0), (PAST, 0), (0, 0), (0, 0)))
    vp = jnp.pad(v.reshape(B, S, H, Dh), ((0, 0), (PAST, 0), (0, 0), (0, 0)))
    qi = jnp.arange(CHUNK)[:, None]
    kj = jnp.arange(BAND)[None, :]
    rel_idx = jnp.clip(qi - kj + PAST, -REL_CLIP, REL_CLIP) + REL_CLIP
    bias = rel_bias[:, rel_idx].astype(jnp.float32)
    key_offsets = jnp.arange(BAND) - PAST

    def one_chunk(c):
        start = c * CHUNK
        qc = lax.dynamic_slice_in_dim(q, start, CHUNK, axis=1)
        kc = lax.dynamic_slice_in_dim(kp, start, BAND, axis=1)
        vc = lax.dynamic_slice_in_dim(vp, start, BAND, axis=1)
        s = jnp.einsum('bqhd,bkhd->bhqk', qc, kc).astype(jnp.float32) + bias
        valid = (start + key_offsets) >= 0
        s = jnp.where(valid[None, None, None, :], s, jnp.float32(-1e30))
        p = jax.nn.softmax(s, axis=-1).astype(vc.dtype)
        return jnp.einsum('bhqk,bkhd->bqhd', p, vc)

    o = lax.map(one_chunk, jnp.arange(n_chunks))
    return jnp.moveaxis(o, 0, 1).reshape(B, S, H * Dh)

def first_inputs(seed: int = 0) -> dict:
    key = jax.random.key(seed)
    ks = jax.random.split(key, 24)
    L, D, DB, H, N = DEPTH, D_MODEL, D_BRANCH, RWKV_HEADS, HEAD_DIM
    nrm = lambda k, shape, s: jax.random.normal(k, shape, jnp.float32) * s
    return {
        "x": nrm(ks[0], (BATCH, SEQ, D), 1.0),
        "pre_norm_g": 1.0 + nrm(ks[1], (L, D), 0.02),
        "post_norm_g": 1.0 + nrm(ks[2], (L, D), 0.02),
        "w_in": nrm(ks[3], (L, D, D_IN), D ** -0.5),
        "mu_rkv": jax.random.uniform(ks[4], (L, 3, DB), jnp.float32),
        "mu_wa": jax.random.uniform(ks[5], (L, 2, D), jnp.float32),
        "w0": -1.5 + nrm(ks[6], (L, DB), 1.0),
        "w1": nrm(ks[7], (L, D, LORA_DECAY), D ** -0.5),
        "w2": nrm(ks[8], (L, LORA_DECAY, DB), 0.5 * LORA_DECAY ** -0.5),
        "a0": nrm(ks[9], (L, DB), 0.3),
        "a1": nrm(ks[10], (L, D, LORA_ICLR), D ** -0.5),
        "a2": nrm(ks[11], (L, LORA_ICLR, DB), 0.5 * LORA_ICLR ** -0.5),
        "k_k": 0.85 + nrm(ks[12], (L, DB), 0.02),
        "k_a": 1.0 + nrm(ks[13], (L, DB), 0.02),
        "r_k": nrm(ks[14], (L, H, N), 0.1),
        "ln_x_g": 1.0 + nrm(ks[15], (L, DB), 0.02),
        "ln_x_b": nrm(ks[16], (L, DB), 0.02),
        "rel_bias": nrm(ks[17], (L, ATTN_HEADS, 2 * REL_CLIP + 1), 0.1),
        "w_branch_rwkv": nrm(ks[18], (L, DB, D), DB ** -0.5),
        "w_branch_attn": nrm(ks[19], (L, DB, D), DB ** -0.5),
        "b_merge": nrm(ks[20], (L, N_BRANCH, D), 0.1),
        "w_out": nrm(ks[21], (L, D, D), D ** -0.5),
    }

def first_block(x, pre_norm_g, post_norm_g, w_in, mu_rkv, mu_wa, w0, w1, w2, a0, a1, a2,
              k_k, k_a, r_k, ln_x_g, ln_x_b, rel_bias, w_branch_rwkv, w_branch_attn,
              b_merge, w_out):
    split_points = np.cumsum(IN_SIZES)[:-1].tolist()
    for l in range(DEPTH):
        h = _rms_norm(x, pre_norm_g[l])
        proj = h @ w_in[l]
        p_r, p_k, p_v, z_r, q_a, k_a_att, v_a, z_a, m_r, m_a = jnp.split(
            proj, split_points, axis=-1)
        y_r = _rwkv7_mixer(h, p_r, p_k, p_v, mu_rkv[l], mu_wa[l], w0[l], w1[l], w2[l],
                           a0[l], a1[l], a2[l], k_k[l], k_a[l], r_k[l],
                           ln_x_g[l], ln_x_b[l]) * jax.nn.silu(z_r)
        y_a = _chunk_band_attention(q_a, k_a_att, v_a, rel_bias[l]) * jax.nn.silu(z_a)
        u_r = y_r @ w_branch_rwkv[l]
        u_a = y_a @ w_branch_attn[l]
        merged = (jax.nn.sigmoid(m_r + b_merge[l, 0]) * u_r
                  + jax.nn.sigmoid(m_a + b_merge[l, 1]) * u_a)
        o = merged @ w_out[l]
        x = x + _rms_norm(o, post_norm_g[l])
    return x


_first_inputs = first_inputs


def first_inputs(seed=0):
    import zlib

    import numpy as np

    out = dict(_first_inputs(seed))
    spreads = {}
    factors = {'post_norm_g': 11.184,
     'k_k': 63.073,
     'k_a': 3.233,
     'ln_x_g': 12.905,
     'ln_x_b': 12.687,
     'rel_bias': 17.086}
    for name, (base, spread) in spreads.items():
        noise = np.random.default_rng([zlib.crc32(name.encode()), seed]).standard_normal(out[name].shape)
        drawn = base * np.exp(spread * noise) if base else spread * noise
        out[name] = __import__('jax').numpy.asarray(drawn.astype(out[name].dtype))
    for name, factor in factors.items():
        out[name] = (out[name] * factor).astype(out[name].dtype)
    return out


_narrow_inputs = first_inputs


def first_inputs(seed=0):

    out = dict(_narrow_inputs(seed))
    wider = {'post_norm_g': 3.13, 'k_k': 8.6, 'ln_x_g': 3.29, 'ln_x_b': 3.29}
    for name, times in wider.items():
        mean = out[name].mean()
        out[name] = (mean + times * (out[name] - mean)).astype(out[name].dtype)
    return out


N_HEADS = 16
HEAD_DIM_2 = 128
N_KV_HEADS = 4
KV_REP = N_HEADS // N_KV_HEADS
D_ATTN = N_HEADS * HEAD_DIM_2
D_KV = N_KV_HEADS * HEAD_DIM_2
IDX_HEADS = 8
IDX_DIM = 64
TOPK_MAX = 256
Q_BLOCK = 128
SGU_CHUNK = 128
SGU_GROUPS = 16
D_SGU = D_MODEL
SGU_GROUP_DIM = D_SGU // SGU_GROUPS
D_FF = 4 * D_MODEL
REL_BUCKETS = 32
REL_MAX_DIST = 128
EPS = 1e-6
N_BRANCHES = 2
COL_SIZES = (D_ATTN, D_KV, D_KV, IDX_HEADS * IDX_DIM, IDX_DIM, IDX_HEADS,
             D_SGU, D_SGU, D_MODEL, D_MODEL)
D_IN_2 = 2 * D_ATTN // 2 + 2 * D_KV + IDX_HEADS * IDX_DIM + IDX_DIM + IDX_HEADS + 2 * D_SGU + N_BRANCHES * D_MODEL


def rms_norm(x, g):
    xf = x.astype(jnp.float32)
    y = xf * lax.rsqrt(jnp.mean(xf * xf, axis=-1, keepdims=True) + EPS)
    return (y * g.astype(jnp.float32)).astype(x.dtype)

def layer_norm(x, g, b):
    xf = x.astype(jnp.float32)
    mu = jnp.mean(xf, axis=-1, keepdims=True)
    var = jnp.mean(jnp.square(xf - mu), axis=-1, keepdims=True)
    y = (xf - mu) * lax.rsqrt(var + EPS)
    return (y * g.astype(jnp.float32) + b.astype(jnp.float32)).astype(x.dtype)

def rel_bucket(dist):
    n = jnp.maximum(dist, 0)
    max_exact = REL_BUCKETS // 2
    nf = jnp.maximum(n, 1).astype(jnp.float32)
    large = max_exact + (jnp.log(nf / max_exact) / math.log(REL_MAX_DIST / max_exact)
                         * (REL_BUCKETS - max_exact)).astype(jnp.int32)
    large = jnp.minimum(large, REL_BUCKETS - 1)
    return jnp.where(n < max_exact, n, large)

def sparse_attention(q, k, v, qi, ki, wi, rel_bias):
    B, T = q.shape[0], q.shape[1]
    L = k.shape[1]
    top_k = min(TOPK_MAX, L // 4)
    nb = T // Q_BLOCK

    def to_blocks(a):
        return a.reshape((B, nb, Q_BLOCK) + a.shape[2:]).swapaxes(0, 1)

    starts = jnp.arange(nb, dtype=jnp.int32) * Q_BLOCK
    key_pos = jnp.arange(L, dtype=jnp.int32)
    ki32 = ki.astype(jnp.float32)
    idx_scale = (IDX_HEADS ** -0.5) * (IDX_DIM ** -0.5)

    def block(args):
        qb, qib, wib, start = args
        q_pos = start + jnp.arange(Q_BLOCK, dtype=jnp.int32)
        s = jnp.einsum('bqhd,bsd->bqhs', qib.astype(jnp.float32), ki32)
        score = jnp.einsum('bqh,bqhs->bqs', wib.astype(jnp.float32) * idx_scale, jax.nn.relu(s))
        causal = key_pos[None, :] <= q_pos[:, None]
        score = jnp.where(causal[None], score, -jnp.inf)
        _, idx = lax.top_k(score, top_k)
        valid = idx <= q_pos[None, :, None]
        k_sel = jax.vmap(lambda kb, ib: kb[ib])(k, idx)
        v_sel = jax.vmap(lambda vb, ib: vb[ib])(v, idx)
        qg = qb.reshape(B, Q_BLOCK, N_KV_HEADS, KV_REP, HEAD_DIM_2)
        logits = jnp.einsum('bqgrd,bqngd->bqgrn', qg, k_sel).astype(jnp.float32) * (HEAD_DIM_2 ** -0.5)
        bucket = rel_bucket(q_pos[None, :, None] - idx)
        bias = rel_bias[bucket].astype(jnp.float32)
        bias = bias.reshape(B, Q_BLOCK, top_k, N_KV_HEADS, KV_REP).transpose(0, 1, 3, 4, 2)
        logits = jnp.where(valid[:, :, None, None, :], logits + bias, -1e30)
        p = jax.nn.softmax(logits, axis=-1).astype(v.dtype)
        o = jnp.einsum('bqgrn,bqngd->bqgrd', p, v_sel)
        return o.reshape(B, Q_BLOCK, D_ATTN)

    out = lax.map(block, (to_blocks(q), to_blocks(qi), to_blocks(wi), starts))
    return out.swapaxes(0, 1).reshape(B, T, D_ATTN)

def spatial_gating(u, v, ln_g, ln_b, w_s, b_s):
    B, T = v.shape[0], v.shape[1]
    nc = T // SGU_CHUNK
    vn = layer_norm(v, ln_g, ln_b)
    vc = vn.reshape(B, nc, SGU_CHUNK, SGU_GROUPS, SGU_GROUP_DIM)
    mask = jnp.tril(jnp.ones((SGU_CHUNK, SGU_CHUNK), dtype=bool))
    ws = jnp.where(mask[None], w_s, jnp.zeros_like(w_s))
    mixed = jnp.einsum('gts,bcsgd->bctgd', ws, vc) + b_s.T[None, None, :, :, None]
    return u * mixed.reshape(B, T, D_SGU)

def second_inputs(seed: int = 0) -> dict:
    key = jax.random.key(seed)
    ks = jax.random.split(key, 16)
    f32 = jnp.float32
    d_in = sum(COL_SIZES)
    x = jax.random.normal(ks[0], (BATCH, SEQ, D_MODEL), f32)
    rel_bias = 0.5 * jax.random.normal(ks[1], (REL_BUCKETS, N_HEADS), f32)
    norm1_g = 1.0 + 0.01 * jax.random.normal(ks[2], (DEPTH, D_MODEL), f32)
    w_in = jax.random.normal(ks[3], (DEPTH, D_MODEL, d_in), f32) * D_MODEL ** -0.5
    sgu_ln_g = 1.0 + 0.01 * jax.random.normal(ks[4], (DEPTH, D_SGU), f32)
    sgu_ln_b = 0.01 * jax.random.normal(ks[5], (DEPTH, D_SGU), f32)
    sgu_w = jax.random.normal(ks[6], (DEPTH, SGU_GROUPS, SGU_CHUNK, SGU_CHUNK), f32) * SGU_CHUNK ** -0.5
    sgu_b = 1.0 + 0.01 * jax.random.normal(ks[7], (DEPTH, SGU_GROUPS, SGU_CHUNK), f32)
    w_out = jax.random.normal(ks[8], (DEPTH, D_MODEL, D_MODEL), f32) * D_MODEL ** -0.5
    norm2_g = 1.0 + 0.01 * jax.random.normal(ks[9], (DEPTH, D_MODEL), f32)
    w_ff1 = jax.random.normal(ks[10], (DEPTH, D_MODEL, D_FF), f32) * D_MODEL ** -0.5
    w_ff2 = jax.random.normal(ks[11], (DEPTH, D_FF, D_MODEL), f32) * D_FF ** -0.5
    final_g = 1.0 + 0.01 * jax.random.normal(ks[12], (D_MODEL,), f32)
    return {"x": x, "rel_bias": rel_bias, "norm1_g": norm1_g, "w_in": w_in,
            "sgu_ln_g": sgu_ln_g, "sgu_ln_b": sgu_ln_b, "sgu_w": sgu_w, "sgu_b": sgu_b,
            "w_out": w_out, "norm2_g": norm2_g, "w_ff1": w_ff1, "w_ff2": w_ff2,
            "final_g": final_g}

def second_block(x, rel_bias, norm1_g, w_in, sgu_ln_g, sgu_ln_b, sgu_w, sgu_b,
              w_out, norm2_g, w_ff1, w_ff2, final_g):
    B, T, _ = x.shape
    split_pts = [int(p) for p in np.cumsum(COL_SIZES)[:-1]]
    for l in range(DEPTH):
        h = rms_norm(x, norm1_g[l])
        proj = jnp.einsum('btd,dc->btc', h, w_in[l])
        q, k, v, qi, ki, wi, u_s, v_s, ga, gb = jnp.split(proj, split_pts, axis=-1)
        q = q.reshape(B, T, N_HEADS, HEAD_DIM_2)
        k = k.reshape(B, T, N_KV_HEADS, HEAD_DIM_2)
        v = v.reshape(B, T, N_KV_HEADS, HEAD_DIM_2)
        qi = qi.reshape(B, T, IDX_HEADS, IDX_DIM)
        attn = sparse_attention(q, k, v, qi, ki, wi, rel_bias)
        sgu = spatial_gating(jax.nn.gelu(u_s), jax.nn.gelu(v_s),
                             sgu_ln_g[l], sgu_ln_b[l], sgu_w[l], sgu_b[l])
        merged = jax.nn.sigmoid(ga) * attn + jax.nn.sigmoid(gb) * sgu
        x = x + jnp.einsum('btc,cd->btd', merged, w_out[l])
        h2 = rms_norm(x, norm2_g[l])
        ff = jnp.square(jax.nn.relu(jnp.einsum('btd,df->btf', h2, w_ff1[l])))
        x = x + jnp.einsum('btf,fd->btd', ff, w_ff2[l])
    return rms_norm(x, final_g)


_first_inputs_2 = second_inputs


def second_inputs(seed=0):
    import zlib

    import numpy as np

    out = dict(_first_inputs_2(seed))
    spreads = {}
    factors = {}
    for name, (base, spread) in spreads.items():
        noise = np.random.default_rng([zlib.crc32(name.encode()), seed]).standard_normal(out[name].shape)
        drawn = base * np.exp(spread * noise) if base else spread * noise
        out[name] = __import__('jax').numpy.asarray(drawn.astype(out[name].dtype))
    for name, factor in factors.items():
        out[name] = (out[name] * factor).astype(out[name].dtype)
    return out


_narrow_inputs_2 = second_inputs


def second_inputs(seed=0):

    out = dict(_narrow_inputs_2(seed))
    wider = {'norm1_g': 5.01,
     'sgu_ln_g': 12.0,
     'sgu_ln_b': 12.0,
     'sgu_b': 12.0,
     'norm2_g': 7.29,
     'final_g': 6.55}
    for name, times in wider.items():
        mean = out[name].mean()
        out[name] = (mean + times * (out[name] - mean)).astype(out[name].dtype)
    return out


MIX_WIDTH = D_MODEL
POOL_WIDTH = MIX_WIDTH // 2
POOL_WINDOWS = (2, 4, 8, 16)
POOL_GROUP = POOL_WIDTH // len(POOL_WINDOWS)
ATTN_WIDTH = MIX_WIDTH - POOL_WIDTH
HEAD_DIM_3 = 128
N_HEADS_3 = ATTN_WIDTH // HEAD_DIM_3
DILATED_PATTERNS = ((128, 1), (512, 4), (2048, 16))
MAX_WINDOW = max(w for w, _ in DILATED_PATTERNS)
IN_WIDTH = POOL_WIDTH + 3 * ATTN_WIDTH
D_FF_3 = 4 * D_MODEL


def rmsnorm(x, g):
    xf = x.astype(jnp.float32)
    y = xf * lax.rsqrt(jnp.mean(xf * xf, axis=-1, keepdims=True) + NORM_EPS)
    return (y * g.astype(jnp.float32)).astype(x.dtype)

def alibi_slopes():
    return 2.0 ** (-8.0 * jnp.arange(1, N_HEADS_3 + 1, dtype=jnp.float32) / N_HEADS_3)

def pool_mixer(u, pool_w, pool_scale):
    B, S, _ = u.shape
    uf = u.astype(jnp.float32)
    cs = jnp.cumsum(uf, axis=1)
    pos = jnp.arange(1, S + 1, dtype=jnp.float32)[None, :, None]
    diffs = []
    for g, w in enumerate(POOL_WINDOWS):
        c = cs[..., g * POOL_GROUP:(g + 1) * POOL_GROUP]
        trailing = c - jnp.pad(c, ((0, 0), (w, 0), (0, 0)))[:, :S]
        mean = trailing / jnp.minimum(pos, float(w))
        diffs.append(mean - uf[..., g * POOL_GROUP:(g + 1) * POOL_GROUP])
    d = jnp.stack(diffs, axis=2).astype(u.dtype)
    y = jnp.einsum('bsgc,gcf->bsgf', d, pool_w).reshape(B, S, POOL_WIDTH)
    return y * pool_scale

def dilated_attention(q, k, v, slopes):
    B, S, H, Dh = q.shape
    scale = Dh ** -0.5
    kp = jnp.pad(k, ((0, 0), (MAX_WINDOW, 0), (0, 0), (0, 0)))
    vp = jnp.pad(v, ((0, 0), (MAX_WINDOW, 0), (0, 0), (0, 0)))
    qi = jnp.arange(Q_BLOCK)

    def block(b0):
        qb = lax.dynamic_slice_in_dim(q, b0, Q_BLOCK, axis=1).astype(jnp.float32) * scale
        kwin = lax.dynamic_slice_in_dim(kp, b0, Q_BLOCK + MAX_WINDOW, axis=1)
        vwin = lax.dynamic_slice_in_dim(vp, b0, Q_BLOCK + MAX_WINDOW, axis=1)
        ms, dens, nums = [], [], []
        for window, dil in DILATED_PATTERNS:
            dist = jnp.arange(window // dil + 1) * dil
            idx = qi[:, None] + MAX_WINDOW - dist[None, :]
            valid = (b0 + qi)[:, None] >= dist[None, :]
            kg = jnp.take(kwin, idx, axis=1).astype(jnp.float32)
            vg = jnp.take(vwin, idx, axis=1).astype(jnp.float32)
            s = jnp.einsum('bqhd,bqjhd->bqhj', qb, kg)
            s = s - slopes[:, None] * dist.astype(jnp.float32)[None, :]
            s = jnp.where(valid[None, :, None, :], s, -jnp.inf)
            m = jnp.max(s, axis=-1)
            p = jnp.exp(s - m[..., None])
            ms.append(m)
            dens.append(jnp.sum(p, axis=-1))
            nums.append(jnp.einsum('bqhj,bqjhd->bqhd', p, vg))
        m_all = jnp.stack(ms)
        w = jnp.exp(m_all - jnp.max(m_all, axis=0))
        den = jnp.sum(w * jnp.stack(dens), axis=0)
        num = jnp.sum(w[..., None] * jnp.stack(nums), axis=0)
        return num / den[..., None]

    starts = jnp.arange(S // Q_BLOCK) * Q_BLOCK
    out = lax.map(block, starts)
    return out.transpose(1, 0, 2, 3, 4).reshape(B, S, H * Dh).astype(q.dtype)

def third_inputs(seed: int = 0) -> dict:
    key = jax.random.key(seed)
    ks = jax.random.split(key, 12)
    f32 = jnp.float32
    x = jax.random.normal(ks[0], (BATCH, SEQ, D_MODEL), f32)
    norm_mix_g = 1.0 + 0.05 * jax.random.normal(ks[1], (DEPTH, D_MODEL), f32)
    w_in = jax.random.normal(ks[2], (DEPTH, D_MODEL, IN_WIDTH), f32) * D_MODEL ** -0.5
    pool_w = jax.random.normal(ks[3], (DEPTH, len(POOL_WINDOWS), POOL_GROUP, POOL_GROUP), f32) * POOL_GROUP ** -0.5
    pool_scale = 1.0 + 0.1 * jax.random.normal(ks[4], (DEPTH, POOL_WIDTH), f32)
    pool_out_norm_g = 1.0 + 0.05 * jax.random.normal(ks[5], (DEPTH, POOL_WIDTH), f32)
    attn_out_norm_g = 1.0 + 0.05 * jax.random.normal(ks[6], (DEPTH, ATTN_WIDTH), f32)
    w_out = jax.random.normal(ks[7], (DEPTH, MIX_WIDTH, D_MODEL), f32) * MIX_WIDTH ** -0.5
    norm_mlp_g = 1.0 + 0.05 * jax.random.normal(ks[8], (DEPTH, D_MODEL), f32)
    w_up = jax.random.normal(ks[9], (DEPTH, D_MODEL, D_FF_3), f32) * D_MODEL ** -0.5
    w_down = jax.random.normal(ks[10], (DEPTH, D_FF_3, D_MODEL), f32) * D_FF_3 ** -0.5
    norm_final_g = 1.0 + 0.05 * jax.random.normal(ks[11], (D_MODEL,), f32)
    return {"x": x, "norm_mix_g": norm_mix_g, "w_in": w_in, "pool_w": pool_w,
            "pool_scale": pool_scale, "pool_out_norm_g": pool_out_norm_g,
            "attn_out_norm_g": attn_out_norm_g, "w_out": w_out, "norm_mlp_g": norm_mlp_g,
            "w_up": w_up, "w_down": w_down, "norm_final_g": norm_final_g}

def third_block(x, norm_mix_g, w_in, pool_w, pool_scale, pool_out_norm_g, attn_out_norm_g,
              w_out, norm_mlp_g, w_up, w_down, norm_final_g):
    B, S, _ = x.shape
    slopes = alibi_slopes()
    for l in range(DEPTH):
        h = rmsnorm(x, norm_mix_g[l])
        proj = h @ w_in[l]
        u = proj[..., :POOL_WIDTH]
        qkv = proj[..., POOL_WIDTH:].reshape(B, S, 3, N_HEADS_3, HEAD_DIM_3)
        y_pool = rmsnorm(pool_mixer(u, pool_w[l], pool_scale[l]), pool_out_norm_g[l])
        y_attn = rmsnorm(dilated_attention(qkv[:, :, 0], qkv[:, :, 1], qkv[:, :, 2], slopes),
                         attn_out_norm_g[l])
        x = x + jnp.concatenate([y_pool, y_attn], axis=-1) @ w_out[l]
        h = rmsnorm(x, norm_mlp_g[l])
        x = x + jnp.square(jax.nn.relu(h @ w_up[l])) @ w_down[l]
    return rmsnorm(x, norm_final_g)


def setup_inputs(seed=0):
    out = dict(first_inputs(seed))
    for name, value in second_inputs(seed + 1).items():
        if name != "x":
            out[name + "_2"] = value
    for name, value in third_inputs(seed + 2).items():
        if name != "x":
            out[name + "_3"] = value
    return out


def reference(
    x, pre_norm_g, post_norm_g, w_in, mu_rkv, mu_wa, w0, w1, w2, a0, a1, a2, k_k, k_a, r_k,
    ln_x_g, ln_x_b, rel_bias, w_branch_rwkv, w_branch_attn, b_merge, w_out, rel_bias_2,
    norm1_g_2, w_in_2, sgu_ln_g_2, sgu_ln_b_2, sgu_w_2, sgu_b_2, w_out_2, norm2_g_2, w_ff1_2,
    w_ff2_2, final_g_2, norm_mix_g_3, w_in_3, pool_w_3, pool_scale_3, pool_out_norm_g_3,
    attn_out_norm_g_3, w_out_3, norm_mlp_g_3, w_up_3, w_down_3, norm_final_g_3,
):
    x = first_block(
        x, pre_norm_g, post_norm_g, w_in, mu_rkv, mu_wa, w0, w1, w2, a0, a1, a2, k_k, k_a, r_k,
        ln_x_g, ln_x_b, rel_bias, w_branch_rwkv, w_branch_attn, b_merge, w_out,
    )
    x = second_block(
        x, rel_bias_2, norm1_g_2, w_in_2, sgu_ln_g_2, sgu_ln_b_2, sgu_w_2, sgu_b_2, w_out_2,
        norm2_g_2, w_ff1_2, w_ff2_2, final_g_2,
    )
    return third_block(
        x, norm_mix_g_3, w_in_3, pool_w_3, pool_scale_3, pool_out_norm_g_3, attn_out_norm_g_3,
        w_out_3, norm_mlp_g_3, w_up_3, w_down_3, norm_final_g_3,
    )


_drawn_inputs = setup_inputs


def setup_inputs(seed=0):
    import zlib

    import numpy as np

    out = dict(_drawn_inputs(seed))
    spreads = {}
    factors = {'rel_bias_2': 8.0,
     'norm1_g_2': 8.0,
     'sgu_ln_g_2': 8.0,
     'sgu_ln_b_2': 8.0,
     'sgu_b_2': 8.0,
     'norm2_g_2': 5.285}
    for name, (base, spread) in spreads.items():
        noise = np.random.default_rng([zlib.crc32(name.encode()), seed]).standard_normal(out[name].shape)
        drawn = base * np.exp(spread * noise) if base else spread * noise
        out[name] = __import__('jax').numpy.asarray(drawn.astype(out[name].dtype))
    for name, factor in factors.items():
        out[name] = (out[name] * factor).astype(out[name].dtype)
    return out
```

```python
from contextlib import ExitStack
import math
import numpy as np
import concourse.bass as bass
from concourse import mybir

F32 = mybir.dt.float32
I32 = mybir.dt.int32
ALU = mybir.AluOpType
ACT = mybir.ActivationFunctionType
AX = mybir.AxisListType.X

P = 128
TOK = 256
D = 2048
DB = 1024
DC = D // P
BC = DB // P
KG = 8
UC = 512
SLOTS = 4
NEG = -1.0e30
EPS = 1e-6
DECAY = 0.606531
CH = 64
NCH = TOK // CH
CENTRE = DECAY * CH / 2


class Section:
    def __init__(self, iters, sources):
        self.iters, self.sources = iters, sources
        self.unit0 = 0


def build_kernel(nc, I, out_dram, upto=None):
    ctx = ExitStack()
    with ctx:
        def sb(name, shape, dt=F32):
            return ctx.enter_context(nc.sbuf_tensor(name, shape, dt))

        def sem(name):
            return ctx.enter_context(nc.semaphore(name))

        ring = sb("ring", [P, SLOTS, KG, UC])
        arena = sb("arena", [P, 33812])
        ident = sb("ident", [P, P])
        ones = sb("ones", [P, P])
        headones = sb("headones", [P, P])
        prm = sb("prm", [P, 384])
        rstd = sb("rstd", [P, TOK])
        variance = sb("variance", [P, TOK])
        variance_t = sb("variance_t", [P, TOK])
        p_turned = sb("p_turned", [P, 384])
        smalls = sb("smalls", [P, 32])

        gp = ctx.enter_context(nc.psum_tensor("gp", [P, 2, 4, TOK], F32))
        sp_ = ctx.enter_context(nc.psum_tensor("sidep", [P, 4, 512], F32))

        unit_loaded = [sem(f"unit_loaded_{k}") for k in range(SLOTS)]
        unit_used = sem("unit_used")
        pair_evacuated = [sem(f"pair_evacuated_{b}") for b in range(2)]
        idx_extra_loaded = sem("idx_extra_loaded")

        def area(start, chunks, width=TOK):
            return arena[:, start:start + chunks * width].rearrange("p (c t) -> p c t", t=width)

        A0 = 4096 + 4112
        xt = area(0, DC)
        hp = area(4096, DC, TOK + 1)
        h = area(4096, DC)

        def cols(w, rows, c):
            return w[rows * KG * P:(rows + 1) * KG * P, c].rearrange("(c p) n -> p c n", p=P)

        w1, w2_, w3 = I["w_in"][0], I["w_in_2"][0], I["w_in_3"][0]

        def at(expr, n):
            if isinstance(expr, int):
                return slice(expr, expr + n)
            return bass.ds(expr, n)

        def two_by_two(w, base):
            return lambda k, i: [(cols(w, k % 2, at(i * 1024 + base + 512 * (k // 2), UC)), 0, UC)]

        def branches(k, i):
            w = (I["w_branch_rwkv"], I["w_branch_attn"])[k % 2][0]
            return [(cols(w, 0, at(i * 1024 + 512 * (k // 2), UC)), 0, UC)]

        def index_cols(k, i):
            if k < 2:
                return [(cols(w2_, k, slice(3072, 3584)), 0, UC)]
            r = k - 2
            return [(cols(w2_, r, slice(3584, 3648)), 0, 64), (cols(w2_, r, slice(3584, 3648)), 64, 64),
                    (cols(w2_, r, slice(3648, 3656)), 128, 8)]

        def down(w):
            return w

        S = {}
        order = []

        def section(name, iters, sources):
            s = Section(iters, sources)
            s.unit0 = (order[-1].unit0 + order[-1].iters * SLOTS) if order else 0
            s.name = name
            S[name] = s
            order.append(s)

        section("rkv", 3, two_by_two(w1, 0))
        section("zr", 1, two_by_two(w1, 3072))
        section("qkv", 3, two_by_two(w1, 4096))
        section("za", 1, two_by_two(w1, 7168))
        section("gates", 4, two_by_two(w1, 8192))
        section("branch", 2, branches)
        section("out", 2, two_by_two(I["w_out"][0], 0))
        section("qkv2", 3, two_by_two(w2_, 0))
        section("index2", 1, index_cols)
        section("uv2", 4, two_by_two(w2_, 3656))
        section("gates2", 4, two_by_two(w2_, 7752))
        section("out2", 2, two_by_two(I["w_out_2"][0], 0))
        section("up2", 8, two_by_two(I["w_ff1_2"][0], 0))
        section("down2", 8, None)
        section("in3", 4, two_by_two(w3, 0))
        section("out3", 2, two_by_two(I["w_out_3"][0], 0))
        section("up3", 8, two_by_two(I["w_up_3"][0], 0))
        section("down3", 8, None)
        DOWN = {"down2": I["w_ff2_2"][0], "down3": I["w_down_3"][0]}

        def load_unit(sp, k, pieces, used):
            if used is not None:
                sp.wait_ge(unit_used, used)
            for n, (src, c0, width) in enumerate(pieces):
                last = n == len(pieces) - 1
                sp.dma_start(ring[:, k, :, c0:c0 + width], src).then_inc(
                    unit_loaded[k] if last else idx_extra_loaded, 16)

        def first_units(sp, s, fresh=False):
            for k in range(SLOTS):
                if s.sources is None:
                    pieces = [(cols(DOWN[s.name], k, slice(0, UC)), 0, UC)]
                else:
                    pieces = s.sources(k, 0)
                load_unit(sp, k, pieces, None if fresh else s.unit0 - SLOTS + k + 1)

        def load_section(sp, s):
            if s.sources is not None:
                if s.iters > 1:
                    with sp.Fori(1, s.iters) as i:
                        for k in range(SLOTS):
                            load_unit(sp, k, s.sources(k, i), i * SLOTS + (s.unit0 - SLOTS + k + 1))
            else:
                w = DOWN[s.name]
                with sp.Fori(0, 3) as b:
                    for k in range(SLOTS):
                        load_unit(sp, k, [(cols(w, k + 4, at(b * UC, UC)), 0, UC)],
                                  b * 8 + (s.unit0 + k + 1))
                    for k in range(SLOTS):
                        load_unit(sp, k, [(cols(w, k, at(b * UC + UC, UC)), 0, UC)],
                                  b * 8 + (s.unit0 + 4 + k + 1))
                for k in range(SLOTS):
                    load_unit(sp, k, [(cols(w, k + 4, slice(3 * UC, 4 * UC)), 0, UC)],
                              s.unit0 + 24 + k + 1)
            n = order.index(s) + 1
            if n < len(order):
                first_units(sp, order[n])

        blocks_before = {}
        n = 0
        for s in order:
            blocks_before[s.name] = n
            per = {"branch": 4, "index2": 2}.get(s.name, 2)
            n += 4 if s.sources is None else s.iters * per

        def multiply_unit(pe, k, loaded, pair, x, first, last, tiles=4):
            pe.wait_ge(unit_loaded[k], loaded)
            for c in range(KG):
                for j in range(tiles):
                    m = pe.matmul(gp[:, pair, j, :], ring[:, k, c, j * P:(j + 1) * P], x(c),
                                  start=(first and c == 0 and j % 2 == 0),
                                  stop=(last and c == KG - 1), skip_group_check=True)
            m.then_inc(unit_used, 1)

        def multiply_section(pe, s, x, tiles=(4, 4)):
            b0 = blocks_before[s.name]
            assert b0 % 2 == 0
            def body(i):
                for b in range(2):
                    if b0 or not isinstance(i, int):
                        pe.wait_ge(pair_evacuated[b], i + b0 // 2)
                    for u in range(2):
                        k = 2 * b + u
                        multiply_unit(pe, k, i * 16 + 16 * (s.unit0 // SLOTS + 1), b,
                                      lambda c: x(u * KG + c), u == 0, u == 1, tiles[b])
            if s.iters == 1:
                body(0)
            else:
                with pe.Fori(0, s.iters) as i:
                    body(i)

        def block_done(eng, s, i, b):
            eng.wait_ge(unit_used, i * 4 + (s.unit0 + 2 * b + 2))

        class Steps:
            def __init__(self, ectx, name, steps):
                self.s, self.steps, self.at = local(ectx, name), steps, 0

            def did(self, ins, step):
                assert self.steps[self.at % len(self.steps)] == step, (step, self.steps[self.at % len(self.steps)])
                self.at += 1
                ins.then_inc(self.s, 1)

            def value(self, step, i=0):
                return i * len(self.steps) + (self.steps.index(step) + 1)

            def wait(self, eng, step, i=0):
                eng.wait_ge(self.s, self.value(step, i))

        names = [0]

        def local(ectx, name):
            names[0] += 1
            return ectx.enter_context(nc.semaphore(f"{name}_{names[0]}"))

        rows = {}
        row_list = []
        r = 0
        def add_rows(name, key, ap, n):
            nonlocal r
            if r // P != (r + n - 1) // P:
                r = (r // P + 1) * P
            rows[name] = r
            row_list.append((r, n, ap))
            r += n
        flat = lambda key: I[key]
        add_rows("pre", None, I["pre_norm_g"][0].rearrange("(c p) -> c p", p=P), 16)
        add_rows("post", None, I["post_norm_g"][0].rearrange("(c p) -> c p", p=P), 16)
        add_rows("mu_rkv", None, I["mu_rkv"][0].rearrange("m (c p) -> (m c) p", p=P), 24)
        add_rows("mu_wa", None, I["mu_wa"][0].rearrange("m (c p) -> (m c) p", p=P), 32)
        add_rows("a0", None, I["a0"][0].rearrange("(c p) -> c p", p=P), 8)
        add_rows("k_k", None, I["k_k"][0].rearrange("(c p) -> c p", p=P), 8)
        add_rows("k_a", None, I["k_a"][0].rearrange("(c p) -> c p", p=P), 8)
        add_rows("r_k", None, I["r_k"][0].rearrange("(c h) n -> c (h n)", h=2), 8)
        add_rows("ln_g", None, I["ln_x_g"][0].rearrange("(c p) -> c p", p=P), 8)
        add_rows("ln_b", None, I["ln_x_b"][0].rearrange("(c p) -> c p", p=P), 8)
        add_rows("b_merge", None, I["b_merge"][0].rearrange("m (c p) -> (m c) p", p=P), 32)
        add_rows("norm1", None, I["norm1_g_2"][0].rearrange("(c p) -> c p", p=P), 16)
        add_rows("sgu_g", None, I["sgu_ln_g_2"][0].rearrange("(c p) -> c p", p=P), 16)
        add_rows("sgu_b", None, I["sgu_ln_b_2"][0].rearrange("(c p) -> c p", p=P), 16)
        add_rows("norm2", None, I["norm2_g_2"][0].rearrange("(c p) -> c p", p=P), 16)
        add_rows("final2", None, I["final_g_2"].rearrange("(c p) -> c p", p=P), 16)
        add_rows("mix3", None, I["norm_mix_g_3"][0].rearrange("(c p) -> c p", p=P), 16)
        add_rows("pscale", None, I["pool_scale_3"][0].rearrange("(c p) -> c p", p=P), 8)
        add_rows("pout", None, I["pool_out_norm_g_3"][0].rearrange("(c p) -> c p", p=P), 8)
        add_rows("aout", None, I["attn_out_norm_g_3"][0].rearrange("(c p) -> c p", p=P), 8)
        add_rows("mlp3", None, I["norm_mlp_g_3"][0].rearrange("(c p) -> c p", p=P), 16)
        add_rows("final3", None, I["norm_final_g_3"].rearrange("(c p) -> c p", p=P), 16)
        assert r <= 384

        def par(name, c=0, n=1):
            return prm[:, rows[name] + c:rows[name] + c + n]

        def start_stage():
            xrow = arena[:, A0:A0 + 4096].rearrange("p (t c) -> p t c", t=2)
            prow = arena[:, A0 + 4096:A0 + 4096 + 384].rearrange("p (t c) -> p t c", t=3)
            with ExitStack() as e:
                x_loaded, p_loaded, filled, made, turned, copied = (
                    local(e, x) for x in ("x_loaded", "params_loaded", "filled", "consts_made", "turned", "copied"))
                with nc.Block() as block:
                    @block.sync
                    def _(sp):
                        for t in range(2):
                            sp.dma_start(xrow[:, t, :], I["x"][0, t * P:(t + 1) * P, :]).then_inc(x_loaded, 16)
                        sp.wait_ge(filled, 1)
                        for (r0, nr, ap) in row_list:
                            sp.dma_start(prow[r0 % P:r0 % P + nr, r0 // P, :], ap).then_inc(p_loaded, 16)
                        first_units(sp, order[0], fresh=True)

                    @block.gpsimd
                    def _(pool):
                        pool.memset(prow, 0.0).then_inc(filled, 1)
                        pool.memset(ident[:, :], 0.0).then_inc(filled, 1)
                        pool.memset(ones[:, :], 1.0).then_inc(filled, 1)
                        pool.memset(headones[:, :], 0.0).then_inc(filled, 1)
                        pool.wait_ge(filled, 4)
                        pool.affine_select(out=ident[:, :], in_=ident[:, :], compare_op=ALU.not_equal, fill=1.0,
                                           base=0, pattern=[[-1, P]], channel_multiplier=1).then_inc(made, 1)
                        for q in range(2):
                            pool.wait_ge(made, q + 1)
                            pool.memset(headones[64 * q:64 * q + 64, 64 * q:64 * q + 64], 1.0).then_inc(made, 1)
                        pool.wait_ge(made, 3)
                        pool.memset(hp[:, :, 0:1], 0.0).then_inc(made, 1)

                    @block.tensor
                    def _(pe):
                        pe.wait_ge(made, 4)
                        pe.wait_ge(x_loaded, 32)
                        for g in range(8):
                            if g >= 4:
                                pe.wait_ge(copied, g - 3)
                            for c in range(2):
                                for t in range(2):
                                    m = pe.transpose(sp_[:, g % 4, c * TOK + t * P:c * TOK + t * P + P],
                                                     xrow[:, t, (2 * g + c) * P:(2 * g + c + 1) * P], ident[:, :])
                            m.then_inc(turned, 1)
                        pe.wait_ge(p_loaded, 16 * len(row_list))
                        pe.wait_ge(copied, 5)
                        for t in range(3):
                            m = pe.transpose(sp_[:, 0, t * P:(t + 1) * P], prow[:, t, :], ident[:, :])
                        m.then_inc(turned, 1)

                    @block.vector
                    def _(v):
                        for g in range(8):
                            v.wait_ge(turned, g + 1)
                            v.tensor_copy(xt[:, 2 * g:2 * g + 2, :],
                                          sp_[:, g % 4, :].rearrange("p (c t) -> p c t", c=2)).then_inc(copied, 1)
                        v.wait_ge(turned, 9)
                        v.tensor_copy(prm[:, :], sp_[:, 0, 0:384]).then_inc(copied, 1)

        def inv_root(v, sums, count, summed, meaned, rooted, inverted):
            x, t = variance[:, :], variance_t[:, :]
            v.wait_ge(summed, 1)
            v.tensor_scalar(x, sums, 1.0 / count, EPS, ALU.mult, ALU.add).then_inc(meaned, 1)
            v.wait_ge(rooted, 1)
            v.reciprocal(rstd[:, :], rstd[:, :]).then_inc(inverted, 1)
            v.wait_ge(inverted, 1)
            v.tensor_tensor(t, rstd[:, :], rstd[:, :], ALU.mult).then_inc(inverted, 1)
            v.wait_ge(inverted, 2)
            v.tensor_tensor(t, t, x, ALU.mult).then_inc(inverted, 1)
            v.wait_ge(inverted, 3)
            v.tensor_scalar(t, t, -0.5, 1.5, ALU.mult, ALU.add).then_inc(inverted, 1)
            v.wait_ge(inverted, 4)
            v.tensor_tensor(rstd[:, :], rstd[:, :], t, ALU.mult).then_inc(inverted, 1)
            v.wait_ge(inverted, 5)

        def norm_stage(src, nchunks, gain, dst, add_to=None, scratch=A0):
            sq = area(scratch, nchunks)
            with ExitStack() as e:
                squared, summed, meaned, rooted, inverted, scaled = (
                    local(e, x) for x in ("squared", "summed", "meaned", "rooted", "inverted", "scaled"))
                with nc.Block() as block:
                    @block.scalar
                    def _(act):
                        for q in range(4):
                            n = nchunks // 4
                            act.activation(sq[:, q * n:(q + 1) * n, :], src[:, q * n:(q + 1) * n, :],
                                           ACT.Square).then_inc(squared, 1)
                        act.wait_ge(meaned, 1)
                        act.activation(rstd[:, :], variance[:, :], ACT.Sqrt).then_inc(rooted, 1)

                    @block.tensor
                    def _(pe):
                        for c in range(nchunks):
                            if c % (nchunks // 4) == 0:
                                pe.wait_ge(squared, c // (nchunks // 4) + 1)
                            m = pe.matmul(sp_[:, 0, 0:TOK], ones[:, :], sq[:, c, :], start=(c == 0),
                                          stop=(c == nchunks - 1))
                        m.then_inc(summed, 1)

                    @block.vector
                    def _(v):
                        inv_root(v, sp_[:, 0, 0:TOK], nchunks * P, summed, meaned, rooted, inverted)
                        if add_to is None:
                            with v.Fori(0, nchunks) as c:
                                v.scalar_tensor_tensor(dst[:, at(c, 1), :], src[:, at(c, 1), :],
                                                       prm[:, at(c + rows[gain], 1)], rstd[:, :],
                                                       ALU.mult, ALU.mult).then_inc(scaled, 1)
                        else:
                            with v.Fori(0, nchunks) as c:
                                v.scalar_tensor_tensor(src[:, at(c, 1), :], src[:, at(c, 1), :],
                                                       prm[:, at(c + rows[gain], 1)], rstd[:, :],
                                                       ALU.mult, ALU.mult).then_inc(scaled, 1)
                            v.wait_ge(scaled, nchunks)
                            v.tensor_tensor(add_to, add_to, src, ALU.add).then_inc(scaled, 1)

        def gemm_stage(name, x, evac, engine="scalar", tiles=(4, 4)):
            s = S[name]
            b0 = blocks_before[name]
            with nc.Block() as block:
                @block.sync
                def _(sp):
                    load_section(sp, s)

                @block.tensor
                def _(pe):
                    if name == "index2":
                        pe.wait_ge(idx_extra_loaded, 64)
                    multiply_section(pe, s, x, tiles)

                def prog(eng):
                    def body(i):
                        for b in range(2):
                            block_done(eng, s, i, b)
                            evac(eng, i, b, gp[:, b, :, :]).then_inc(pair_evacuated[b], 1)
                    if s.iters == 1:
                        body(0)
                    else:
                        with eng.Fori(0, s.iters) as i:
                            body(i)
                (block.scalar if engine == "scalar" else block.vector)(prog)

        def copy_to(dst, width=None):
            def evac(eng, i, b, ps):
                return eng.activation(dst[:, at(i * 8 + b * 4, 4), :], ps, ACT.Copy)
            return evac

        consts = sb("consts", [P, 1024])
        mask_su = consts[:, 0:128]
        level = consts[:, 128:512].rearrange("p (l t) -> p l t", l=6)
        tri = consts[:, 512:768]
        eye2 = consts[:, 768:832]
        centre = consts[:, 832:834]
        omka = consts[:, 834:842]
        tri128 = consts[:, 896:1024]
        w2p = arena[:, 32788:33812]
        t1 = arena[:, 32532:32788]

        def lora_stage():
            xw, xa, dh = area(A0, DC), area(A0 + 4096, DC), area(A0 + 8192, DC)
            lw = area(A0 + 12288, DC, 64)
            la = area(A0 + 13312, DC, 64)
            a2s = arena[:, A0 + 14336:A0 + 15360]
            a1t = arena[:, A0 + 15360:A0 + 15616]
            aT = area(24592, BC)
            with ExitStack() as e:
                w_loaded, ones_row, differed, xmixed, hidden, activated, projected = (
                    local(e, x) for x in ("lora_loaded", "ones_row", "differed", "xmixed", "hidden", "activated", "projected"))
                with nc.Block() as block:
                    @block.sync
                    def _(sp):
                        sp.dma_start(lw, I["w1"][0].rearrange("(c p) n -> p c n", p=P)).then_inc(w_loaded, 16)
                        sp.dma_start(la, I["a1"][0].rearrange("(c p) n -> p c n", p=P)).then_inc(w_loaded, 16)
                        sp.dma_start(w2p[0:64, :], I["w2"][0]).then_inc(w_loaded, 16)
                        sp.dma_start(w2p[64:65, :], I["w0"]).then_inc(w_loaded, 16)
                        sp.dma_start(a2s[0:64, :], I["a2"][0]).then_inc(w_loaded, 16)
                        sp.wait_ge(w_loaded, 80)

                    @block.gpsimd
                    def _(pool):
                        pool.memset(t1[64:65, :], 1.0).then_inc(ones_row, 1)
                        pool.wait_ge(ones_row, 1)
                        pool.memset(centre[:, 0:1], CENTRE).then_inc(ones_row, 1)
                        pool.wait_ge(ones_row, 2)
                        pool.memset(centre[:, 1:2], -CENTRE).then_inc(ones_row, 1)

                    @block.vector
                    def _(v):
                        v.tensor_tensor(dh, hp[:, :, 0:TOK], hp[:, :, 1:TOK + 1], ALU.subtract).then_inc(differed, 1)
                        v.tensor_scalar(omka, par("k_a", 0, 8), -1.0, 1.0, ALU.mult, ALU.add).then_inc(differed, 1)
                        v.wait_ge(differed, 1)
                        with v.Fori(0, DC) as c:
                            for m, dst in ((0, xw), (1, xa)):
                                v.scalar_tensor_tensor(dst[:, at(c, 1), :], dh[:, at(c, 1), :],
                                                       prm[:, at(c + (rows["mu_wa"] + 16 * m), 1)],
                                                       hp[:, at(c, 1), 1:TOK + 1], ALU.mult, ALU.add).then_inc(xmixed, 1)

                    @block.tensor
                    def _(pe):
                        pe.wait_ge(w_loaded, 80)
                        for c in range(DC):
                            pe.wait_ge(xmixed, 2 * c + 2)
                            for m, (w, x) in enumerate(((lw, xw), (la, xa))):
                                mm = pe.matmul(sp_[0:64, m, 0:TOK], w[:, c, :], x[:, c, :], start=(c == 0), stop=(c == DC - 1))
                        mm.then_inc(hidden, 1)
                        pe.wait_ge(activated, 2)
                        for g in range(4):
                            if g >= 2:
                                pe.wait_ge(activated, 2 + 2 * (g - 1))
                            for k in range(2):
                                mm = pe.matmul(sp_[:, 2 + g % 2, k * TOK:(k + 1) * TOK],
                                               a2s[0:64, (2 * g + k) * P:(2 * g + k + 1) * P], a1t[0:64, :], start=True, stop=True)
                            mm.then_inc(projected, 1)

                    @block.scalar
                    def _(act):
                        act.wait_ge(hidden, 1)
                        act.activation(a1t[0:64, :], sp_[0:64, 1, 0:TOK], ACT.Copy).then_inc(activated, 1)
                        act.activation(t1[0:64, :], sp_[0:64, 0, 0:TOK], ACT.Tanh).then_inc(activated, 1)
                        for g in range(4):
                            act.wait_ge(projected, g + 1)
                            for k in range(2):
                                act.activation(aT[:, 2 * g + k, :], sp_[:, 2 + g % 2, k * TOK:(k + 1) * TOK], ACT.Sigmoid,
                                               bias=par("a0", 2 * g + k)).then_inc(activated, 1)

        def mix_stage():
            pp = area(A0, 24, TOK + 1)
            rkv = area(18448, 24)
            with ExitStack() as e:
                differed, mixed = local(e, "differed"), local(e, "mixed")
                with nc.Block() as block:
                    @block.vector
                    def _(v):
                        v.tensor_tensor(rkv, pp[:, :, 0:TOK], pp[:, :, 1:TOK + 1], ALU.subtract).then_inc(differed, 1)
                        v.wait_ge(differed, 1)
                        with v.Fori(0, 24) as c:
                            v.scalar_tensor_tensor(rkv[:, at(c, 1), :], rkv[:, at(c, 1), :],
                                                   prm[:, at(c + rows["mu_rkv"], 1)],
                                                   pp[:, at(c, 1), 1:TOK + 1], ALU.mult, ALU.add).then_inc(mixed, 1)

        def bias_table_ap(table, stride, offset):
            return bass.AP(table.tensor, offset, [[1, P], [stride, 16], [1, TOK]])

        masks_made = sem("masks_made")

        def masks_stage():
            with ExitStack() as e:
                filled, made = local(e, "filled"), local(e, "made")
                with nc.Block() as block:
                    @block.gpsimd
                    def _(pool):
                        pool.memset(consts[:, 0:832], 1.0).then_inc(filled, 1)
                        pool.memset(tri128, 1.0).then_inc(filled, 1)
                        pool.wait_ge(filled, 2)
                        n = 0
                        def keep(ap, base, pattern, mult, op=ALU.is_ge, fill=0.0):
                            nonlocal n
                            n += 1
                            pool.affine_select(out=ap, in_=ap, compare_op=op, fill=fill, base=base,
                                               pattern=pattern, channel_multiplier=mult).then_inc(made, 1)
                            pool.wait_ge(made, n)
                        keep(tri128, 0, [[1, P]], -1)
                        keep(tri[:, 0:128], 0, [[1, P]], -1)
                        keep(tri[:, 128:256], -1, [[1, P]], -1)
                        for q in range(2):
                            pool.memset(tri[0:64, 128 * q + 64:128 * q + 128], 0.0).then_inc(made, 1)
                            n += 1
                            pool.wait_ge(made, n)
                        for q in range(2):
                            half = slice(64 * q, 64 * q + 64)
                            keep(mask_su[half, 0:64], -1, [[1, 64]], -1)
                            keep(mask_su[half, 64:128], 0, [[1, 64]], -1)
                            keep(eye2[half, :], 0, [[1, 64]], -1, ALU.is_equal)
                            for l in range(6):
                                w = 1 << l
                                v4 = level[half, l, :].rearrange("p (b u w) -> p b u w", u=2, w=w)
                                pat = [[2 * w, 32 // w], [0, 2], [0, w]]
                                pool.memset(v4[:, :, 0, :], 0.0).then_inc(made, 1)
                                n += 1
                                pool.wait_ge(made, n)
                                keep(v4, 0, [[-2 * w, 32 // w], [0, 2], [0, w]], 1)
                                keep(v4, w - 1, pat, -1)
                        pool.wait_ge(made, n)
                        pool.memset(smalls[:, 0:1], 0.0).then_inc(masks_made, 1)
        def attention1_stage():
            q = area(A0 + 2048, BC)
            kk, vv, za = area(A0 + 4096, BC), area(A0 + 6144, BC), area(A0 + 8192, BC)
            bt = area(26640, 16)
            base = 30740
            q_st, k_st, v_st = (arena[:, base + n * TOK:base + (n + 1) * TOK] for n in range(3))
            sc = arena[:, base + 768:base + 1536].rearrange("p (h s) -> p h s", h=2)
            v_tok = arena[:, base + 1536:base + 1792].rearrange("p (t c) -> p t c", t=2)
            p_t = p_turned[:, :]
            small = smalls[:, :]
            DV = ["q_staged", "scored0", "scored1", "max0", "max0b", "max1", "max1b",
                  "rec0", "prob0", "rec1", "prob1", "gated"]
            AC = ["k_staged", "v_staged", "v_turned", "e0", "e0b", "e1", "e1b", "pt0", "pt1"]
            PE = ["v_tok", "s0", "s1", "turned0", "o0", "turned1", "o1"]
            with ExitStack() as e:
                table_loaded, table_masked = local(e, "table_loaded"), local(e, "table_masked")
                dv, ac, pe_ = Steps(e, "att_vector", DV), Steps(e, "att_scalar", AC), Steps(e, "att_tensor", PE)
                with nc.Block() as block:
                    @block.sync
                    def _(sp):
                        sp.dma_start(bt, bias_table_ap(I["rel_bias"], 513, 129)).then_inc(table_loaded, 16)

                    @block.gpsimd
                    def _(pool):
                        pool.wait_ge(table_loaded, 16)
                        pool.memset(bt[0:64, :, 0:64], NEG).then_inc(table_masked, 1)

                    @block.vector
                    def _(v):
                        v.wait_ge(table_masked, 1)
                        with v.Fori(0, BC) as j:
                            dv.did(v.tensor_scalar(q_st, q[:, at(j, 1), :], 0.125, None, ALU.mult), "q_staged")
                            for hh in range(2):
                                pe_.wait(v, f"s{hh}", j)
                                v.tensor_tensor(sc[:, hh, 0:128], sp_[:, hh, 0:128],
                                                bt[:, at(j * 2 + hh, 1), 0:128], ALU.add)
                                dv.did(v.tensor_tensor(sc[:, hh, 128:384], sp_[:, hh, 128:384],
                                                       bt[:, at(j * 2 + hh, 1), :], ALU.add), f"scored{hh}")
                            for hh in range(2):
                                dv.wait(v, f"scored{hh}", j)
                                dv.did(v.tensor_reduce(small[:, 4 * hh:4 * hh + 1], sc[:, hh, 0:128], AX, ALU.max, negate=True), f"max{hh}")
                                dv.did(v.tensor_reduce(small[:, 4 * hh + 1:4 * hh + 2], sc[:, hh, 128:384], AX, ALU.max, negate=True), f"max{hh}b")
                            for hh in range(2):
                                ac.wait(v, f"e{hh}b", j)
                                dv.did(v.reciprocal(small[:, 4 * hh + 2:4 * hh + 4], small[:, 8 + 2 * hh:10 + 2 * hh]), f"rec{hh}")
                                dv.wait(v, f"rec{hh}", j)
                                v.tensor_scalar(sc[:, hh, 0:128], sc[:, hh, 0:128], small[:, 4 * hh + 2:4 * hh + 3], None, ALU.mult)
                                dv.did(v.tensor_scalar(sc[:, hh, 128:384], sc[:, hh, 128:384], small[:, 4 * hh + 3:4 * hh + 4], None, ALU.mult), f"prob{hh}")
                            pe_.wait(v, "o1", j)
                            dv.did(v.tensor_tensor(q[:, at(j, 1), :], sp_[:, 3, 0:TOK], za[:, at(j, 1), :], ALU.mult), "gated")

                    @block.scalar
                    def _(act):
                        with act.Fori(0, BC) as j:
                            dv.wait(act, "q_staged", j)
                            ac.did(act.activation(k_st[:, ::-1], kk[:, at(j, 1), :].rearrange("p o t -> p (o t)"), ACT.Copy), "k_staged")
                            ac.did(act.activation(v_st[:, ::-1], vv[:, at(j, 1), :].rearrange("p o t -> p (o t)"), ACT.Copy), "v_staged")
                            pe_.wait(act, "v_tok", j)
                            ac.did(act.activation(v_tok, sp_[:, 3, 256:512].rearrange("p (t c) -> p t c", t=2), ACT.Copy), "v_turned")
                            for hh in range(2):
                                dv.wait(act, f"max{hh}b", j)
                                ac.did(act.activation(sc[:, hh, 0:128], sc[:, hh, 0:128], ACT.Exp, bias=small[:, 4 * hh:4 * hh + 1],
                                                      accum_out=small[:, 8 + 2 * hh:9 + 2 * hh]), f"e{hh}")
                                ac.did(act.activation(sc[:, hh, 128:384], sc[:, hh, 128:384], ACT.Exp, bias=small[:, 4 * hh + 1:4 * hh + 2],
                                                      accum_out=small[:, 9 + 2 * hh:10 + 2 * hh]), f"e{hh}b")
                            for hh in range(2):
                                pe_.wait(act, f"turned{hh}", j)
                                if hh:
                                    pe_.wait(act, "o0", j)
                                ac.did(act.activation(p_t, sp_[:, 2, 0:384], ACT.Copy), f"pt{hh}")

                    @block.tensor
                    def _(pe):
                        with pe.Fori(0, BC) as j:
                            ac.wait(pe, "v_staged", j)
                            for t in range(2):
                                m = pe.transpose(sp_[:, 3, 256 + t * P:256 + (t + 1) * P], v_st[:, t * P:(t + 1) * P], ident[:, :])
                            pe_.did(m, "v_tok")
                            for hh in range(2):
                                hs = slice(64 * hh, 64 * hh + 64)
                                pe.matmul(sp_[:, hh, 0:128], q_st[hs, 0:128], k_st[hs, 128:256], start=True, stop=True)
                                pe_.did(pe.matmul(sp_[:, hh, 128:384], q_st[hs, 128:256], k_st[hs, :], start=True, stop=True, skip_group_check=True), f"s{hh}")
                            ac.wait(pe, "v_turned", j)
                            for hh in range(2):
                                hs = slice(64 * hh, 64 * hh + 64)
                                dv.wait(pe, f"prob{hh}", j)
                                if hh:
                                    ac.wait(pe, "pt0", j)
                                for n in range(3):
                                    m = pe.transpose(sp_[:, 2, n * P:(n + 1) * P], sc[:, hh, n * P:(n + 1) * P], ident[:, :])
                                pe_.did(m, f"turned{hh}")
                                ac.wait(pe, f"pt{hh}", j)
                                pe.matmul(sp_[hs, 3, 0:128], v_tok[:, 1, hs], p_t[:, 0:128], start=True, stop=True, skip_group_check=True)
                                pe.matmul(sp_[hs, 3, 128:256], v_tok[:, 0, hs], p_t[:, 128:256], start=True, stop=False, skip_group_check=True)
                                pe_.did(pe.matmul(sp_[hs, 3, 128:256], v_tok[:, 1, hs], p_t[:, 256:384], start=False, stop=True, skip_group_check=True), f"o{hh}")

        def rwkv_stage():
            r_, k_, v_, a_ = area(18448, BC), area(20496, BC), area(22544, BC), area(24592, BC)
            zr = area(A0, BC)
            o = [12304]
            def buf(n):
                o[0] += n
                assert o[0] <= 16400 or o[0] - n >= 26640
                return arena[:, o[0] - n:o[0]]
            sg = buf(256).rearrange("p (t c) -> p t c", t=2)
            p_in, p_ex, p_inv = buf(256), buf(256), buf(256)
            kn, sqr, inv, kmod, tmp = buf(256), buf(256), buf(256), buf(256), buf(256)
            zrb = buf(512).rearrange("p (c g t) -> p c g t", c=4, g=2)
            b_t, k_t = buf(256), buf(256)
            tok = buf(768).rearrange("p (g c n) -> p g c n", g=3, c=4)
            assert o[0] <= 16400, o[0]
            o[0] = 26640
            ab = buf(512).rearrange("p (c s) -> p c s", c=4)
            ak = buf(512).rearrange("p (c s) -> p c s", c=4)
            al = buf(512).rearrange("p (u c s) -> p u c s", u=2, c=4)
            xx = buf(512).rearrange("p (u c s) -> p u c s", u=2, c=4)
            yb = buf(256).rearrange("p (c s) -> p c s", c=4)
            w0b, stp = buf(64), buf(64)
            states = (buf(64), buf(64))
            sa = buf(256).rearrange("p (c s) -> p c s", c=4)
            pc = buf(4)
            v_st, rk, bonus, y, ysq = buf(256), buf(256), buf(256), buf(256), buf(256)
            c4 = lambda x: x.rearrange("p (c t) -> p c t", c=4)
            th = lambda x: x.rearrange("p (h t) -> p h t", h=2)
            over4 = lambda m, w: m.rearrange("p (o t) -> p o t", o=1).to_broadcast([P, 4, w])
            eye4 = over4(eye2, 64)
            HS = [slice(0, 64), slice(64, 128)]

            DV = ["kk", "kk_squared", "a_scaled", "kmod", "rk", "norm_floored", "norm_inverted", "kk_normed",
                  "kka", "r_hat", "z_hat", "b_hat", "k_hat", "ab", "ak", "al0", "xt0", "x0"]
            for l in range(1, 6):
                DV += [f"al{l}", f"xx{l}"]
            for c in range(4):
                DV += [f"sa{c}"] + ([f"st_sum{c}", f"st{c}"] if 0 < c < 3 else [f"st{c}"] if c == 0 else [])
            DV += ["y_centred", "variance", "deviation_inverted", "y_normed", "y_scaled", "bonus_v", "y_bonus", "y_gated"]
            AC = ["v_staged", "decay", "root", "p_in", "p_ex", "p_inv", "p_chunk", "tok_vb", "tok_k", "bonus"]
            AC += [f"y{l}" for l in range(1, 6)] + [f"w{c}" for c in range(4)] + ["y_out", "y_squared", "deviation"]
            PE = ["decay_logits", "kk_norm", "cumulated", "ab", "ak", "tok_vb", "tok_k", "bonus", "n0"]
            for l in range(1, 6):
                PE += [f"y{l}", f"xx{l}"]
            for c in range(4):
                PE += [f"w{c}", f"sa{c}"] + ([f"st{c}"] if c < 3 else [])
            PE += ["o", "mean", "var"]

            with ExitStack() as e:
                waited = local(e, "rwkv_tensor_waited")
                dv, ac, pe_ = Steps(e, "rwkv_vector", DV), Steps(e, "rwkv_scalar", AC), Steps(e, "rwkv_tensor", PE)
                with nc.Block() as block:
                    @block.vector
                    def _(v):
                        with v.Fori(0, BC) as j:
                            one = at(j, 1)
                            pr = lambda name: prm[:, at(j + rows[name], 1)]
                            dv.did(v.tensor_scalar(kn, k_[:, one, :], pr("k_k"), None, ALU.mult), "kk")
                            dv.wait(v, "kk", j)
                            dv.did(v.tensor_tensor(sqr, kn, kn, ALU.mult), "kk_squared")
                            dv.did(v.tensor_scalar(kmod, a_[:, one, :], pr("k_a"), omka[:, one], ALU.mult, ALU.add), "a_scaled")
                            dv.wait(v, "a_scaled", j)
                            dv.did(v.tensor_tensor(kmod, kmod, k_[:, one, :], ALU.mult), "kmod")
                            dv.wait(v, "kmod", j)
                            dv.did(v.scalar_tensor_tensor(rk, r_[:, one, :], pr("r_k"), kmod, ALU.mult, ALU.mult), "rk")
                            ac.wait(v, "root", j)
                            dv.did(v.tensor_scalar(inv, inv, 1e-12, None, ALU.max), "norm_floored")
                            dv.wait(v, "norm_floored", j)
                            dv.did(v.reciprocal(inv, inv), "norm_inverted")
                            dv.wait(v, "norm_inverted", j)
                            dv.did(v.tensor_tensor(kn, kn, inv, ALU.mult), "kk_normed")
                            dv.wait(v, "kk_normed", j)
                            dv.did(v.tensor_tensor(tmp, kn, a_[:, one, :], ALU.mult), "kka")
                            ac.wait(v, "p_inv", j)
                            dv.did(v.tensor_tensor(zrb[:, :, 1, :], c4(r_[:, one, :].rearrange("p o t -> p (o t)")), c4(p_in), ALU.mult), "r_hat")
                            dv.did(v.scalar_tensor_tensor(zrb[:, :, 0, :], c4(kn), -1.0, c4(p_ex), ALU.mult, ALU.mult), "z_hat")
                            dv.wait(v, "kka", j)
                            dv.did(v.tensor_tensor(b_t, tmp, p_inv, ALU.mult), "b_hat")
                            dv.did(v.tensor_tensor(k_t, kmod, p_inv, ALU.mult), "k_hat")
                            m4 = over4(mask_su, 128)
                            pe_.wait(v, "ab", j)
                            dv.did(v.tensor_tensor(ab, sp_[:, 0, :].rearrange("p (c s) -> p c s", c=4), m4, ALU.mult), "ab")
                            pe_.wait(v, "ak", j)
                            dv.did(v.tensor_tensor(ak, sp_[:, 3, :].rearrange("p (c s) -> p c s", c=4), m4, ALU.mult), "ak")
                            dv.wait(v, "ab", j)
                            dv.did(v.tensor_tensor(al[:, 0], ab[:, :, 0:64], over4(level[:, 0, :], 64), ALU.mult), "al0")
                            dv.wait(v, "al0", j)
                            dv.did(v.tensor_tensor(xx[:, 1], al[:, 0], eye4, ALU.add), "xt0")
                            pe_.wait(v, "n0", j)
                            dv.did(v.tensor_tensor(xx[:, 0], sp_[:, 0, 0:256].rearrange("p (c s) -> p c s", c=4), eye4, ALU.add), "x0")
                            for l in range(1, 6):
                                if l >= 2:
                                    pe_.wait(v, f"xx{l - 1}", j)
                                dv.did(v.tensor_tensor(al[:, l % 2], ab[:, :, 0:64], over4(level[:, l, :], 64), ALU.mult), f"al{l}")
                                pe_.wait(v, f"xx{l}", j)
                                dv.wait(v, f"xx{l - 1}" if l > 1 else "x0", j)
                                dv.did(v.tensor_tensor(xx, sp_[:, 1, :].rearrange("p (u c s) -> p u c s", u=2, c=4), xx, ALU.add), f"xx{l}")
                            for c in range(4):
                                pe_.wait(v, f"sa{c}", j)
                                dv.did(v.tensor_copy(sa[:, c, :], sp_[:, 1, 0:64]), f"sa{c}")
                                if c == 0:
                                    pe_.wait(v, "st0", j)
                                    dv.did(v.tensor_scalar(states[0], sp_[:, 3, 0:64], pc[:, 0:1], None, ALU.mult), "st0")
                                elif c < 3:
                                    pe_.wait(v, f"st{c}", j)
                                    dv.did(v.tensor_tensor(stp, sp_[:, 3, 0:64], states[(c - 1) % 2], ALU.add), f"st_sum{c}")
                                    dv.wait(v, f"st_sum{c}", j)
                                    dv.did(v.tensor_scalar(states[c % 2], stp, pc[:, c:c + 1], None, ALU.mult), f"st{c}")
                            pe_.wait(v, "mean", j)
                            dv.did(v.scalar_tensor_tensor(y, sp_[:, 0, 0:256], -1.0 / 64, y, ALU.mult, ALU.add), "y_centred")
                            pe_.wait(v, "var", j)
                            dv.did(v.tensor_scalar(inv, sp_[:, 1, 0:256], 1.0 / 64, 64e-5, ALU.mult, ALU.add), "variance")
                            ac.wait(v, "deviation", j)
                            dv.did(v.reciprocal(inv, inv), "deviation_inverted")
                            dv.wait(v, "deviation_inverted", j)
                            dv.did(v.tensor_tensor(y, y, inv, ALU.mult), "y_normed")
                            dv.wait(v, "y_normed", j)
                            dv.did(v.tensor_scalar(y, y, pr("ln_g"), pr("ln_b"), ALU.mult, ALU.add), "y_scaled")
                            dv.did(v.tensor_tensor(bonus, bonus, v_st, ALU.mult), "bonus_v")
                            dv.wait(v, "bonus_v", j)
                            dv.did(v.tensor_tensor(y, y, bonus, ALU.add), "y_bonus")
                            dv.wait(v, "y_bonus", j)
                            dv.did(v.tensor_tensor(zr[:, one, :], y, zr[:, one, :], ALU.mult), "y_gated")
                            dv.wait(v, "y_gated", j)

                    @block.scalar
                    def _(act):
                        with act.Fori(0, BC) as j:
                            dv.wait(act, "kk", j)
                            ac.did(act.activation(v_st, v_[:, at(j, 1), :].rearrange("p o t -> p (o t)"), ACT.Copy), "v_staged")
                            pe_.wait(act, "decay_logits", j)
                            ac.did(act.activation(sg, sp_[:, 0, 0:256].rearrange("p (t c) -> p t c", t=2), ACT.Sigmoid), "decay")
                            pe_.wait(act, "kk_norm", j)
                            ac.did(act.activation(inv, sp_[:, 1, 0:256], ACT.Sqrt), "root")
                            pe_.wait(act, "cumulated", j)
                            cum = sp_[:, 2, :].rearrange("p (h g t) -> p h g t", h=2, g=2)
                            ac.did(act.activation(th(p_in), cum[:, :, 0, :], ACT.Exp, bias=centre[:, 0:1], scale=-DECAY), "p_in")
                            ac.did(act.activation(th(p_ex), cum[:, :, 1, :], ACT.Exp, bias=centre[:, 0:1], scale=-DECAY), "p_ex")
                            ac.did(act.activation(th(p_inv), cum[:, :, 0, :], ACT.Exp, bias=centre[:, 1:2], scale=DECAY), "p_inv")
                            ac.did(act.activation(pc.rearrange("p (h c) -> p h c", h=2), cum[:, :, 0, 63:128:64], ACT.Exp, scale=-DECAY), "p_chunk")
                            pe_.wait(act, "tok_vb", j)
                            ac.did(act.activation(tok[:, 0:2], sp_[:, 2, :].rearrange("p (g c n) -> p g c n", g=2, c=4), ACT.Copy), "tok_vb")
                            pe_.wait(act, "bonus", j)
                            ac.did(act.activation(tok[:, 2], sp_[:, 1, 256:512].rearrange("p (c n) -> p c n", c=4), ACT.Copy), "tok_k")
                            ac.did(act.activation(bonus, sp_[:, 1, 0:256], ACT.Copy), "bonus")
                            for l in range(1, 6):
                                pe_.wait(act, f"y{l}", j)
                                ac.did(act.activation(yb, sp_[:, 0, 0:256].rearrange("p (c s) -> p c s", c=4), ACT.Copy), f"y{l}")
                            for c in range(4):
                                pe_.wait(act, f"w{c}", j)
                                ac.did(act.activation(w0b, sp_[:, 0, 0:64], ACT.Copy), f"w{c}")
                            pe_.wait(act, "o", j)
                            ac.did(act.activation(y, sp_[:, 2, 0:256], ACT.Copy), "y_out")
                            dv.wait(act, "y_centred", j)
                            ac.did(act.activation(ysq, y, ACT.Square), "y_squared")
                            dv.wait(act, "variance", j)
                            ac.did(act.activation(inv, inv, ACT.Sqrt), "deviation")

                    @block.tensor
                    def _(pe):
                        def wait(steps, step, j):
                            steps.wait(pe, step, j)
                            pe.sem_inc(waited, 1)

                        def mm(out, lhs, rhs, start=True, stop=True):
                            return pe.matmul(out, lhs, rhs, start=start, stop=stop, skip_group_check=True)
                        with pe.Fori(0, BC) as j:
                            wait(dv, "kk", j)
                            for t in range(2):
                                m = mm(sp_[:, 0, t * P:(t + 1) * P], t1[0:65, t * P:(t + 1) * P], w2p[0:65, at(j * P, P)])
                            pe_.did(m, "decay_logits")
                            wait(dv, "kk_squared", j)
                            pe_.did(mm(sp_[:, 1, 0:256], headones[:, :], sqr), "kk_norm")
                            wait(ac, "decay", j)
                            for t in range(2):
                                m = mm(sp_[:, 2, t * 256:(t + 1) * 256], sg[:, t, :], tri)
                            pe_.did(m, "cumulated")
                            wait(dv, "b_hat", j)
                            for c in range(4):
                                for s in HS:
                                    m = mm(sp_[s, 0, c * 128:(c + 1) * 128], b_t[s, c * 64:(c + 1) * 64], zrb[s, c].rearrange("p g t -> p (g t)"))
                            pe_.did(m, "ab")
                            wait(dv, "k_hat", j)
                            for c in range(4):
                                for s in HS:
                                    m = mm(sp_[s, 3, c * 128:(c + 1) * 128], k_t[s, c * 64:(c + 1) * 64], zrb[s, c].rearrange("p g t -> p (g t)"))
                            pe_.did(m, "ak")
                            wait(ac, "p_chunk", j)
                            for g, x in enumerate((v_st, b_t)):
                                for c in range(4):
                                    for s in HS:
                                        m = mm(sp_[s, 2, g * 256 + c * 64:g * 256 + (c + 1) * 64], x[s, c * 64:(c + 1) * 64], eye2[s, :])
                            pe_.did(m, "tok_vb")
                            for c in range(4):
                                for s in HS:
                                    m = mm(sp_[s, 1, 256 + c * 64:256 + (c + 1) * 64], k_t[s, c * 64:(c + 1) * 64], eye2[s, :])
                            pe_.did(m, "tok_k")
                            pe_.did(mm(sp_[:, 1, 0:256], headones[:, :], rk), "bonus")
                            wait(dv, "al0", j)
                            for c in range(4):
                                for s in HS:
                                    m = mm(sp_[s, 0, c * 64:(c + 1) * 64], al[s, 0, c, :], eye2[s, :])
                            pe_.did(m, "n0")
                            wait(ac, "bonus", j)
                            for l in range(1, 6):
                                wait(dv, f"al{l}", j)
                                wait(dv, "x0" if l == 1 else f"xx{l - 1}", j)
                                for c in range(4):
                                    for s in HS:
                                        m = mm(sp_[s, 0, c * 64:(c + 1) * 64], al[s, l % 2, c, :], xx[s, 0, c, :])
                                pe_.did(m, f"y{l}")
                                wait(ac, f"y{l}", j)
                                for c in range(4):
                                    for s in HS:
                                        mm(sp_[s, 1, c * 64:(c + 1) * 64], xx[s, 1, c, :], yb[s, c, :])
                                        m = mm(sp_[s, 1, 256 + c * 64:256 + (c + 1) * 64], yb[s, c, :], xx[s, 1, c, :])
                                pe_.did(m, f"xx{l}")
                            wait(dv, "xx5", j)
                            wait(dv, "ak", j)
                            for c in range(4):
                                if c:
                                    wait(dv, f"st{c - 1}", j)
                                for s in HS:
                                    if c:
                                        mm(sp_[s, 0, 0:64], zrb[s, c, 0, :], states[(c - 1) % 2][s, :], True, False)
                                    m = mm(sp_[s, 0, 0:64], ak[s, c, 0:64], tok[s, 0, c, :], c == 0, True)
                                pe_.did(m, f"w{c}")
                                wait(ac, f"w{c}", j)
                                for s in HS:
                                    m = mm(sp_[s, 1, 0:64], xx[s, 1, c, :], w0b[s, :])
                                pe_.did(m, f"sa{c}")
                                wait(dv, f"sa{c}", j)
                                if c < 3:
                                    for s in HS:
                                        mm(sp_[s, 3, 0:64], tok[s, 1, c, :], sa[s, c, :], True, False)
                                        m = mm(sp_[s, 3, 0:64], tok[s, 2, c, :], tok[s, 0, c, :], False, True)
                                    pe_.did(m, f"st{c}")
                                for s in HS:
                                    oc = sp_[s, 2, c * 64:(c + 1) * 64]
                                    if c:
                                        mm(oc, states[(c - 1) % 2][s, :], zrb[s, c, 1, :], True, False)
                                    mm(oc, sa[s, c, :], ab[s, c, 64:128], c == 0, False)
                                    m = mm(oc, tok[s, 0, c, :], ak[s, c, 64:128], False, True)
                                if c == 3:
                                    pe_.did(m, "o")
                            wait(ac, "y_out", j)
                            pe_.did(mm(sp_[:, 0, 0:256], headones[:, :], y), "mean")
                            wait(ac, "y_squared", j)
                            pe_.did(mm(sp_[:, 1, 0:256], headones[:, :], ysq), "var")
        def gates_evac(eng, i, b, ps):
            mg = area(18448, 32)
            for n in range(4):
                ins = eng.activation(mg[:, at(i * 8 + (b * 4 + n), 1), :], ps[:, n, :], ACT.Sigmoid,
                                     bias=prm[:, at(i * 8 + (b * 4 + n + rows["b_merge"]), 1)])
            return ins

        def branch_stage():
            s = S["branch"]
            b0 = blocks_before["branch"] // 2
            xs = (area(A0, BC), area(A0 + 2048, BC))
            mg, mer = area(18448, 32), area(12304, DC)
            part = area(26640, 4)
            with ExitStack() as e:
                gated_r, gated_a, added = local(e, "gated_r"), local(e, "gated_a"), local(e, "added")
                with nc.Block() as block:
                    @block.sync
                    def _(sp):
                        load_section(sp, s)

                    @block.tensor
                    def _(pe):
                        with pe.Fori(0, s.iters) as i:
                            for k in range(SLOTS):
                                pe.wait_ge(pair_evacuated[k % 2], i * 2 + (b0 + k // 2))
                                multiply_unit(pe, k, i * 16 + 16 * (s.unit0 // SLOTS + 1), k % 2,
                                              lambda c: xs[k % 2][:, c, :], True, True)

                    @block.vector
                    def _(v):
                        with v.Fori(0, s.iters) as i:
                            for b in range(2):
                                c = at(i * 8 + b * 4, 4)
                                v.wait_ge(unit_used, i * 4 + (s.unit0 + 2 * b + 1))
                                v.tensor_tensor(mer[:, c, :], gp[:, 0], mg[:, c, :], ALU.mult).then_inc(pair_evacuated[0], 1)
                                v.wait_ge(unit_used, i * 4 + (s.unit0 + 2 * b + 2))
                                v.tensor_tensor(part, gp[:, 1], mg[:, at(i * 8 + b * 4 + 16, 4), :], ALU.mult).then_inc(pair_evacuated[1], 1)
                                v.wait_ge(pair_evacuated[0], i * 2 + (b0 + b + 1))
                                v.wait_ge(pair_evacuated[1], i * 2 + (b0 + b + 1))
                                v.tensor_tensor(mer[:, c, :], mer[:, c, :], part, ALU.add).then_inc(added, 1)
                                v.wait_ge(added, i * 2 + (b + 1))
        qkvi = area(A0, 28)
        ki = arena[:, A0 + 7168:A0 + 7424]
        wi = arena[:, A0 + 7424:A0 + 7680]
        t2 = area(26640, 16)
        HEADS2, KV2 = 16, 4

        def bucket_edges():
            def bucket(n):
                if n < 16:
                    return n
                return min(16 + int(math.log(n / 16) / math.log(128 / 16) * 16 + 1e-9), 31)
            edges = []
            for b in range(32):
                ds = [n for n in range(TOK) if bucket(n) == b]
                edges.append((min(ds), max(ds) + 1) if ds else None)
            return edges

        scratch_rows = nc.dram_tensor("bias_rows", [16, 384], F32, kind="Internal").ap()

        def bias2_stage():
            by_bucket = arena[:, 30740:30772]
            by_dist = arena[:, 30772:31156]
            with ExitStack() as e:
                loaded, spread, stored, tabled = (local(e, x) for x in ("buckets_loaded", "spread", "rows_stored", "tabled"))
                with nc.Block() as block:
                    @block.sync
                    def _(sp):
                        with nc.allow_non_contiguous_dma(reason="512 numbers"):
                            sp.dma_start(by_bucket[0:16, :], I["rel_bias_2"].rearrange("b h -> h b")).then_inc(loaded, 16)
                        sp.wait_ge(spread, 33)
                        sp.dma_start(scratch_rows, by_dist[0:16, :]).then_inc(stored, 16)
                        sp.wait_ge(stored, 16)
                        sp.dma_start(t2, bass.AP(scratch_rows.tensor, 0, [[1, P], [384, 16], [1, TOK]])).then_inc(tabled, 16)
                        sp.wait_ge(tabled, 16)

                    @block.vector
                    def _(v):
                        v.wait_ge(loaded, 16)
                        v.tensor_copy(by_dist[0:16, 0:127], by_bucket[0:16, 0:1].to_broadcast([16, 127])).then_inc(spread, 1)
                        n = 0
                        for b, edge in enumerate(bucket_edges()):
                            lo, hi = edge
                            if b == 31:
                                hi = TOK + 1
                            v.tensor_copy(by_dist[0:16, 127 + lo:127 + hi],
                                          by_bucket[0:16, b:b + 1].to_broadcast([16, hi - lo])).then_inc(spread, 1)

        def index_evac(eng, i, b, ps):
            if b == 0:
                return eng.activation(qkvi[:, 24:28, :], ps, ACT.Copy)
            eng.activation(ki, ps[:, 0, :], ACT.Copy)
            return eng.activation(wi[0:8, :], ps[0:8, 1, :], ACT.Copy)

        def index_stage():
            s = S["index2"]
            b0 = blocks_before["index2"] // 2
            with nc.Block() as block:
                @block.sync
                def _(sp):
                    load_section(sp, s)

                @block.tensor
                def _(pe):
                    for k in range(SLOTS):
                        u, b = k % 2, k // 2
                        pe.wait_ge(pair_evacuated[b], b0)
                        pe.wait_ge(unit_loaded[k], 16 * (s.unit0 // SLOTS + 1))
                        if k >= 2:
                            pe.wait_ge(idx_extra_loaded, 64)
                        tiles = [(j * P, P) for j in range(4)] if b == 0 else [(0, P), (P, 8)]
                        for c in range(KG):
                            for j, (c0, w) in enumerate(tiles):
                                m = pe.matmul(gp[0:w, b, j, :], ring[:, k, c, c0:c0 + w], h[:, u * KG + c, :],
                                              start=(u == 0 and c == 0 and j % 2 == 0), stop=(u == 1 and c == KG - 1),
                                              skip_group_check=True)
                        m.then_inc(unit_used, 1)

                @block.scalar
                def _(act):
                    for b in range(2):
                        block_done(act, s, 0, b)
                        index_evac(act, 0, b, gp[:, b]).then_inc(pair_evacuated[b], 1)

        FAR, TAKEN = -1.0e38, -3.0e38
        kept = arena[:, 30740:31124]

        def select_stage():
            score = arena[:, 31124:31636].rearrange("p (h s) -> p h s", h=2)
            part = arena[:, 31636:32148].rearrange("p (h s) -> p h s", h=2)
            wt = smalls[:, 0:16].rearrange("p (t h) -> p t h", t=2)
            best = smalls[:, 16:32].rearrange("p (t n) -> p t n", t=2)
            with ExitStack() as e:
                turned, wt_ready, scored, weighed, masked, picked = (
                    local(e, x) for x in ("wi_turned", "wi_ready", "scored", "weighed", "masked", "picked"))
                with nc.Block() as block:
                    @block.tensor
                    def _(pe):
                        for t in range(2):
                            m = pe.transpose(sp_[:, 0, t * 8:(t + 1) * 8], wi[0:8, t * P:(t + 1) * P], ident[0:8, 0:8])
                        m.then_inc(turned, 1)
                        pe.wait_ge(wt_ready, 1)
                        for n in range(8):
                            s = slice(64 * (n % 2), 64 * (n % 2) + 64)
                            if n >= 4:
                                pe.wait_ge(weighed, n - 3)
                            for t in range(2):
                                m = pe.matmul(sp_[:, n % 4, t * TOK:(t + 1) * TOK], qkvi[s, 24 + n // 2, t * P:(t + 1) * P],
                                              ki[s, :], start=True, stop=True, skip_group_check=True)
                            m.then_inc(scored, 1)

                    @block.vector
                    def _(v):
                        v.wait_ge(turned, 1)
                        v.tensor_scalar(wt, sp_[:, 0, 0:16].rearrange("p (t h) -> p t h", t=2),
                                        (8 ** -0.5) * (64 ** -0.5), None, ALU.mult).then_inc(wt_ready, 1)
                        v.wait_ge(wt_ready, 1)
                        steps = 0
                        for n in range(8):
                            v.wait_ge(scored, n + 1)
                            dst = part if n else score
                            if n > 1:
                                v.wait_ge(masked, n - 1)
                            for t in range(2):
                                ins = v.tensor_scalar(dst[:, t, :], sp_[:, n % 4, t * TOK:(t + 1) * TOK], 0.0,
                                                      wt[:, t, n:n + 1], ALU.max, ALU.mult)
                            ins.then_inc(weighed, 1)
                            if n:
                                v.wait_ge(weighed, n + 1)
                                v.tensor_tensor(score, score, part, ALU.add).then_inc(masked, 1)
                        v.wait_ge(masked, 8)
                        for n in range(8):
                            for t in range(2):
                                if n:
                                    v.wait_ge(picked, 4 * n - 1 + t)
                                v.max(best[:, t, :], score[:, t, :]).then_inc(picked, 1)
                            for t in range(2):
                                v.wait_ge(picked, 4 * n + 1 + t)
                                v.match_replace(score[:, t, :], best[:, t, :], score[:, t, :], TAKEN).then_inc(picked, 1)
                        v.wait_ge(picked, 32)
                        for t, (c0, w) in enumerate(((0, 128), (128, 256))):
                            v.tensor_scalar(kept[:, c0:c0 + w], score[:, t, w - 1::-1], -2.0e38, NEG, ALU.is_gt, ALU.mult).then_inc(picked, 1)

                    @block.gpsimd
                    def _(pool):
                        pool.wait_ge(masked, 7)
                        pool.affine_select(out=score, in_=score, compare_op=ALU.is_ge, fill=FAR, base=0,
                                           pattern=[[P, 2], [-1, TOK]], channel_multiplier=1).then_inc(masked, 1)
                        pool.wait_ge(picked, 34)
                        pool.affine_select(out=kept[:, 0:128], in_=kept[:, 0:128], compare_op=ALU.is_ge, fill=NEG,
                                           base=-127, pattern=[[1, 128]], channel_multiplier=1).then_inc(masked, 1)
                        pool.wait_ge(masked, 9)
                        pool.affine_select(out=kept[:, 128:384], in_=kept[:, 128:384], compare_op=ALU.is_ge, fill=NEG,
                                           base=-127, pattern=[[1, TOK]], channel_multiplier=1).then_inc(masked, 1)

        def attention_stage(q, k_of, v_of, groups, rep, scale, logits, weigh, nlog, scratch):
            q_st, v_st = arena[:, scratch:scratch + 256], arena[:, scratch + 256:scratch + 512]
            v_tok = arena[:, scratch + 512:scratch + 768].rearrange("p (t c) -> p t c", t=2)
            sc = arena[:, scratch + 768:scratch + 1152]
            k_st = arena[:, scratch + 1152:scratch + 1408]
            small = smalls[:, :]
            p_t = p_turned[:, :]
            DV, AC, PE = ["v_staged", "k_staged"], ["v_tok"], ["v_tok"]
            for r in range(rep):
                DV += [f"q{r}"] + [f"log{r}_{n}" for n in range(nlog)] + [f"max{r}", f"maxb{r}", f"w{r}", f"rec{r}", f"p{r}", f"out{r}"]
                AC += [f"e{r}", f"pt{r}"]
                PE += [f"s{r}", f"t{r}", f"o{r}"]
            with ExitStack() as e:
                dv, ac, pe_ = Steps(e, "att_vector", DV), Steps(e, "att_scalar", AC), Steps(e, "att_tensor", PE)
                with nc.Block() as block:
                    @block.vector
                    def _(v):
                        with v.Fori(0, groups) as g:
                            dv.did(v.tensor_scalar(v_st[:, ::-1], v_of(g).rearrange("p o t -> p (o t)"), 1.0, None, ALU.mult), "v_staged")
                            dv.did(v.tensor_scalar(k_st[:, ::-1], k_of(g).rearrange("p o t -> p (o t)"), 1.0, None, ALU.mult), "k_staged")
                            for r in range(rep):
                                head = g * rep + r
                                dv.did(v.tensor_scalar(q_st, q[:, at(head, 1), :].rearrange("p o t -> p (o t)"), scale, None, ALU.mult), f"q{r}")
                                pe_.wait(v, f"s{r}", g)
                                logits(v, dv, g, r, head, sp_[:, 0, 0:384], sc)
                                dv.wait(v, f"log{r}_{nlog - 1}", g)
                                dv.did(v.tensor_reduce(small[:, 0:1], sc[:, 0:128], AX, ALU.max, negate=True), f"max{r}")
                                dv.did(v.tensor_reduce(small[:, 1:2], sc[:, 128:384], AX, ALU.max, negate=True), f"maxb{r}")
                                ac.wait(v, f"e{r}", g)
                                weigh(v, g, sc, small)
                                dv.did(v.tensor_copy(small[:, 8:10], small[:, 4:6]), f"w{r}")
                                dv.wait(v, f"w{r}", g)
                                dv.did(v.reciprocal(small[:, 2:4], small[:, 8:10]), f"rec{r}")
                                dv.wait(v, f"rec{r}", g)
                                v.tensor_scalar(sc[:, 0:128], sc[:, 0:128], small[:, 2:3], None, ALU.mult)
                                dv.did(v.tensor_scalar(sc[:, 128:384], sc[:, 128:384], small[:, 3:4], None, ALU.mult), f"p{r}")
                                pe_.wait(v, f"o{r}", g)
                                dv.did(v.tensor_scalar(q[:, at(head, 1), :], sp_[:, 3, 0:TOK].rearrange("p (o t) -> p o t", o=1), 1.0, None, ALU.mult), f"out{r}")
                                dv.wait(v, f"out{r}", g)

                    @block.scalar
                    def _(act):
                        with act.Fori(0, groups) as g:
                            pe_.wait(act, "v_tok", g)
                            ac.did(act.activation(v_tok, sp_[:, 2, 0:256].rearrange("p (t c) -> p t c", t=2), ACT.Copy), "v_tok")
                            for r in range(rep):
                                dv.wait(act, f"maxb{r}", g)
                                act.activation(sc[:, 0:128], sc[:, 0:128], ACT.Exp, bias=small[:, 0:1], accum_out=small[:, 4:5])
                                ac.did(act.activation(sc[:, 128:384], sc[:, 128:384], ACT.Exp, bias=small[:, 1:2], accum_out=small[:, 5:6]), f"e{r}")
                                pe_.wait(act, f"t{r}", g)
                                ac.did(act.activation(p_t, sp_[:, 1, 0:384], ACT.Copy), f"pt{r}")

                    @block.tensor
                    def _(pe):
                        with pe.Fori(0, groups) as g:
                            dv.wait(pe, "v_staged", g)
                            for t in range(2):
                                m = pe.transpose(sp_[:, 2, t * P:(t + 1) * P], v_st[:, t * P:(t + 1) * P], ident[:, :])
                            pe_.did(m, "v_tok")
                            for r in range(rep):
                                dv.wait(pe, f"q{r}", g)
                                pe.matmul(sp_[:, 0, 0:128], q_st[:, 0:128], k_st[:, 128:256], start=True, stop=True, skip_group_check=True)
                                pe_.did(pe.matmul(sp_[:, 0, 128:384], q_st[:, 128:256], k_st, start=True, stop=True, skip_group_check=True), f"s{r}")
                                dv.wait(pe, f"p{r}", g)
                                for n in range(3):
                                    m = pe.transpose(sp_[:, 1, n * P:(n + 1) * P], sc[:, n * P:(n + 1) * P], ident[:, :])
                                pe_.did(m, f"t{r}")
                                ac.wait(pe, f"pt{r}", g)
                                pe.matmul(sp_[:, 3, 0:128], v_tok[:, 1, :], p_t[:, 0:128], start=True, stop=True, skip_group_check=True)
                                pe.matmul(sp_[:, 3, 128:256], v_tok[:, 0, :], p_t[:, 128:256], start=True, stop=False, skip_group_check=True)
                                pe_.did(pe.matmul(sp_[:, 3, 128:256], v_tok[:, 1, :], p_t[:, 256:384], start=False, stop=True, skip_group_check=True), f"o{r}")

        def attention2_stage():
            def logits(v, dv, g, r, head, ps, sc):
                v.tensor_tensor(sc[:, 0:128], ps[:, 0:128], t2[:, at(head, 1), 0:128].rearrange("p o t -> p (o t)"), ALU.add)
                dv.did(v.tensor_tensor(sc[:, 128:384], ps[:, 128:384], t2[:, at(head, 1), :].rearrange("p o t -> p (o t)"), ALU.add), f"log{r}_0")
                dv.wait(v, f"log{r}_0", g)
                dv.did(v.tensor_tensor(sc, sc, kept, ALU.add), f"log{r}_1")
            attention_stage(area(A0, 16), lambda g: area(A0, 28)[:, at(g + 16, 1), :], lambda g: area(A0, 28)[:, at(g + 20, 1), :],
                            KV2, HEADS2 // KV2, 128 ** -0.5, logits, lambda v, g, sc, small: None, 2, 31156)

        def sgu_stage():
            u, vv = area(15888, DC), area(19984, DC)
            sq = area(24080, DC)
            ws = arena[:, 28176:30224].rearrange("p (g s) -> p g s", g=16)
            bs = arena[:, 30224:32272].rearrange("p (g s) -> p g s", g=16)
            vn, ws_st = variance_t[:, :], p_turned[:, 256:384]
            tok = sq_tok = arena[:, 24080:24464].rearrange("p (n s) -> p n s", n=3)
            mean = variance[:, :]
            DV = ["normed", "shifted", "w_turned", "out"]
            AC = ["w_staged", "tok"]
            PE = ["turned", "mixed"]
            with ExitStack() as e:
                loaded, summed, meaned, centred, squared, summed2, meaned2, rooted, inverted = (
                    local(e, x) for x in ("sgu_loaded", "summed", "meaned", "centred", "squared", "summed2", "meaned2", "rooted", "inverted"))
                dv, ac, pe_ = Steps(e, "sgu_vector", DV), Steps(e, "sgu_scalar", AC), Steps(e, "sgu_tensor", PE)
                with nc.Block() as block:
                    @block.sync
                    def _(sp):
                        for q in range(4):
                            sp.dma_start(ws[:, 4 * q:4 * q + 4], I["sgu_w_2"][0, 4 * q:4 * q + 4].rearrange("g t s -> t g s")).then_inc(loaded, 16)
                        sp.dma_start(bs[0:1], I["sgu_b_2"]).then_inc(loaded, 16)
                        sp.wait_ge(loaded, 80)

                    @block.vector
                    def _(v):
                        v.wait_ge(summed, 1)
                        v.tensor_scalar(mean, sp_[:, 0, 0:TOK], 1.0 / D, None, ALU.mult).then_inc(meaned, 1)
                        v.wait_ge(meaned, 1)
                        for q in range(4):
                            v.tensor_tensor(vv[:, 4 * q:4 * q + 4, :], vv[:, 4 * q:4 * q + 4, :],
                                            mean.rearrange("p (o t) -> p o t", o=1).to_broadcast([P, 4, TOK]),
                                            ALU.subtract).then_inc(centred, 1)
                        v.wait_ge(centred, 4)
                        inv_root(v, sp_[:, 1, 0:TOK], D, summed2, meaned2, rooted, inverted)
                        with v.Fori(0, 16) as g:
                            dv.did(v.scalar_tensor_tensor(vn, vv[:, at(g, 1), :].rearrange("p o t -> p (o t)"),
                                                          prm[:, at(g + rows["sgu_g"], 1)], rstd[:, :], ALU.mult, ALU.mult), "normed")
                            dv.wait(v, "normed", g)
                            dv.did(v.tensor_scalar(vn, vn, prm[:, at(g + rows["sgu_b"], 1)], None, ALU.add), "shifted")
                            ac.wait(v, "tok", g)
                            pe_.wait(v, "turned", g)
                            dv.did(v.tensor_tensor(tok[:, 2, :], sp_[:, 3, 0:P], tri128, ALU.mult), "w_turned")
                            pe_.wait(v, "mixed", g)
                            dv.did(v.tensor_tensor(u[:, at(g, 1), :].rearrange("p o t -> p (o t)"), sp_[:, 0, 0:TOK],
                                                   u[:, at(g, 1), :].rearrange("p o t -> p (o t)"), ALU.mult), "out")

                    @block.scalar
                    def _(act):
                        for q in range(4):
                            act.wait_ge(centred, q + 1)
                            act.activation(sq[:, 4 * q:4 * q + 4, :], vv[:, 4 * q:4 * q + 4, :], ACT.Square).then_inc(squared, 1)
                        act.wait_ge(meaned2, 1)
                        act.activation(rstd[:, :], variance[:, :], ACT.Sqrt).then_inc(rooted, 1)
                        act.wait_ge(loaded, 80)
                        with act.Fori(0, 16) as g:
                            dv.wait(act, "normed", g)
                            ac.did(act.activation(ws_st, ws[:, at(g, 1), :].rearrange("p o t -> p (o t)"), ACT.Copy), "w_staged")
                            pe_.wait(act, "turned", g)
                            ac.did(act.activation(tok[:, 0:2, :], sp_[:, 2, 0:256].rearrange("p (n s) -> p n s", n=2), ACT.Copy), "tok")

                    @block.tensor
                    def _(pe):
                        for c in range(DC):
                            m = pe.matmul(sp_[:, 0, 0:TOK], ones[:, :], vv[:, c, :], start=(c == 0), stop=(c == DC - 1))
                        m.then_inc(summed, 1)
                        for c in range(DC):
                            pe.wait_ge(squared, c // 4 + 1)
                            m = pe.matmul(sp_[:, 1, 0:TOK], ones[:, :], sq[:, c, :], start=(c == 0), stop=(c == DC - 1))
                        m.then_inc(summed2, 1)
                        pe.wait_ge(loaded, 80)
                        with pe.Fori(0, 16) as g:
                            dv.wait(pe, "shifted", g)
                            ac.wait(pe, "w_staged", g)
                            for t in range(2):
                                pe.transpose(sp_[:, 2, t * P:(t + 1) * P], vn[:, t * P:(t + 1) * P], ident[:, :])
                            pe_.did(pe.transpose(sp_[:, 3, 0:P], ws_st, ident[:, :]), "turned")
                            dv.wait(pe, "w_turned", g)
                            for t in range(2):
                                pe.matmul(sp_[:, 0, t * P:(t + 1) * P], ones[0:1, :], bs[0:1, at(g, 1), :].rearrange("p o t -> p (o t)"),
                                          start=True, stop=False, skip_group_check=True)
                                m = pe.matmul(sp_[:, 0, t * P:(t + 1) * P], tok[:, t, :], tok[:, 2, :],
                                              start=False, stop=True, skip_group_check=True)
                            pe_.did(m, "mixed")

        def merge2_stage():
            att, u, ga, gb = area(A0, DC), area(15888, DC), area(24080, DC), area(28176, DC)
            with ExitStack() as e:
                gated, added = local(e, "gated"), local(e, "added")
                with nc.Block() as block:
                    @block.vector
                    def _(v):
                        v.tensor_tensor(att, att, ga, ALU.mult).then_inc(gated, 1)
                        v.tensor_tensor(u, u, gb, ALU.mult).then_inc(gated, 1)
                        v.wait_ge(gated, 2)
                        v.tensor_tensor(att, att, u, ALU.add).then_inc(added, 1)

        def residual_evac(eng, i, b, ps):
            c = at(i * 8 + b * 4, 4)
            return eng.tensor_tensor(xt[:, c, :], ps, xt[:, c, :], ALU.add)

        ff = area(A0, 64)

        def up_stage(name):
            s = S[name]
            with ExitStack() as e:
                rectified, squared = local(e, "rectified"), local(e, "squared")
                with nc.Block() as block:
                    @block.sync
                    def _(sp):
                        load_section(sp, s)

                    @block.tensor
                    def _(pe):
                        multiply_section(pe, s, lambda c: h[:, c, :])

                    @block.scalar
                    def _(act):
                        with act.Fori(0, s.iters) as i:
                            for b in range(2):
                                block_done(act, s, i, b)
                                act.activation(ff[:, at(i * 8 + b * 4, 4), :], gp[:, b], ACT.Relu).then_inc(pair_evacuated[b], 1)

                    @block.vector
                    def _(v):
                        with v.Fori(0, s.iters) as i:
                            for b in range(2):
                                v.wait_ge(pair_evacuated[b], i + (blocks_before[name] // 2 + 1))
                                f = ff[:, at(i * 8 + b * 4, 4), :]
                                v.tensor_tensor(f, f, f, ALU.mult).then_inc(squared, 1)

        def down_stage(name):
            s = S[name]
            b0 = blocks_before[name]
            with nc.Block() as block:
                @block.sync
                def _(sp):
                    load_section(sp, s)

                @block.tensor
                def _(pe):
                    with pe.Fori(0, 2) as i:
                        for b in range(2):
                            pe.wait_ge(pair_evacuated[b], i + b0 // 2)
                            for u in range(8):
                                multiply_unit(pe, u % 4, i * 64 + 16 * (s.unit0 // SLOTS + 1 + 2 * b + u // 4), b,
                                              lambda c: ff[:, u * KG + c, :], u == 0, u == 7)

                @block.vector
                def _(v):
                    with v.Fori(0, 2) as i:
                        for b in range(2):
                            v.wait_ge(unit_used, i * 16 + (s.unit0 + 8 * b + 8))
                            residual_evac(v, i, b, gp[:, b]).then_inc(pair_evacuated[b], 1)
        in3 = area(A0, 32)
        WINDOWS = (2, 4, 8, 16)
        negd = consts[:, 0:256]
        count = consts[:, 256:512]
        slopes = consts[:, 512:520]
        dist = consts[:, 520:776]

        def tables3_stage():
            disti = variance_t[:, :].bitcast(I32)
            with ExitStack() as e:
                made, done = local(e, "distances"), local(e, "tables")
                with nc.Block() as block:
                    @block.gpsimd
                    def _(pool):
                        pool.iota(disti, [[1, TOK]], base=-127, channel_multiplier=1).then_inc(made, 1)
                        for n in range(8):
                            pool.wait_ge(made, n + 1)
                            pool.memset(slopes[:, n:n + 1], 2.0 ** (-8.0 * (n + 1) / 8)).then_inc(made, 1)
                        pool.wait_ge(done, 10)
                        pool.affine_select(out=negd, in_=negd, compare_op=ALU.is_ge, fill=-1.0e33, base=-127,
                                           pattern=[[1, TOK]], channel_multiplier=1).then_inc(made, 1)

                    @block.vector
                    def _(v):
                        n = 0
                        def did(ins):
                            nonlocal n
                            n += 1
                            ins.then_inc(done, 1)
                            v.wait_ge(done, n)
                        m = variance[:, :].bitcast(I32)
                        f = rstd[:, :]
                        v.wait_ge(made, 9)
                        did(v.tensor_copy(dist, disti))
                        did(v.tensor_scalar(count, dist, 128.5, None, ALU.is_lt))
                        for mask in (3, 15):
                            did(v.tensor_scalar(m, disti, mask, None, ALU.bitwise_and))
                            did(v.tensor_scalar(f, m, 0, None, ALU.is_equal))
                            did(v.tensor_tensor(count, count, f, ALU.add))
                        did(v.tensor_scalar(f, count, 0.5, -1.0e33, ALU.is_lt, ALU.mult))
                        did(v.tensor_tensor(negd, f, dist, ALU.subtract))

        def pool_stage():
            u, d = in3, area(16400, BC)
            w = arena[:, 18448:20496].rearrange("p (g k n) -> p g k n", g=4, k=2)
            yp = area(20496, BC)
            part = area(22544, 4)
            inv = area(23568, 4)
            with ExitStack() as e:
                loaded, made, summed, diffed, mixed, scaled = (
                    local(e, x) for x in ("pool_loaded", "counts_made", "window_sums", "diffed", "mixed", "scaled"))
                with nc.Block() as block:
                    @block.sync
                    def _(sp):
                        for g in range(4):
                            sp.dma_start(w[:, g], I["pool_w_3"][0, g].rearrange("(k p) n -> p k n", p=P)).then_inc(loaded, 16)
                        sp.wait_ge(loaded, 64)

                    @block.gpsimd
                    def _(pool):
                        n = 0
                        for g, win in enumerate(WINDOWS):
                            pool.memset(inv[:, g, win - 1:], 1.0 / win).then_inc(made, 1)
                            n += 1
                            pool.wait_ge(made, n)
                            for t in range(win - 1):
                                pool.memset(inv[:, g, t:t + 1], 1.0 / (t + 1)).then_inc(made, 1)
                                n += 1
                                pool.wait_ge(made, n)

                    @block.vector
                    def _(v):
                        n = 0
                        def did(ins):
                            nonlocal n
                            n += 1
                            ins.then_inc(summed, 1)
                            v.wait_ge(summed, n)
                        v.wait_ge(made, sum(WINDOWS))
                        for g, win in enumerate(WINDOWS):
                            src = u[:, 2 * g:2 * g + 2, :]
                            w0, k = src, 1
                            while k < win:
                                dst = part[:, 0:2, :] if k in (1, 4) else part[:, 2:4, :]
                                did(v.tensor_copy(dst[:, :, 0:k], w0[:, :, 0:k]))
                                did(v.tensor_tensor(dst[:, :, k:], w0[:, :, k:], w0[:, :, 0:TOK - k], ALU.add))
                                w0, k = dst, 2 * k
                            did(v.tensor_tensor(w0, w0, inv[:, g:g + 1, :].to_broadcast([P, 2, TOK]), ALU.mult))
                            ins = v.tensor_tensor(d[:, 2 * g:2 * g + 2, :], w0, src, ALU.subtract)
                            ins.then_inc(diffed, 1)
                            v.wait_ge(diffed, g + 1)

                    @block.tensor
                    def _(pe):
                        pe.wait_ge(loaded, 64)
                        for g in range(4):
                            pe.wait_ge(diffed, g + 1)
                            for j in range(2):
                                for k in range(2):
                                    m = pe.matmul(sp_[:, g, j * TOK:(j + 1) * TOK], w[:, g, k, j * P:(j + 1) * P], d[:, 2 * g + k, :],
                                                  start=(k == 0), stop=(k == 1), skip_group_check=True)
                            m.then_inc(mixed, 1)

                    @block.scalar
                    def _(act):
                        for g in range(4):
                            act.wait_ge(mixed, g + 1)
                            for j in range(2):
                                act.activation(yp[:, 2 * g + j, :], sp_[:, g, j * TOK:(j + 1) * TOK], ACT.Copy,
                                               scale=par("pscale", 2 * g + j)).then_inc(scaled, 1)

        def attention3_stage():
            def logits(v, dv, g, r, head, ps, sc):
                v.scalar_tensor_tensor(sc[:, 0:128], negd[:, 0:128], slopes[:, at(head, 1)], ps[:, 0:128], ALU.mult, ALU.add)
                dv.did(v.scalar_tensor_tensor(sc[:, 128:384], negd, slopes[:, at(head, 1)], ps[:, 128:384], ALU.mult, ALU.add), f"log{r}_0")
            def weigh(v, g, sc, small):
                v.scalar_tensor_tensor(sc[:, 0:128], sc[:, 0:128], 1.0, count[:, 0:128], ALU.mult, ALU.mult, accum_out=small[:, 4:5])
                v.scalar_tensor_tensor(sc[:, 128:384], sc[:, 128:384], 1.0, count, ALU.mult, ALU.mult, accum_out=small[:, 5:6]).then_inc(weighed, 1)
                v.wait_ge(weighed, g + 1)
            weighed = sem("weighed")
            attention_stage(in3[:, 8:16, :], lambda g: in3[:, at(g + 16, 1), :], lambda g: in3[:, at(g + 24, 1), :],
                            8, 1, 128 ** -0.5, logits, weigh, 1, 26640)

        def store_stage():
            rowsb = arena[:, A0:A0 + 4096].rearrange("p (t c) -> p t c", t=2)
            with ExitStack() as e:
                turned, copied, stored = local(e, "turned"), local(e, "copied"), local(e, "stored")
                with nc.Block() as block:
                    @block.tensor
                    def _(pe):
                        for g in range(8):
                            if g >= 4:
                                pe.wait_ge(copied, g - 3)
                            for n in range(4):
                                m = pe.transpose(sp_[:, g % 4, n * P:(n + 1) * P],
                                                 xt[:, (g % 4) * 4 + n, (g // 4) * P:(g // 4 + 1) * P], ident[:, :])
                            m.then_inc(turned, 1)

                    @block.vector
                    def _(v):
                        for g in range(8):
                            v.wait_ge(turned, g + 1)
                            v.tensor_copy(rowsb[:, g // 4, (g % 4) * 512:(g % 4 + 1) * 512], sp_[:, g % 4, :]).then_inc(copied, 1)

                    @block.sync
                    def _(sp):
                        for t in range(2):
                            sp.wait_ge(copied, 4 * t + 4)
                            sp.dma_start(out_dram[0, t * P:(t + 1) * P, :], rowsb[:, t, :]).then_inc(stored, 16)
                        sp.wait_ge(stored, 32)
        stages = []
        def copy_pad(dst):
            def evac(eng, i, b, ps):
                return eng.activation(dst[:, at(i * 8 + b * 4, 4), 1:TOK + 1], ps, ACT.Copy)
            return evac
        def pad_stage():
            with nc.Block() as block:
                @block.gpsimd
                def _(pool):
                    pool.memset(area(A0, 24, TOK + 1)[:, :, 0:1], 0.0)
        hx = lambda c: hp[:, c, 1:TOK + 1]
        stages += [("start", start_stage), ("masks", masks_stage),
                   ("norm", lambda: norm_stage(xt, DC, "pre", hp[:, :, 1:TOK + 1])),
                   ("lora", lora_stage), ("pad", pad_stage),
                   ("rkv", lambda: gemm_stage("rkv", hx, copy_pad(area(A0, 24, TOK + 1)))),
                   ("mix", mix_stage)]
        def evac_silu(dst):
            def evac(eng, i, b, ps):
                return eng.activation(dst[:, at(i * 8 + b * 4, 4), :], ps, ACT.Silu)
            return evac
        stages += [("zr", lambda: gemm_stage("zr", hx, evac_silu(area(A0, 8)))),
                   ("qkv", lambda: gemm_stage("qkv", hx, copy_to(area(A0 + 2048, 24)))),
                   ("za", lambda: gemm_stage("za", hx, evac_silu(area(A0 + 8192, 8)))),
                   ("att1", attention1_stage), ("rwkv", rwkv_stage),
                   ("gates", lambda: gemm_stage("gates", hx, gates_evac)),
                   ("branch", branch_stage),
                   ("out", lambda: gemm_stage("out", lambda c: area(12304, DC)[:, c, :], copy_to(area(4096, DC)))),
                   ("post", lambda: norm_stage(area(4096, DC), DC, "post", area(4096, DC), add_to=xt))]
        hh_ = lambda c: h[:, c, :]
        def evac_as(dst, func):
            def evac(eng, i, b, ps):
                return eng.activation(dst[:, at(i * 8 + b * 4, 4), :], ps, func)
            return evac
        stages += [("norm1", lambda: norm_stage(xt, DC, "norm1", h)),
                   ("qkv2", lambda: gemm_stage("qkv2", hh_, copy_to(area(A0, 24)))),
                   ("index2", index_stage), ("bias2", bias2_stage), ("select", select_stage),
                   ("att2", attention2_stage),
                   ("uv2", lambda: gemm_stage("uv2", hh_, evac_as(area(15888, 32), ACT.Gelu_apprx_tanh))),
                   ("sgu", sgu_stage),
                   ("gates2", lambda: gemm_stage("gates2", hh_, evac_as(area(24080, 32), ACT.Sigmoid))),
                   ("merge2", merge2_stage),
                   ("out2", lambda: gemm_stage("out2", lambda c: area(A0, DC)[:, c, :], residual_evac, "vector")),
                   ("norm2", lambda: norm_stage(xt, DC, "norm2", h)),
                   ("up2", lambda: up_stage("up2")), ("down2", lambda: down_stage("down2")),
                   ("final2", lambda: norm_stage(xt, DC, "final2", xt))]
        stages += [("mix3", lambda: norm_stage(xt, DC, "mix3", h)),
                   ("in3", lambda: gemm_stage("in3", hh_, copy_to(in3))),
                   ("tables3", tables3_stage), ("pool", pool_stage), ("att3", attention3_stage),
                   ("pout", lambda: norm_stage(area(20496, BC), BC, "pout", area(4096, BC), scratch=26640)),
                   ("aout", lambda: norm_stage(in3[:, 8:16, :], BC, "aout", area(6144, BC), scratch=26640)),
                   ("out3", lambda: gemm_stage("out3", hh_, residual_evac, "vector")),
                   ("mlp3", lambda: norm_stage(xt, DC, "mlp3", h)),
                   ("up3", lambda: up_stage("up3")), ("down3", lambda: down_stage("down3")),
                   ("final3", lambda: norm_stage(xt, DC, "final3", xt)), ("end", store_stage)]
        seen = 0
        for name, f in stages:
            f()
            if name in S:
                seen = order.index(S[name]) + 1
            if name == upto and seen < len(order):
                with nc.Block() as block:
                    @block.sync
                    def _(sp):
                        for k in range(SLOTS):
                            sp.wait_ge(unit_loaded[k], 16 * (order[seen].unit0 // 4 + 1))
                break


def kernel(**inputs):
    import concourse.bacc as bacc
    from concourse.bass_utils import run_bass_kernel_spmd

    nc = bacc.Bacc("TRN2", target_bir_lowering=False, num_devices=1)
    arrays, aps = {}, {}
    for name, a in inputs.items():
        arrays[name] = np.ascontiguousarray(a)
        aps[name] = nc.dram_tensor(name, arrays[name].shape, mybir.dt.from_np(arrays[name].dtype), kind="ExternalInput").ap()
    out = nc.dram_tensor("out", (1, TOK, D), F32, kind="ExternalOutput").ap()
    build_kernel(nc, aps, out)
    return run_bass_kernel_spmd(nc, [arrays], core_ids=[0]).results[0]["out"]
```

```python
from contextlib import ExitStack
import math
import numpy as np
import concourse.bass as bass
from concourse import mybir

F32 = mybir.dt.float32
I32 = mybir.dt.int32
F32R = mybir.dt.float32r
ALU = mybir.AluOpType
ACT = mybir.ActivationFunctionType
AX = mybir.AxisListType.X

P = 128
TOK = 256
D = 2048
DB = 1024
DC = D // P
BC = DB // P
KG = 4
UC = 512
SLOTS = 4
NEG = -1.0e30
EPS = 1e-6
DECAY = 0.606531
CH = 64
NCH = TOK // CH
CENTRE = DECAY * CH / 2


class Section:
    def __init__(self, name, iters, blocks, units, source):
        self.name, self.iters, self.blocks, self.units, self.source = name, iters, blocks, units, source
        self.per_iter = blocks * units
        self.unit0 = self.block0 = 0


def build_kernel(nc, I, out_dram, upto=None):
    ctx = ExitStack()
    with ctx:
        def sb(name, shape, dt=F32):
            return ctx.enter_context(nc.sbuf_tensor(name, shape, dt))

        def sem(name):
            return ctx.enter_context(nc.semaphore(name))

        ring = sb("ring", [P, SLOTS, KG, UC])
        w_parts = sb("w_parts", [P, 2, 2, KG // 2, UC], F32R)
        x_parts = sb("x_parts", [P, 2, DC, TOK], F32R)
        xt = sb("xt", [P, DC, TOK])
        h_all = sb("h_all", [P, DC * (TOK + 1)])
        ident = sb("ident", [P, P])
        ones = sb("ones", [P, P])
        headones = sb("headones", [P, P])
        prm = sb("prm", [P, 368])
        rstd = sb("rstd", [P, TOK])
        variance = sb("variance", [P, TOK])
        variance_t = sb("variance_t", [P, TOK])
        p_turned = sb("p_turned", [P, 384])
        smalls = sb("smalls", [P, 32])

        gp = ctx.enter_context(nc.psum_tensor("gp", [P, 2, 4, TOK], F32))
        sp_ = ctx.enter_context(nc.psum_tensor("sidep", [P, 4, 512], F32))

        unit_loaded = [sem(f"unit_loaded_{k}") for k in range(SLOTS)]
        high_split = sem("high_split")
        low_split = sem("low_split")
        half_used = sem("half_used")
        pair_evacuated = [sem(f"pair_evacuated_{b}") for b in range(2)]
        idx_extra_loaded = sem("idx_extra_loaded")
        x_high_split = sem("x_high_split")
        ff_squared, ff_high_split = sem("ff_squared"), sem("ff_high_split")

        phase, phases = [None], [0]

        def new_phase(*tensors):
            if phase[0] is not None:
                phase[0].close()
            phase[0] = ctx.enter_context(ExitStack())
            phases[0] += 1
            return [phase[0].enter_context(nc.sbuf_tensor(f"{name}_{phases[0]}", shape, dt))
                    for name, shape, dt in tensors]

        A0 = 4096 + 4112
        ARENA = 21560
        arena_box = [None]

        class Space:
            def __getitem__(self, key):
                rows_, cols_ = key
                a, b = cols_.start, cols_.stop
                if b <= 4096:
                    return xt[:, :, :].rearrange("p c t -> p (c t)")[rows_, a:b]
                if b <= A0:
                    return h_all[rows_, a - 4096:b - 4096]
                assert a >= A0 and b <= A0 + ARENA, (a, b)
                return arena_box[0][rows_, a - A0:b - A0]

        arena = Space()

        def area(start, chunks, width=TOK):
            return arena[:, start:start + chunks * width].rearrange("p (c t) -> p c t", t=width)

        hp = h_all[:, :].rearrange("p (c t) -> p c t", t=TOK + 1)
        h = h_all[:, 0:DC * TOK].rearrange("p (c t) -> p c t", t=TOK)

        def cols(w, rows, c):
            return w[rows * KG * P:(rows + 1) * KG * P, c].rearrange("(c p) n -> p c n", p=P)

        w1, w2_, w3 = I["w_in"][0], I["w_in_2"][0], I["w_in_3"][0]

        def at(expr, n):
            if isinstance(expr, int):
                return slice(expr, expr + n)
            return bass.ds(expr, n)

        def two_blocks(w, base):
            return lambda u, i: [(cols(w, u % 4, at(i * 1024 + (base + 512 * (u // 4)), UC)), 0, UC)]

        def branches(u, i):
            b = u // 2
            w = (I["w_branch_rwkv"], I["w_branch_attn"])[b % 2][0]
            return [(cols(w, u % 2, at(i * 1024 + 512 * (b // 2), UC)), 0, UC)]

        def index_cols(u, i):
            r = u % 4
            if u < 4:
                return [(cols(w2_, r, slice(3072, 3584)), 0, UC)]
            return [(cols(w2_, r, slice(3584, 3648)), 0, 64), (cols(w2_, r, slice(3584, 3648)), 64, 64),
                    (cols(w2_, r, slice(3648, 3656)), 128, 8)]

        def up_half(w, n):
            return two_blocks(w, 4096 * n)

        def down_half(w, n):
            return lambda u, i: [(cols(w, 8 * n + u % 8, at(i * 1024 + 512 * (u // 8), UC)), 0, UC)]

        S, order = {}, []

        def section(name, iters, source, blocks=2, units=4):
            s = Section(name, iters, blocks, units, source)
            if order:
                s.unit0 = order[-1].unit0 + order[-1].iters * order[-1].per_iter
                s.block0 = order[-1].block0 + order[-1].iters * order[-1].blocks
            S[name] = s
            order.append(s)

        section("rkv", 3, two_blocks(w1, 0))
        section("zr", 1, two_blocks(w1, 3072))
        section("qkv", 3, two_blocks(w1, 4096))
        section("za", 1, two_blocks(w1, 7168))
        section("gates", 4, two_blocks(w1, 8192))
        section("branch", 2, branches, 4, 2)
        section("out", 2, two_blocks(I["w_out"][0], 0))
        section("qkv2", 3, two_blocks(w2_, 0))
        section("index2", 1, index_cols)
        section("uv2", 4, two_blocks(w2_, 3656))
        section("gates2", 4, two_blocks(w2_, 7752))
        section("out2", 2, two_blocks(I["w_out_2"][0], 0))
        for n in range(2):
            section(f"up2_{n}", 4, up_half(I["w_ff1_2"][0], n))
            section(f"down2_{n}", 2, down_half(I["w_ff2_2"][0], n), 2, 8)
        section("in3", 4, two_blocks(w3, 0))
        section("out3", 2, two_blocks(I["w_out_3"][0], 0))
        for n in range(2):
            section(f"up3_{n}", 4, up_half(I["w_up_3"][0], n))
            section(f"down3_{n}", 2, down_half(I["w_down_3"][0], n), 2, 8)

        def load_unit(sp, s, u, i):
            k = u % SLOTS
            if not (s is order[0] and isinstance(i, int) and i == 0 and u < SLOTS):
                sp.wait_ge(low_split, i * (2 * s.per_iter) + 2 * (s.unit0 + u - SLOTS + 1))
            pieces = s.source(u, i)
            for n, (src, c0, width) in enumerate(pieces):
                last = n == len(pieces) - 1
                sp.dma_start(ring[:, k, :, c0:c0 + width], src).then_inc(
                    unit_loaded[k] if last else idx_extra_loaded, 16)

        def load_section(sp, s):
            if s.iters > 1:
                with sp.Fori(0, s.iters - 1) as i:
                    for u in range(SLOTS, s.per_iter):
                        load_unit(sp, s, u, i)
                    for u in range(SLOTS):
                        load_unit(sp, s, u, i + 1)
            for u in range(SLOTS, s.per_iter):
                load_unit(sp, s, u, s.iters - 1)
            n = order.index(s) + 1
            if n < len(order):
                for u in range(SLOTS):
                    load_unit(sp, order[n], u, 0)

        def halves_before(s, i, q):
            return i * (2 * s.per_iter) + (2 * s.unit0 + q)

        def split_high(act, s, i, q):
            u = q // 2
            act.wait_ge(unit_loaded[u % SLOTS], i * (4 * s.per_iter) + 16 * ((s.unit0 + u) // SLOTS + 1))
            if s.name == "index2" and q == 8:
                act.wait_ge(idx_extra_loaded, 128)
            if not (s is order[0] and isinstance(i, int) and q < 2):
                act.wait_ge(half_used, halves_before(s, i, q - 1))
            act.activation(w_parts[:, q % 2, 0], ring[:, u % SLOTS, (q % 2) * 2:(q % 2) * 2 + 2, :], ACT.Copy).then_inc(high_split, 1)

        def split_low(v, s, i, q):
            u = q // 2
            v.wait_ge(high_split, halves_before(s, i, q + 1))
            v.tensor_tensor(w_parts[:, q % 2, 1], ring[:, u % SLOTS, (q % 2) * 2:(q % 2) * 2 + 2, :],
                            w_parts[:, q % 2, 0].bitcast(F32), ALU.subtract).then_inc(low_split, 1)

        def split_section(eng, s, split, evac):
            halves = 2 * s.units
            def body(i, last):
                for b in range(s.blocks):
                    for q in range(b * halves + 2, (b + 1) * halves + 2):
                        if q < s.blocks * halves:
                            split(eng, s, i, q)
                        elif not last:
                            split(eng, s, i + 1, q - s.blocks * halves)
                    if evac is not None:
                        evac(eng, i, b)
            for q in range(2):
                split(eng, s, 0, q)
            if s.iters > 1:
                with eng.Fori(0, s.iters - 1) as i:
                    body(i, False)
            body(s.iters - 1, True)

        def multiply_section(pe, s, x_high, x_low, tiles=None):
            halves = 2 * s.units
            def body(i):
                for b in range(s.blocks):
                    pe.wait_ge(pair_evacuated[b % 2], i * (s.blocks // 2) + (s.block0 // 2 + b // 2 + 1))
                    for n in range(halves):
                        q = b * halves + n
                        nt = tiles[b] if tiles else 4
                        pe.wait_ge(high_split, halves_before(s, i, q + 1))
                        for c in range(2):
                            for j in range(nt):
                                wh = w_parts[:, q % 2, 0, c, j * P:(j + 1) * P]
                                pe.matmul(gp[:, b % 2, j, :], wh, x_high(b, 2 * n + c),
                                          start=(n == 0 and c == 0 and j % 2 == 0), stop=False, skip_group_check=True)
                                pe.matmul(gp[:, b % 2, j, :], wh, x_low(b, 2 * n + c), start=False, stop=False,
                                          skip_group_check=True)
                        pe.wait_ge(low_split, halves_before(s, i, q + 1))
                        for c in range(2):
                            for j in range(nt):
                                m = pe.matmul(gp[:, b % 2, j, :], w_parts[:, q % 2, 1, c, j * P:(j + 1) * P],
                                              x_high(b, 2 * n + c), start=False,
                                              stop=(n == halves - 1 and c == 1), skip_group_check=True)
                        m.then_inc(half_used, 1)
            if s.iters == 1:
                body(0)
            else:
                with pe.Fori(0, s.iters) as i:
                    body(i)

        def block_done(eng, s, i, b):
            eng.wait_ge(half_used, halves_before(s, i, (b + 1) * 2 * s.units))

        x_hi = lambda b, c: x_parts[:, 0, c, :]
        x_lo = lambda b, c: x_parts[:, 1, c, :]

        class Steps:
            def __init__(self, ectx, name, steps):
                self.s, self.steps, self.at = local(ectx, name), steps, 0

            def did(self, ins, step):
                assert self.steps[self.at % len(self.steps)] == step, (step, self.steps[self.at % len(self.steps)])
                self.at += 1
                ins.then_inc(self.s, 1)

            def value(self, step, i=0):
                return i * len(self.steps) + (self.steps.index(step) + 1)

            def wait(self, eng, step, i=0):
                eng.wait_ge(self.s, self.value(step, i))

        names = [0]

        def local(ectx, name):
            names[0] += 1
            return ectx.enter_context(nc.semaphore(f"{name}_{names[0]}"))

        rows = {}
        row_list = []
        r = 0
        def add_rows(name, key, ap, n):
            nonlocal r
            if r // P != (r + n - 1) // P:
                r = (r // P + 1) * P
            rows[name] = r
            row_list.append((r, n, ap))
            r += n
        flat = lambda key: I[key]
        add_rows("pre", None, I["pre_norm_g"][0].rearrange("(c p) -> c p", p=P), 16)
        add_rows("post", None, I["post_norm_g"][0].rearrange("(c p) -> c p", p=P), 16)
        add_rows("mu_rkv", None, I["mu_rkv"][0].rearrange("m (c p) -> (m c) p", p=P), 24)
        add_rows("mu_wa", None, I["mu_wa"][0].rearrange("m (c p) -> (m c) p", p=P), 32)
        add_rows("a0", None, I["a0"][0].rearrange("(c p) -> c p", p=P), 8)
        add_rows("k_k", None, I["k_k"][0].rearrange("(c p) -> c p", p=P), 8)
        add_rows("k_a", None, I["k_a"][0].rearrange("(c p) -> c p", p=P), 8)
        add_rows("r_k", None, I["r_k"][0].rearrange("(c h) n -> c (h n)", h=2), 8)
        add_rows("ln_g", None, I["ln_x_g"][0].rearrange("(c p) -> c p", p=P), 8)
        add_rows("ln_b", None, I["ln_x_b"][0].rearrange("(c p) -> c p", p=P), 8)
        add_rows("b_merge", None, I["b_merge"][0].rearrange("m (c p) -> (m c) p", p=P), 32)
        add_rows("norm1", None, I["norm1_g_2"][0].rearrange("(c p) -> c p", p=P), 16)
        add_rows("sgu_g", None, I["sgu_ln_g_2"][0].rearrange("(c p) -> c p", p=P), 16)
        add_rows("sgu_b", None, I["sgu_ln_b_2"][0].rearrange("(c p) -> c p", p=P), 16)
        add_rows("norm2", None, I["norm2_g_2"][0].rearrange("(c p) -> c p", p=P), 16)
        add_rows("final2", None, I["final_g_2"].rearrange("(c p) -> c p", p=P), 16)
        add_rows("mix3", None, I["norm_mix_g_3"][0].rearrange("(c p) -> c p", p=P), 16)
        add_rows("pscale", None, I["pool_scale_3"][0].rearrange("(c p) -> c p", p=P), 8)
        add_rows("pout", None, I["pool_out_norm_g_3"][0].rearrange("(c p) -> c p", p=P), 8)
        add_rows("aout", None, I["attn_out_norm_g_3"][0].rearrange("(c p) -> c p", p=P), 8)
        add_rows("mlp3", None, I["norm_mlp_g_3"][0].rearrange("(c p) -> c p", p=P), 16)
        add_rows("final3", None, I["norm_final_g_3"].rearrange("(c p) -> c p", p=P), 16)
        assert r <= 368, r

        def par(name, c=0, n=1):
            return prm[:, rows[name] + c:rows[name] + c + n]

        def start_stage():
            xrow = arena[:, A0:A0 + 4096].rearrange("p (t c) -> p t c", t=2)
            prow = arena[:, A0 + 4096:A0 + 4096 + 384].rearrange("p (t c) -> p t c", t=3)
            with ExitStack() as e:
                x_loaded, p_loaded, filled, made, turned, copied = (
                    local(e, x) for x in ("x_loaded", "params_loaded", "filled", "consts_made", "turned", "copied"))
                with nc.Block() as block:
                    @block.sync
                    def _(sp):
                        for t in range(2):
                            sp.dma_start(xrow[:, t, :], I["x"][0, t * P:(t + 1) * P, :]).then_inc(x_loaded, 16)
                        sp.wait_ge(filled, 1)
                        for (r0, nr, ap) in row_list:
                            sp.dma_start(prow[r0 % P:r0 % P + nr, r0 // P, :], ap).then_inc(p_loaded, 16)
                        for u in range(SLOTS):
                            load_unit(sp, order[0], u, 0)

                    @block.gpsimd
                    def _(pool):
                        pool.memset(prow, 0.0).then_inc(filled, 1)
                        pool.memset(ident[:, :], 0.0).then_inc(filled, 1)
                        pool.memset(ones[:, :], 1.0).then_inc(filled, 1)
                        pool.memset(headones[:, :], 0.0).then_inc(filled, 1)
                        pool.wait_ge(filled, 4)
                        pool.affine_select(out=ident[:, :], in_=ident[:, :], compare_op=ALU.not_equal, fill=1.0,
                                           base=0, pattern=[[-1, P]], channel_multiplier=1).then_inc(made, 1)
                        for q in range(2):
                            pool.wait_ge(made, q + 1)
                            pool.memset(headones[64 * q:64 * q + 64, 64 * q:64 * q + 64], 1.0).then_inc(made, 1)
                        pool.wait_ge(made, 3)
                        pool.memset(hp[:, :, 0:1], 0.0).then_inc(made, 1)

                    @block.tensor
                    def _(pe):
                        pe.wait_ge(made, 4)
                        pe.wait_ge(x_loaded, 32)
                        for g in range(8):
                            if g >= 4:
                                pe.wait_ge(copied, g - 3)
                            for c in range(2):
                                for t in range(2):
                                    m = pe.transpose(sp_[:, g % 4, c * TOK + t * P:c * TOK + t * P + P],
                                                     xrow[:, t, (2 * g + c) * P:(2 * g + c + 1) * P], ident[:, :])
                            m.then_inc(turned, 1)
                        pe.wait_ge(p_loaded, 16 * len(row_list))
                        pe.wait_ge(copied, 5)
                        for t in range(3):
                            m = pe.transpose(sp_[:, 0, t * P:(t + 1) * P], prow[:, t, :], ident[:, :])
                        m.then_inc(turned, 1)

                    @block.vector
                    def _(v):
                        v.memset(smalls[:, 0:1], 0.0).then_inc(pair_evacuated[0], 1)
                        v.memset(smalls[:, 1:2], 0.0).then_inc(pair_evacuated[1], 1)
                        for g in range(8):
                            v.wait_ge(turned, g + 1)
                            v.tensor_copy(xt[:, 2 * g:2 * g + 2, :],
                                          sp_[:, g % 4, :].rearrange("p (c t) -> p c t", c=2)).then_inc(copied, 1)
                        v.wait_ge(turned, 9)
                        v.tensor_copy(prm[:, :], sp_[:, 0, 0:368]).then_inc(copied, 1)

        def inv_root(v, sums, count, summed, meaned, rooted, inverted):
            x, t = variance[:, :], variance_t[:, :]
            v.wait_ge(summed, 1)
            v.tensor_scalar(x, sums, 1.0 / count, EPS, ALU.mult, ALU.add).then_inc(meaned, 1)
            v.wait_ge(rooted, 1)
            v.reciprocal(rstd[:, :], rstd[:, :]).then_inc(inverted, 1)
            v.wait_ge(inverted, 1)
            v.tensor_tensor(t, rstd[:, :], rstd[:, :], ALU.mult).then_inc(inverted, 1)
            v.wait_ge(inverted, 2)
            v.tensor_tensor(t, t, x, ALU.mult).then_inc(inverted, 1)
            v.wait_ge(inverted, 3)
            v.tensor_scalar(t, t, -0.5, 1.5, ALU.mult, ALU.add).then_inc(inverted, 1)
            v.wait_ge(inverted, 4)
            v.tensor_tensor(rstd[:, :], rstd[:, :], t, ALU.mult).then_inc(inverted, 1)
            v.wait_ge(inverted, 5)

        def norm_stage(src, nchunks, gain, dst, add_to=None, scratch=A0):
            sq = area(scratch, nchunks)
            with ExitStack() as e:
                squared, summed, meaned, rooted, inverted, scaled = (
                    local(e, x) for x in ("squared", "summed", "meaned", "rooted", "inverted", "scaled"))
                with nc.Block() as block:
                    @block.scalar
                    def _(act):
                        for q in range(4):
                            n = nchunks // 4
                            act.activation(sq[:, q * n:(q + 1) * n, :], src[:, q * n:(q + 1) * n, :],
                                           ACT.Square).then_inc(squared, 1)
                        act.wait_ge(meaned, 1)
                        act.activation(rstd[:, :], variance[:, :], ACT.Sqrt).then_inc(rooted, 1)

                    @block.tensor
                    def _(pe):
                        for c in range(nchunks):
                            if c % (nchunks // 4) == 0:
                                pe.wait_ge(squared, c // (nchunks // 4) + 1)
                            m = pe.matmul(sp_[:, 0, 0:TOK], ones[:, :], sq[:, c, :], start=(c == 0),
                                          stop=(c == nchunks - 1))
                        m.then_inc(summed, 1)

                    @block.vector
                    def _(v):
                        inv_root(v, sp_[:, 0, 0:TOK], nchunks * P, summed, meaned, rooted, inverted)
                        if add_to is None:
                            with v.Fori(0, nchunks) as c:
                                v.scalar_tensor_tensor(dst[:, at(c, 1), :], src[:, at(c, 1), :],
                                                       prm[:, at(c + rows[gain], 1)], rstd[:, :],
                                                       ALU.mult, ALU.mult).then_inc(scaled, 1)
                        else:
                            with v.Fori(0, nchunks) as c:
                                v.scalar_tensor_tensor(src[:, at(c, 1), :], src[:, at(c, 1), :],
                                                       prm[:, at(c + rows[gain], 1)], rstd[:, :],
                                                       ALU.mult, ALU.mult).then_inc(scaled, 1)
                            v.wait_ge(scaled, nchunks)
                            v.tensor_tensor(add_to, add_to, src, ALU.add).then_inc(scaled, 1)

        groups_split = [0]

        def split_stage(*sources):
            groups = [(src[:, q:q + 4, :], slice(c0 + q, c0 + q + 4))
                      for src, c0 in sources for q in range(0, src.shape[1], 4)]
            before = groups_split[0]
            groups_split[0] += len(groups)
            with nc.Block() as block:
                @block.scalar
                def _(act):
                    for src, c in groups:
                        act.activation(x_parts[:, 0, c, :], src, ACT.Copy).then_inc(x_high_split, 1)

                @block.vector
                def _(v):
                    for n, (src, c) in enumerate(groups):
                        v.wait_ge(x_high_split, before + n + 1)
                        v.tensor_tensor(x_parts[:, 1, c, :], src, x_parts[:, 0, c, :].bitcast(F32), ALU.subtract)

        def gemm_stage(name, evac, engine="scalar", x=(x_hi, x_lo), tiles=None):
            s = S[name]
            def out(eng, i, b):
                block_done(eng, s, i, b)
                evac(eng, i, b, gp[:, b % 2, :, :]).then_inc(pair_evacuated[b % 2], 1)
            with nc.Block() as block:
                @block.sync
                def _(sp):
                    load_section(sp, s)

                @block.tensor
                def _(pe):
                    multiply_section(pe, s, *x, tiles)

                @block.scalar
                def _(act):
                    split_section(act, s, split_high, out if engine == "scalar" else None)

                @block.vector
                def _(v):
                    split_section(v, s, split_low, out if engine == "vector" else None)

        def copy_to(dst, width=None):
            def evac(eng, i, b, ps):
                return eng.activation(dst[:, at(i * 8 + b * 4, 4), :], ps, ACT.Copy)
            return evac

        consts = sb("consts", [P, 1024])
        mask_su = consts[:, 0:128]
        level = consts[:, 128:512].rearrange("p (l t) -> p l t", l=6)
        tri = consts[:, 512:768]
        eye2 = consts[:, 768:832]
        centre = consts[:, 832:834]
        omka = consts[:, 834:842]
        tri128 = consts[:, 896:1024]

        def lora_stage():
            xw, xa, dh = area(A0, DC), area(A0 + 4096, DC), area(A0 + 8192, DC)
            lw = area(A0 + 12288, DC, 64)
            la = area(A0 + 13312, DC, 64)
            a2s = arena[:, A0 + 14336:A0 + 15360]
            a1t = arena[:, A0 + 15360:A0 + 15616]
            aT = area(24592, BC)
            w2p, t1 = arena[:, 28744:29768], arena[:, 28488:28744]
            with ExitStack() as e:
                w_loaded, ones_row, differed, xmixed, hidden, activated, projected = (
                    local(e, x) for x in ("lora_loaded", "ones_row", "differed", "xmixed", "hidden", "activated", "projected"))
                with nc.Block() as block:
                    @block.sync
                    def _(sp):
                        sp.dma_start(lw, I["w1"][0].rearrange("(c p) n -> p c n", p=P)).then_inc(w_loaded, 16)
                        sp.dma_start(la, I["a1"][0].rearrange("(c p) n -> p c n", p=P)).then_inc(w_loaded, 16)
                        sp.dma_start(w2p[0:64, :], I["w2"][0]).then_inc(w_loaded, 16)
                        sp.dma_start(w2p[64:65, :], I["w0"]).then_inc(w_loaded, 16)
                        sp.dma_start(a2s[0:64, :], I["a2"][0]).then_inc(w_loaded, 16)
                        sp.wait_ge(w_loaded, 80)

                    @block.gpsimd
                    def _(pool):
                        pool.memset(t1[64:65, :], 1.0).then_inc(ones_row, 1)
                        pool.wait_ge(ones_row, 1)
                        pool.memset(centre[:, 0:1], CENTRE).then_inc(ones_row, 1)
                        pool.wait_ge(ones_row, 2)
                        pool.memset(centre[:, 1:2], -CENTRE).then_inc(ones_row, 1)

                    @block.vector
                    def _(v):
                        v.tensor_tensor(dh, hp[:, :, 0:TOK], hp[:, :, 1:TOK + 1], ALU.subtract).then_inc(differed, 1)
                        v.tensor_scalar(omka, par("k_a", 0, 8), -1.0, 1.0, ALU.mult, ALU.add).then_inc(differed, 1)
                        v.wait_ge(differed, 1)
                        with v.Fori(0, DC) as c:
                            for m, dst in ((0, xw), (1, xa)):
                                v.scalar_tensor_tensor(dst[:, at(c, 1), :], dh[:, at(c, 1), :],
                                                       prm[:, at(c + (rows["mu_wa"] + 16 * m), 1)],
                                                       hp[:, at(c, 1), 1:TOK + 1], ALU.mult, ALU.add).then_inc(xmixed, 1)

                    @block.tensor
                    def _(pe):
                        pe.wait_ge(w_loaded, 80)
                        for c in range(DC):
                            pe.wait_ge(xmixed, 2 * c + 2)
                            for m, (w, x) in enumerate(((lw, xw), (la, xa))):
                                mm = pe.matmul(sp_[0:64, m, 0:TOK], w[:, c, :], x[:, c, :], start=(c == 0), stop=(c == DC - 1))
                        mm.then_inc(hidden, 1)
                        pe.wait_ge(activated, 2)
                        for g in range(4):
                            if g >= 2:
                                pe.wait_ge(activated, 2 + 2 * (g - 1))
                            for k in range(2):
                                mm = pe.matmul(sp_[:, 2 + g % 2, k * TOK:(k + 1) * TOK],
                                               a2s[0:64, (2 * g + k) * P:(2 * g + k + 1) * P], a1t[0:64, :], start=True, stop=True)
                            mm.then_inc(projected, 1)

                    @block.scalar
                    def _(act):
                        act.wait_ge(hidden, 1)
                        act.activation(a1t[0:64, :], sp_[0:64, 1, 0:TOK], ACT.Copy).then_inc(activated, 1)
                        act.activation(t1[0:64, :], sp_[0:64, 0, 0:TOK], ACT.Tanh).then_inc(activated, 1)
                        for g in range(4):
                            act.wait_ge(projected, g + 1)
                            for k in range(2):
                                act.activation(aT[:, 2 * g + k, :], sp_[:, 2 + g % 2, k * TOK:(k + 1) * TOK], ACT.Sigmoid,
                                               bias=par("a0", 2 * g + k)).then_inc(activated, 1)

        def mix_stage():
            pp = area(A0, 24, TOK + 1)
            rkv = area(18448, 24)
            with ExitStack() as e:
                differed, mixed = local(e, "differed"), local(e, "mixed")
                with nc.Block() as block:
                    @block.vector
                    def _(v):
                        v.tensor_tensor(rkv, pp[:, :, 0:TOK], pp[:, :, 1:TOK + 1], ALU.subtract).then_inc(differed, 1)
                        v.wait_ge(differed, 1)
                        with v.Fori(0, 24) as c:
                            v.scalar_tensor_tensor(rkv[:, at(c, 1), :], rkv[:, at(c, 1), :],
                                                   prm[:, at(c + rows["mu_rkv"], 1)],
                                                   pp[:, at(c, 1), 1:TOK + 1], ALU.mult, ALU.add).then_inc(mixed, 1)

        def bias_table_ap(table, stride, offset):
            return bass.AP(table.tensor, offset, [[1, P], [stride, 16], [1, TOK]])

        masks_made = sem("masks_made")

        def masks_stage():
            with ExitStack() as e:
                filled, made = local(e, "filled"), local(e, "made")
                with nc.Block() as block:
                    @block.gpsimd
                    def _(pool):
                        pool.memset(consts[:, 0:832], 1.0).then_inc(filled, 1)
                        pool.memset(tri128, 1.0).then_inc(filled, 1)
                        pool.wait_ge(filled, 2)
                        n = 0
                        def keep(ap, base, pattern, mult, op=ALU.is_ge, fill=0.0):
                            nonlocal n
                            n += 1
                            pool.affine_select(out=ap, in_=ap, compare_op=op, fill=fill, base=base,
                                               pattern=pattern, channel_multiplier=mult).then_inc(made, 1)
                            pool.wait_ge(made, n)
                        keep(tri128, 0, [[1, P]], -1)
                        keep(tri[:, 0:128], 0, [[1, P]], -1)
                        keep(tri[:, 128:256], -1, [[1, P]], -1)
                        for q in range(2):
                            pool.memset(tri[0:64, 128 * q + 64:128 * q + 128], 0.0).then_inc(made, 1)
                            n += 1
                            pool.wait_ge(made, n)
                        for q in range(2):
                            half = slice(64 * q, 64 * q + 64)
                            keep(mask_su[half, 0:64], -1, [[1, 64]], -1)
                            keep(mask_su[half, 64:128], 0, [[1, 64]], -1)
                            keep(eye2[half, :], 0, [[1, 64]], -1, ALU.is_equal)
                            for l in range(6):
                                w = 1 << l
                                v4 = level[half, l, :].rearrange("p (b u w) -> p b u w", u=2, w=w)
                                pat = [[2 * w, 32 // w], [0, 2], [0, w]]
                                pool.memset(v4[:, :, 0, :], 0.0).then_inc(made, 1)
                                n += 1
                                pool.wait_ge(made, n)
                                keep(v4, 0, [[-2 * w, 32 // w], [0, 2], [0, w]], 1)
                                keep(v4, w - 1, pat, -1)
                        pool.wait_ge(made, n)
                        pool.memset(smalls[:, 0:1], 0.0).then_inc(masks_made, 1)
        def attention1_stage():
            q = area(A0 + 2048, BC)
            kk, vv, za = area(A0 + 4096, BC), area(A0 + 6144, BC), area(A0 + 8192, BC)
            bt = area(4096, 16)
            base = 26640
            q_st, k_st, v_st = (arena[:, base + n * TOK:base + (n + 1) * TOK] for n in range(3))
            sc = arena[:, base + 768:base + 1536].rearrange("p (h s) -> p h s", h=2)
            v_tok = arena[:, base + 1536:base + 1792].rearrange("p (t c) -> p t c", t=2)
            p_t = p_turned[:, :]
            small = smalls[:, :]
            DV = ["q_staged", "scored0", "scored1", "max0", "max0b", "max1", "max1b",
                  "rec0", "prob0", "rec1", "prob1", "gated"]
            AC = ["k_staged", "v_staged", "v_turned", "e0", "e0b", "e1", "e1b", "pt0", "pt1"]
            PE = ["v_tok", "s0", "s1", "turned0", "o0", "turned1", "o1"]
            with ExitStack() as e:
                table_loaded, table_masked = local(e, "table_loaded"), local(e, "table_masked")
                dv, ac, pe_ = Steps(e, "att_vector", DV), Steps(e, "att_scalar", AC), Steps(e, "att_tensor", PE)
                with nc.Block() as block:
                    @block.sync
                    def _(sp):
                        sp.dma_start(bt, bias_table_ap(I["rel_bias"], 513, 129)).then_inc(table_loaded, 16)

                    @block.gpsimd
                    def _(pool):
                        pool.wait_ge(table_loaded, 16)
                        pool.memset(bt[0:64, :, 0:64], NEG).then_inc(table_masked, 1)

                    @block.vector
                    def _(v):
                        v.wait_ge(table_masked, 1)
                        with v.Fori(0, BC) as j:
                            dv.did(v.tensor_scalar(q_st, q[:, at(j, 1), :], 0.125, None, ALU.mult), "q_staged")
                            for hh in range(2):
                                pe_.wait(v, f"s{hh}", j)
                                v.tensor_tensor(sc[:, hh, 0:128], sp_[:, hh, 0:128],
                                                bt[:, at(j * 2 + hh, 1), 0:128], ALU.add)
                                dv.did(v.tensor_tensor(sc[:, hh, 128:384], sp_[:, hh, 128:384],
                                                       bt[:, at(j * 2 + hh, 1), :], ALU.add), f"scored{hh}")
                            for hh in range(2):
                                dv.wait(v, f"scored{hh}", j)
                                dv.did(v.tensor_reduce(small[:, 4 * hh:4 * hh + 1], sc[:, hh, 0:128], AX, ALU.max, negate=True), f"max{hh}")
                                dv.did(v.tensor_reduce(small[:, 4 * hh + 1:4 * hh + 2], sc[:, hh, 128:384], AX, ALU.max, negate=True), f"max{hh}b")
                            for hh in range(2):
                                ac.wait(v, f"e{hh}b", j)
                                dv.did(v.reciprocal(small[:, 4 * hh + 2:4 * hh + 4], small[:, 8 + 2 * hh:10 + 2 * hh]), f"rec{hh}")
                                dv.wait(v, f"rec{hh}", j)
                                v.tensor_scalar(sc[:, hh, 0:128], sc[:, hh, 0:128], small[:, 4 * hh + 2:4 * hh + 3], None, ALU.mult)
                                dv.did(v.tensor_scalar(sc[:, hh, 128:384], sc[:, hh, 128:384], small[:, 4 * hh + 3:4 * hh + 4], None, ALU.mult), f"prob{hh}")
                            pe_.wait(v, "o1", j)
                            dv.did(v.tensor_tensor(q[:, at(j, 1), :], sp_[:, 3, 0:TOK], za[:, at(j, 1), :], ALU.mult), "gated")

                    @block.scalar
                    def _(act):
                        with act.Fori(0, BC) as j:
                            dv.wait(act, "q_staged", j)
                            ac.did(act.activation(k_st[:, ::-1], kk[:, at(j, 1), :].rearrange("p o t -> p (o t)"), ACT.Copy), "k_staged")
                            ac.did(act.activation(v_st[:, ::-1], vv[:, at(j, 1), :].rearrange("p o t -> p (o t)"), ACT.Copy), "v_staged")
                            pe_.wait(act, "v_tok", j)
                            ac.did(act.activation(v_tok, sp_[:, 3, 256:512].rearrange("p (t c) -> p t c", t=2), ACT.Copy), "v_turned")
                            for hh in range(2):
                                dv.wait(act, f"max{hh}b", j)
                                ac.did(act.activation(sc[:, hh, 0:128], sc[:, hh, 0:128], ACT.Exp, bias=small[:, 4 * hh:4 * hh + 1],
                                                      accum_out=small[:, 8 + 2 * hh:9 + 2 * hh]), f"e{hh}")
                                ac.did(act.activation(sc[:, hh, 128:384], sc[:, hh, 128:384], ACT.Exp, bias=small[:, 4 * hh + 1:4 * hh + 2],
                                                      accum_out=small[:, 9 + 2 * hh:10 + 2 * hh]), f"e{hh}b")
                            for hh in range(2):
                                pe_.wait(act, f"turned{hh}", j)
                                if hh:
                                    pe_.wait(act, "o0", j)
                                ac.did(act.activation(p_t, sp_[:, 2, 0:384], ACT.Copy), f"pt{hh}")

                    @block.tensor
                    def _(pe):
                        with pe.Fori(0, BC) as j:
                            ac.wait(pe, "v_staged", j)
                            for t in range(2):
                                m = pe.transpose(sp_[:, 3, 256 + t * P:256 + (t + 1) * P], v_st[:, t * P:(t + 1) * P], ident[:, :])
                            pe_.did(m, "v_tok")
                            for hh in range(2):
                                hs = slice(64 * hh, 64 * hh + 64)
                                pe.matmul(sp_[:, hh, 0:128], q_st[hs, 0:128], k_st[hs, 128:256], start=True, stop=True)
                                pe_.did(pe.matmul(sp_[:, hh, 128:384], q_st[hs, 128:256], k_st[hs, :], start=True, stop=True, skip_group_check=True), f"s{hh}")
                            ac.wait(pe, "v_turned", j)
                            for hh in range(2):
                                hs = slice(64 * hh, 64 * hh + 64)
                                dv.wait(pe, f"prob{hh}", j)
                                if hh:
                                    ac.wait(pe, "pt0", j)
                                for n in range(3):
                                    m = pe.transpose(sp_[:, 2, n * P:(n + 1) * P], sc[:, hh, n * P:(n + 1) * P], ident[:, :])
                                pe_.did(m, f"turned{hh}")
                                ac.wait(pe, f"pt{hh}", j)
                                pe.matmul(sp_[hs, 3, 0:128], v_tok[:, 1, hs], p_t[:, 0:128], start=True, stop=True, skip_group_check=True)
                                pe.matmul(sp_[hs, 3, 128:256], v_tok[:, 0, hs], p_t[:, 128:256], start=True, stop=False, skip_group_check=True)
                                pe_.did(pe.matmul(sp_[hs, 3, 128:256], v_tok[:, 1, hs], p_t[:, 256:384], start=False, stop=True, skip_group_check=True), f"o{hh}")

        def rwkv_stage():
            r_, k_, v_, a_ = area(18448, BC), area(20496, BC), area(22544, BC), area(24592, BC)
            zr = area(A0, BC)
            w2p, t1 = arena[:, 28744:29768], arena[:, 28488:28744]
            o = [12304]
            def buf(n):
                o[0] += n
                assert o[0] <= 8208 or (12304 <= o[0] - n and o[0] <= 16400)
                return arena[:, o[0] - n:o[0]]
            sg = buf(256).rearrange("p (t c) -> p t c", t=2)
            p_in, p_ex, p_inv = buf(256), buf(256), buf(256)
            kn, sqr, inv, kmod, tmp = buf(256), buf(256), buf(256), buf(256), buf(256)
            zrb = buf(512).rearrange("p (c g t) -> p c g t", c=4, g=2)
            b_t, k_t = buf(256), buf(256)
            tok = buf(768).rearrange("p (g c n) -> p g c n", g=3, c=4)
            assert o[0] <= 16400, o[0]
            o[0] = 4096
            ab = buf(512).rearrange("p (c s) -> p c s", c=4)
            ak = buf(512).rearrange("p (c s) -> p c s", c=4)
            al = buf(512).rearrange("p (u c s) -> p u c s", u=2, c=4)
            xx = buf(512).rearrange("p (u c s) -> p u c s", u=2, c=4)
            yb = buf(256).rearrange("p (c s) -> p c s", c=4)
            w0b, stp = buf(64), buf(64)
            states = (buf(64), buf(64))
            sa = buf(256).rearrange("p (c s) -> p c s", c=4)
            pc = buf(4)
            v_st, rk, bonus, y, ysq = buf(256), buf(256), buf(256), buf(256), buf(256)
            c4 = lambda x: x.rearrange("p (c t) -> p c t", c=4)
            th = lambda x: x.rearrange("p (h t) -> p h t", h=2)
            over4 = lambda m, w: m.rearrange("p (o t) -> p o t", o=1).to_broadcast([P, 4, w])
            eye4 = over4(eye2, 64)
            HS = [slice(0, 64), slice(64, 128)]

            DV = ["kk", "kk_squared", "a_scaled", "kmod", "rk", "norm_floored", "norm_inverted", "kk_normed",
                  "kka", "r_hat", "z_hat", "b_hat", "k_hat", "ab", "ak", "al0", "xt0", "x0"]
            for l in range(1, 6):
                DV += [f"al{l}", f"xx{l}"]
            for c in range(4):
                DV += [f"sa{c}"] + ([f"st_sum{c}", f"st{c}"] if 0 < c < 3 else [f"st{c}"] if c == 0 else [])
            DV += ["y_centred", "variance", "deviation_inverted", "y_normed", "y_scaled", "bonus_v", "y_bonus", "y_gated"]
            AC = ["v_staged", "decay", "root", "p_in", "p_ex", "p_inv", "p_chunk", "tok_vb", "tok_k", "bonus"]
            AC += [f"y{l}" for l in range(1, 6)] + [f"w{c}" for c in range(4)] + ["y_out", "y_squared", "deviation"]
            PE = ["decay_logits", "kk_norm", "cumulated", "ab", "ak", "tok_vb", "tok_k", "bonus", "n0"]
            for l in range(1, 6):
                PE += [f"y{l}", f"xx{l}"]
            for c in range(4):
                PE += [f"w{c}", f"sa{c}"] + ([f"st{c}"] if c < 3 else [])
            PE += ["o", "mean", "var"]

            with ExitStack() as e:
                waited = local(e, "rwkv_tensor_waited")
                dv, ac, pe_ = Steps(e, "rwkv_vector", DV), Steps(e, "rwkv_scalar", AC), Steps(e, "rwkv_tensor", PE)
                with nc.Block() as block:
                    @block.vector
                    def _(v):
                        with v.Fori(0, BC) as j:
                            one = at(j, 1)
                            pr = lambda name: prm[:, at(j + rows[name], 1)]
                            dv.did(v.tensor_scalar(kn, k_[:, one, :], pr("k_k"), None, ALU.mult), "kk")
                            dv.wait(v, "kk", j)
                            dv.did(v.tensor_tensor(sqr, kn, kn, ALU.mult), "kk_squared")
                            dv.did(v.tensor_scalar(kmod, a_[:, one, :], pr("k_a"), omka[:, one], ALU.mult, ALU.add), "a_scaled")
                            dv.wait(v, "a_scaled", j)
                            dv.did(v.tensor_tensor(kmod, kmod, k_[:, one, :], ALU.mult), "kmod")
                            dv.wait(v, "kmod", j)
                            dv.did(v.scalar_tensor_tensor(rk, r_[:, one, :], pr("r_k"), kmod, ALU.mult, ALU.mult), "rk")
                            ac.wait(v, "root", j)
                            dv.did(v.tensor_scalar(inv, inv, 1e-12, None, ALU.max), "norm_floored")
                            dv.wait(v, "norm_floored", j)
                            dv.did(v.reciprocal(inv, inv), "norm_inverted")
                            dv.wait(v, "norm_inverted", j)
                            dv.did(v.tensor_tensor(kn, kn, inv, ALU.mult), "kk_normed")
                            dv.wait(v, "kk_normed", j)
                            dv.did(v.tensor_tensor(tmp, kn, a_[:, one, :], ALU.mult), "kka")
                            ac.wait(v, "p_inv", j)
                            dv.did(v.tensor_tensor(zrb[:, :, 1, :], c4(r_[:, one, :].rearrange("p o t -> p (o t)")), c4(p_in), ALU.mult), "r_hat")
                            dv.did(v.scalar_tensor_tensor(zrb[:, :, 0, :], c4(kn), -1.0, c4(p_ex), ALU.mult, ALU.mult), "z_hat")
                            dv.wait(v, "kka", j)
                            dv.did(v.tensor_tensor(b_t, tmp, p_inv, ALU.mult), "b_hat")
                            dv.did(v.tensor_tensor(k_t, kmod, p_inv, ALU.mult), "k_hat")
                            m4 = over4(mask_su, 128)
                            pe_.wait(v, "ab", j)
                            dv.did(v.tensor_tensor(ab, sp_[:, 0, :].rearrange("p (c s) -> p c s", c=4), m4, ALU.mult), "ab")
                            pe_.wait(v, "ak", j)
                            dv.did(v.tensor_tensor(ak, sp_[:, 3, :].rearrange("p (c s) -> p c s", c=4), m4, ALU.mult), "ak")
                            dv.wait(v, "ab", j)
                            dv.did(v.tensor_tensor(al[:, 0], ab[:, :, 0:64], over4(level[:, 0, :], 64), ALU.mult), "al0")
                            dv.wait(v, "al0", j)
                            dv.did(v.tensor_tensor(xx[:, 1], al[:, 0], eye4, ALU.add), "xt0")
                            pe_.wait(v, "n0", j)
                            dv.did(v.tensor_tensor(xx[:, 0], sp_[:, 0, 0:256].rearrange("p (c s) -> p c s", c=4), eye4, ALU.add), "x0")
                            for l in range(1, 6):
                                if l >= 2:
                                    pe_.wait(v, f"xx{l - 1}", j)
                                dv.did(v.tensor_tensor(al[:, l % 2], ab[:, :, 0:64], over4(level[:, l, :], 64), ALU.mult), f"al{l}")
                                pe_.wait(v, f"xx{l}", j)
                                dv.wait(v, f"xx{l - 1}" if l > 1 else "x0", j)
                                dv.did(v.tensor_tensor(xx, sp_[:, 1, :].rearrange("p (u c s) -> p u c s", u=2, c=4), xx, ALU.add), f"xx{l}")
                            for c in range(4):
                                pe_.wait(v, f"sa{c}", j)
                                dv.did(v.tensor_copy(sa[:, c, :], sp_[:, 1, 0:64]), f"sa{c}")
                                if c == 0:
                                    pe_.wait(v, "st0", j)
                                    dv.did(v.tensor_scalar(states[0], sp_[:, 3, 0:64], pc[:, 0:1], None, ALU.mult), "st0")
                                elif c < 3:
                                    pe_.wait(v, f"st{c}", j)
                                    dv.did(v.tensor_tensor(stp, sp_[:, 3, 0:64], states[(c - 1) % 2], ALU.add), f"st_sum{c}")
                                    dv.wait(v, f"st_sum{c}", j)
                                    dv.did(v.tensor_scalar(states[c % 2], stp, pc[:, c:c + 1], None, ALU.mult), f"st{c}")
                            pe_.wait(v, "mean", j)
                            dv.did(v.scalar_tensor_tensor(y, sp_[:, 0, 0:256], -1.0 / 64, y, ALU.mult, ALU.add), "y_centred")
                            pe_.wait(v, "var", j)
                            dv.did(v.tensor_scalar(inv, sp_[:, 1, 0:256], 1.0 / 64, 64e-5, ALU.mult, ALU.add), "variance")
                            ac.wait(v, "deviation", j)
                            dv.did(v.reciprocal(inv, inv), "deviation_inverted")
                            dv.wait(v, "deviation_inverted", j)
                            dv.did(v.tensor_tensor(y, y, inv, ALU.mult), "y_normed")
                            dv.wait(v, "y_normed", j)
                            dv.did(v.tensor_scalar(y, y, pr("ln_g"), pr("ln_b"), ALU.mult, ALU.add), "y_scaled")
                            dv.did(v.tensor_tensor(bonus, bonus, v_st, ALU.mult), "bonus_v")
                            dv.wait(v, "bonus_v", j)
                            dv.did(v.tensor_tensor(y, y, bonus, ALU.add), "y_bonus")
                            dv.wait(v, "y_bonus", j)
                            dv.did(v.tensor_tensor(zr[:, one, :], y, zr[:, one, :], ALU.mult), "y_gated")
                            dv.wait(v, "y_gated", j)

                    @block.scalar
                    def _(act):
                        with act.Fori(0, BC) as j:
                            dv.wait(act, "kk", j)
                            ac.did(act.activation(v_st, v_[:, at(j, 1), :].rearrange("p o t -> p (o t)"), ACT.Copy), "v_staged")
                            pe_.wait(act, "decay_logits", j)
                            ac.did(act.activation(sg, sp_[:, 0, 0:256].rearrange("p (t c) -> p t c", t=2), ACT.Sigmoid), "decay")
                            pe_.wait(act, "kk_norm", j)
                            ac.did(act.activation(inv, sp_[:, 1, 0:256], ACT.Sqrt), "root")
                            pe_.wait(act, "cumulated", j)
                            cum = sp_[:, 2, :].rearrange("p (h g t) -> p h g t", h=2, g=2)
                            ac.did(act.activation(th(p_in), cum[:, :, 0, :], ACT.Exp, bias=centre[:, 0:1], scale=-DECAY), "p_in")
                            ac.did(act.activation(th(p_ex), cum[:, :, 1, :], ACT.Exp, bias=centre[:, 0:1], scale=-DECAY), "p_ex")
                            ac.did(act.activation(th(p_inv), cum[:, :, 0, :], ACT.Exp, bias=centre[:, 1:2], scale=DECAY), "p_inv")
                            ac.did(act.activation(pc.rearrange("p (h c) -> p h c", h=2), cum[:, :, 0, 63:128:64], ACT.Exp, scale=-DECAY), "p_chunk")
                            pe_.wait(act, "tok_vb", j)
                            ac.did(act.activation(tok[:, 0:2], sp_[:, 2, :].rearrange("p (g c n) -> p g c n", g=2, c=4), ACT.Copy), "tok_vb")
                            pe_.wait(act, "bonus", j)
                            ac.did(act.activation(tok[:, 2], sp_[:, 1, 256:512].rearrange("p (c n) -> p c n", c=4), ACT.Copy), "tok_k")
                            ac.did(act.activation(bonus, sp_[:, 1, 0:256], ACT.Copy), "bonus")
                            for l in range(1, 6):
                                pe_.wait(act, f"y{l}", j)
                                ac.did(act.activation(yb, sp_[:, 0, 0:256].rearrange("p (c s) -> p c s", c=4), ACT.Copy), f"y{l}")
                            for c in range(4):
                                pe_.wait(act, f"w{c}", j)
                                ac.did(act.activation(w0b, sp_[:, 0, 0:64], ACT.Copy), f"w{c}")
                            pe_.wait(act, "o", j)
                            ac.did(act.activation(y, sp_[:, 2, 0:256], ACT.Copy), "y_out")
                            dv.wait(act, "y_centred", j)
                            ac.did(act.activation(ysq, y, ACT.Square), "y_squared")
                            dv.wait(act, "variance", j)
                            ac.did(act.activation(inv, inv, ACT.Sqrt), "deviation")

                    @block.tensor
                    def _(pe):
                        def wait(steps, step, j):
                            steps.wait(pe, step, j)
                            pe.sem_inc(waited, 1)

                        def mm(out, lhs, rhs, start=True, stop=True):
                            return pe.matmul(out, lhs, rhs, start=start, stop=stop, skip_group_check=True)
                        with pe.Fori(0, BC) as j:
                            wait(dv, "kk", j)
                            for t in range(2):
                                m = mm(sp_[:, 0, t * P:(t + 1) * P], t1[0:65, t * P:(t + 1) * P], w2p[0:65, at(j * P, P)])
                            pe_.did(m, "decay_logits")
                            wait(dv, "kk_squared", j)
                            pe_.did(mm(sp_[:, 1, 0:256], headones[:, :], sqr), "kk_norm")
                            wait(ac, "decay", j)
                            for t in range(2):
                                m = mm(sp_[:, 2, t * 256:(t + 1) * 256], sg[:, t, :], tri)
                            pe_.did(m, "cumulated")
                            wait(dv, "b_hat", j)
                            for c in range(4):
                                for s in HS:
                                    m = mm(sp_[s, 0, c * 128:(c + 1) * 128], b_t[s, c * 64:(c + 1) * 64], zrb[s, c].rearrange("p g t -> p (g t)"))
                            pe_.did(m, "ab")
                            wait(dv, "k_hat", j)
                            for c in range(4):
                                for s in HS:
                                    m = mm(sp_[s, 3, c * 128:(c + 1) * 128], k_t[s, c * 64:(c + 1) * 64], zrb[s, c].rearrange("p g t -> p (g t)"))
                            pe_.did(m, "ak")
                            wait(ac, "p_chunk", j)
                            for g, x in enumerate((v_st, b_t)):
                                for c in range(4):
                                    for s in HS:
                                        m = mm(sp_[s, 2, g * 256 + c * 64:g * 256 + (c + 1) * 64], x[s, c * 64:(c + 1) * 64], eye2[s, :])
                            pe_.did(m, "tok_vb")
                            for c in range(4):
                                for s in HS:
                                    m = mm(sp_[s, 1, 256 + c * 64:256 + (c + 1) * 64], k_t[s, c * 64:(c + 1) * 64], eye2[s, :])
                            pe_.did(m, "tok_k")
                            pe_.did(mm(sp_[:, 1, 0:256], headones[:, :], rk), "bonus")
                            wait(dv, "al0", j)
                            for c in range(4):
                                for s in HS:
                                    m = mm(sp_[s, 0, c * 64:(c + 1) * 64], al[s, 0, c, :], eye2[s, :])
                            pe_.did(m, "n0")
                            wait(ac, "bonus", j)
                            for l in range(1, 6):
                                wait(dv, f"al{l}", j)
                                wait(dv, "x0" if l == 1 else f"xx{l - 1}", j)
                                for c in range(4):
                                    for s in HS:
                                        m = mm(sp_[s, 0, c * 64:(c + 1) * 64], al[s, l % 2, c, :], xx[s, 0, c, :])
                                pe_.did(m, f"y{l}")
                                wait(ac, f"y{l}", j)
                                for c in range(4):
                                    for s in HS:
                                        mm(sp_[s, 1, c * 64:(c + 1) * 64], xx[s, 1, c, :], yb[s, c, :])
                                        m = mm(sp_[s, 1, 256 + c * 64:256 + (c + 1) * 64], yb[s, c, :], xx[s, 1, c, :])
                                pe_.did(m, f"xx{l}")
                            wait(dv, "xx5", j)
                            wait(dv, "ak", j)
                            for c in range(4):
                                if c:
                                    wait(dv, f"st{c - 1}", j)
                                for s in HS:
                                    if c:
                                        mm(sp_[s, 0, 0:64], zrb[s, c, 0, :], states[(c - 1) % 2][s, :], True, False)
                                    m = mm(sp_[s, 0, 0:64], ak[s, c, 0:64], tok[s, 0, c, :], c == 0, True)
                                pe_.did(m, f"w{c}")
                                wait(ac, f"w{c}", j)
                                for s in HS:
                                    m = mm(sp_[s, 1, 0:64], xx[s, 1, c, :], w0b[s, :])
                                pe_.did(m, f"sa{c}")
                                wait(dv, f"sa{c}", j)
                                if c < 3:
                                    for s in HS:
                                        mm(sp_[s, 3, 0:64], tok[s, 1, c, :], sa[s, c, :], True, False)
                                        m = mm(sp_[s, 3, 0:64], tok[s, 2, c, :], tok[s, 0, c, :], False, True)
                                    pe_.did(m, f"st{c}")
                                for s in HS:
                                    oc = sp_[s, 2, c * 64:(c + 1) * 64]
                                    if c:
                                        mm(oc, states[(c - 1) % 2][s, :], zrb[s, c, 1, :], True, False)
                                    mm(oc, sa[s, c, :], ab[s, c, 64:128], c == 0, False)
                                    m = mm(oc, tok[s, 0, c, :], ak[s, c, 64:128], False, True)
                                if c == 3:
                                    pe_.did(m, "o")
                            wait(ac, "y_out", j)
                            pe_.did(mm(sp_[:, 0, 0:256], headones[:, :], y), "mean")
                            wait(ac, "y_squared", j)
                            pe_.did(mm(sp_[:, 1, 0:256], headones[:, :], ysq), "var")
        def gates_evac(eng, i, b, ps):
            mg = area(18448, 32)
            for n in range(4):
                ins = eng.activation(mg[:, at(i * 8 + (b * 4 + n), 1), :], ps[:, n, :], ACT.Sigmoid,
                                     bias=prm[:, at(i * 8 + (b * 4 + n + rows["b_merge"]), 1)])
            return ins

        def branch_stage():
            s = S["branch"]
            mg, mer = area(18448, 32), area(12304, DC)
            part = area(4096, 4)
            per = s.blocks // 2
            xb = (lambda b, c: x_parts[:, 0, 8 * (b % 2) + c, :], lambda b, c: x_parts[:, 1, 8 * (b % 2) + c, :])
            with ExitStack() as e:
                added = local(e, "added")
                def out(v, i, b):
                    c = i * 8 + (b // 2) * 4
                    block_done(v, s, i, b)
                    if b % 2 == 0:
                        v.tensor_tensor(mer[:, at(c, 4), :], gp[:, 0], mg[:, at(c, 4), :], ALU.mult).then_inc(pair_evacuated[0], 1)
                    else:
                        v.tensor_tensor(part, gp[:, 1], mg[:, at(c + 16, 4), :], ALU.mult).then_inc(pair_evacuated[1], 1)
                        for k in range(2):
                            v.wait_ge(pair_evacuated[k], i * per + (s.block0 // 2 + b // 2 + 2))
                        v.tensor_tensor(mer[:, at(c, 4), :], mer[:, at(c, 4), :], part, ALU.add).then_inc(added, 1)
                        v.wait_ge(added, i * per + (b // 2 + 1))
                with nc.Block() as block:
                    @block.sync
                    def _(sp):
                        load_section(sp, s)

                    @block.tensor
                    def _(pe):
                        multiply_section(pe, s, *xb)

                    @block.scalar
                    def _(act):
                        split_section(act, s, split_high, None)

                    @block.vector
                    def _(v):
                        split_section(v, s, split_low, out)
        HEADS2, KV2 = 16, 4

        def bucket_edges():
            def bucket(n):
                if n < 16:
                    return n
                return min(16 + int(math.log(n / 16) / math.log(128 / 16) * 16 + 1e-9), 31)
            edges = []
            for b in range(32):
                ds = [n for n in range(TOK) if bucket(n) == b]
                edges.append((min(ds), max(ds) + 1) if ds else None)
            return edges

        scratch_rows = nc.dram_tensor("bias_rows", [16, 384], F32, kind="Internal").ap()

        def bias2_stage():
            t2 = area(4096, 16)
            by_bucket = arena[:, 27024:27056]
            by_dist = arena[:, 27056:27440]
            with ExitStack() as e:
                loaded, spread, stored, tabled = (local(e, x) for x in ("buckets_loaded", "spread", "rows_stored", "tabled"))
                with nc.Block() as block:
                    @block.sync
                    def _(sp):
                        with nc.allow_non_contiguous_dma(reason="512 numbers"):
                            sp.dma_start(by_bucket[0:16, :], I["rel_bias_2"].rearrange("b h -> h b")).then_inc(loaded, 16)
                        sp.wait_ge(spread, 33)
                        sp.dma_start(scratch_rows, by_dist[0:16, :]).then_inc(stored, 16)
                        sp.wait_ge(stored, 16)
                        sp.dma_start(t2, bass.AP(scratch_rows.tensor, 0, [[1, P], [384, 16], [1, TOK]])).then_inc(tabled, 16)
                        sp.wait_ge(tabled, 16)

                    @block.vector
                    def _(v):
                        v.wait_ge(loaded, 16)
                        v.tensor_copy(by_dist[0:16, 0:127], by_bucket[0:16, 0:1].to_broadcast([16, 127])).then_inc(spread, 1)
                        n = 0
                        for b, edge in enumerate(bucket_edges()):
                            lo, hi = edge
                            if b == 31:
                                hi = TOK + 1
                            v.tensor_copy(by_dist[0:16, 127 + lo:127 + hi],
                                          by_bucket[0:16, b:b + 1].to_broadcast([16, hi - lo])).then_inc(spread, 1)

        def index_evac(eng, i, b, ps):
            if b == 0:
                return eng.activation(area(A0, 28)[:, 24:28, :], ps, ACT.Copy)
            return eng.activation(area(A0, 30)[:, 28:30, :], ps[:, 0:2, :], ACT.Copy)

        FAR, TAKEN = -1.0e38, -3.0e38
        def select_stage():
            kept = arena[:, 26640:27024]
            qkvi = area(A0, 28)
            ki = arena[:, A0 + 7168:A0 + 7424]
            wi = arena[:, A0 + 7424:A0 + 7680]
            score = arena[:, 27024:27536].rearrange("p (h s) -> p h s", h=2)
            part = arena[:, 27536:28048].rearrange("p (h s) -> p h s", h=2)
            wt = smalls[:, 0:16].rearrange("p (t h) -> p t h", t=2)
            best = smalls[:, 16:32].rearrange("p (t n) -> p t n", t=2)
            with ExitStack() as e:
                turned, wt_ready, scored, weighed, masked, picked = (
                    local(e, x) for x in ("wi_turned", "wi_ready", "scored", "weighed", "masked", "picked"))
                with nc.Block() as block:
                    @block.tensor
                    def _(pe):
                        for t in range(2):
                            m = pe.transpose(sp_[:, 0, t * 8:(t + 1) * 8], wi[0:8, t * P:(t + 1) * P], ident[0:8, 0:8])
                        m.then_inc(turned, 1)
                        pe.wait_ge(wt_ready, 1)
                        for n in range(8):
                            s = slice(64 * (n % 2), 64 * (n % 2) + 64)
                            if n >= 4:
                                pe.wait_ge(weighed, n - 3)
                            for t in range(2):
                                m = pe.matmul(sp_[:, n % 4, t * TOK:(t + 1) * TOK], qkvi[s, 24 + n // 2, t * P:(t + 1) * P],
                                              ki[s, :], start=True, stop=True, skip_group_check=True)
                            m.then_inc(scored, 1)

                    @block.vector
                    def _(v):
                        v.wait_ge(turned, 1)
                        v.tensor_scalar(wt, sp_[:, 0, 0:16].rearrange("p (t h) -> p t h", t=2),
                                        (8 ** -0.5) * (64 ** -0.5), None, ALU.mult).then_inc(wt_ready, 1)
                        v.wait_ge(wt_ready, 1)
                        steps = 0
                        for n in range(8):
                            v.wait_ge(scored, n + 1)
                            dst = part if n else score
                            if n > 1:
                                v.wait_ge(masked, n - 1)
                            for t in range(2):
                                ins = v.tensor_scalar(dst[:, t, :], sp_[:, n % 4, t * TOK:(t + 1) * TOK], 0.0,
                                                      wt[:, t, n:n + 1], ALU.max, ALU.mult)
                            ins.then_inc(weighed, 1)
                            if n:
                                v.wait_ge(weighed, n + 1)
                                v.tensor_tensor(score, score, part, ALU.add).then_inc(masked, 1)
                        v.wait_ge(masked, 8)
                        for n in range(8):
                            for t in range(2):
                                if n:
                                    v.wait_ge(picked, 4 * n - 1 + t)
                                v.max(best[:, t, :], score[:, t, :]).then_inc(picked, 1)
                            for t in range(2):
                                v.wait_ge(picked, 4 * n + 1 + t)
                                v.match_replace(score[:, t, :], best[:, t, :], score[:, t, :], TAKEN).then_inc(picked, 1)
                        v.wait_ge(picked, 32)
                        for t, (c0, w) in enumerate(((0, 128), (128, 256))):
                            v.tensor_scalar(kept[:, c0:c0 + w], score[:, t, w - 1::-1], -2.0e38, NEG, ALU.is_gt, ALU.mult).then_inc(picked, 1)

                    @block.gpsimd
                    def _(pool):
                        pool.wait_ge(masked, 7)
                        pool.affine_select(out=score, in_=score, compare_op=ALU.is_ge, fill=FAR, base=0,
                                           pattern=[[P, 2], [-1, TOK]], channel_multiplier=1).then_inc(masked, 1)
                        pool.wait_ge(picked, 34)
                        pool.affine_select(out=kept[:, 0:128], in_=kept[:, 0:128], compare_op=ALU.is_ge, fill=NEG,
                                           base=-127, pattern=[[1, 128]], channel_multiplier=1).then_inc(masked, 1)
                        pool.wait_ge(masked, 9)
                        pool.affine_select(out=kept[:, 128:384], in_=kept[:, 128:384], compare_op=ALU.is_ge, fill=NEG,
                                           base=-127, pattern=[[1, TOK]], channel_multiplier=1).then_inc(masked, 1)

        def attention_stage(q, k_of, v_of, groups, rep, scale, logits, weigh, nlog, scratch):
            q_st, v_st = arena[:, scratch:scratch + 256], arena[:, scratch + 256:scratch + 512]
            v_tok = arena[:, scratch + 512:scratch + 768].rearrange("p (t c) -> p t c", t=2)
            sc = arena[:, scratch + 768:scratch + 1152]
            k_st = arena[:, scratch + 1152:scratch + 1408]
            small = smalls[:, :]
            p_t = p_turned[:, :]
            DV, AC, PE = ["v_staged", "k_staged"], ["v_tok"], ["v_tok"]
            for r in range(rep):
                DV += [f"q{r}"] + [f"log{r}_{n}" for n in range(nlog)] + [f"max{r}", f"maxb{r}", f"w{r}", f"rec{r}", f"p{r}", f"out{r}"]
                AC += [f"e{r}", f"pt{r}"]
                PE += [f"s{r}", f"t{r}", f"o{r}"]
            with ExitStack() as e:
                dv, ac, pe_ = Steps(e, "att_vector", DV), Steps(e, "att_scalar", AC), Steps(e, "att_tensor", PE)
                with nc.Block() as block:
                    @block.vector
                    def _(v):
                        with v.Fori(0, groups) as g:
                            dv.did(v.tensor_scalar(v_st[:, ::-1], v_of(g).rearrange("p o t -> p (o t)"), 1.0, None, ALU.mult), "v_staged")
                            dv.did(v.tensor_scalar(k_st[:, ::-1], k_of(g).rearrange("p o t -> p (o t)"), 1.0, None, ALU.mult), "k_staged")
                            for r in range(rep):
                                head = g * rep + r
                                dv.did(v.tensor_scalar(q_st, q[:, at(head, 1), :].rearrange("p o t -> p (o t)"), scale, None, ALU.mult), f"q{r}")
                                pe_.wait(v, f"s{r}", g)
                                logits(v, dv, g, r, head, sp_[:, 0, 0:384], sc)
                                dv.wait(v, f"log{r}_{nlog - 1}", g)
                                dv.did(v.tensor_reduce(small[:, 0:1], sc[:, 0:128], AX, ALU.max, negate=True), f"max{r}")
                                dv.did(v.tensor_reduce(small[:, 1:2], sc[:, 128:384], AX, ALU.max, negate=True), f"maxb{r}")
                                ac.wait(v, f"e{r}", g)
                                weigh(v, g, sc, small)
                                dv.did(v.tensor_copy(small[:, 8:10], small[:, 4:6]), f"w{r}")
                                dv.wait(v, f"w{r}", g)
                                dv.did(v.reciprocal(small[:, 2:4], small[:, 8:10]), f"rec{r}")
                                dv.wait(v, f"rec{r}", g)
                                v.tensor_scalar(sc[:, 0:128], sc[:, 0:128], small[:, 2:3], None, ALU.mult)
                                dv.did(v.tensor_scalar(sc[:, 128:384], sc[:, 128:384], small[:, 3:4], None, ALU.mult), f"p{r}")
                                pe_.wait(v, f"o{r}", g)
                                dv.did(v.tensor_scalar(q[:, at(head, 1), :], sp_[:, 3, 0:TOK].rearrange("p (o t) -> p o t", o=1), 1.0, None, ALU.mult), f"out{r}")
                                dv.wait(v, f"out{r}", g)

                    @block.scalar
                    def _(act):
                        with act.Fori(0, groups) as g:
                            pe_.wait(act, "v_tok", g)
                            ac.did(act.activation(v_tok, sp_[:, 2, 0:256].rearrange("p (t c) -> p t c", t=2), ACT.Copy), "v_tok")
                            for r in range(rep):
                                dv.wait(act, f"maxb{r}", g)
                                act.activation(sc[:, 0:128], sc[:, 0:128], ACT.Exp, bias=small[:, 0:1], accum_out=small[:, 4:5])
                                ac.did(act.activation(sc[:, 128:384], sc[:, 128:384], ACT.Exp, bias=small[:, 1:2], accum_out=small[:, 5:6]), f"e{r}")
                                pe_.wait(act, f"t{r}", g)
                                ac.did(act.activation(p_t, sp_[:, 1, 0:384], ACT.Copy), f"pt{r}")

                    @block.tensor
                    def _(pe):
                        with pe.Fori(0, groups) as g:
                            dv.wait(pe, "v_staged", g)
                            for t in range(2):
                                m = pe.transpose(sp_[:, 2, t * P:(t + 1) * P], v_st[:, t * P:(t + 1) * P], ident[:, :])
                            pe_.did(m, "v_tok")
                            for r in range(rep):
                                dv.wait(pe, f"q{r}", g)
                                pe.matmul(sp_[:, 0, 0:128], q_st[:, 0:128], k_st[:, 128:256], start=True, stop=True, skip_group_check=True)
                                pe_.did(pe.matmul(sp_[:, 0, 128:384], q_st[:, 128:256], k_st, start=True, stop=True, skip_group_check=True), f"s{r}")
                                dv.wait(pe, f"p{r}", g)
                                for n in range(3):
                                    m = pe.transpose(sp_[:, 1, n * P:(n + 1) * P], sc[:, n * P:(n + 1) * P], ident[:, :])
                                pe_.did(m, f"t{r}")
                                ac.wait(pe, f"pt{r}", g)
                                pe.matmul(sp_[:, 3, 0:128], v_tok[:, 1, :], p_t[:, 0:128], start=True, stop=True, skip_group_check=True)
                                pe.matmul(sp_[:, 3, 128:256], v_tok[:, 0, :], p_t[:, 128:256], start=True, stop=False, skip_group_check=True)
                                pe_.did(pe.matmul(sp_[:, 3, 128:256], v_tok[:, 1, :], p_t[:, 256:384], start=False, stop=True, skip_group_check=True), f"o{r}")

        def attention2_stage():
            t2, kept = area(4096, 16), arena[:, 26640:27024]
            def logits(v, dv, g, r, head, ps, sc):
                v.tensor_tensor(sc[:, 0:128], ps[:, 0:128], t2[:, at(head, 1), 0:128].rearrange("p o t -> p (o t)"), ALU.add)
                dv.did(v.tensor_tensor(sc[:, 128:384], ps[:, 128:384], t2[:, at(head, 1), :].rearrange("p o t -> p (o t)"), ALU.add), f"log{r}_0")
                dv.wait(v, f"log{r}_0", g)
                dv.did(v.tensor_tensor(sc, sc, kept, ALU.add), f"log{r}_1")
            attention_stage(area(A0, 16), lambda g: area(A0, 28)[:, at(g + 16, 1), :], lambda g: area(A0, 28)[:, at(g + 20, 1), :],
                            KV2, HEADS2 // KV2, 128 ** -0.5, logits, lambda v, g, sc, small: None, 2, 27024)

        def sgu_stage():
            u, vv = area(15888, DC), area(19984, DC)
            sq = area(24080, DC)
            ws = arena[:, 4096:6144].rearrange("p (g s) -> p g s", g=16)
            bs = arena[:, 6144:8192].rearrange("p (g s) -> p g s", g=16)
            vn, ws_st = variance_t[:, :], p_turned[:, 256:384]
            tok = sq_tok = arena[:, 24080:24464].rearrange("p (n s) -> p n s", n=3)
            mean = variance[:, :]
            DV = ["normed", "shifted", "w_turned", "out"]
            AC = ["w_staged", "tok"]
            PE = ["turned", "mixed"]
            with ExitStack() as e:
                loaded, summed, meaned, centred, squared, summed2, meaned2, rooted, inverted = (
                    local(e, x) for x in ("sgu_loaded", "summed", "meaned", "centred", "squared", "summed2", "meaned2", "rooted", "inverted"))
                dv, ac, pe_ = Steps(e, "sgu_vector", DV), Steps(e, "sgu_scalar", AC), Steps(e, "sgu_tensor", PE)
                with nc.Block() as block:
                    @block.sync
                    def _(sp):
                        for q in range(4):
                            sp.dma_start(ws[:, 4 * q:4 * q + 4], I["sgu_w_2"][0, 4 * q:4 * q + 4].rearrange("g t s -> t g s")).then_inc(loaded, 16)
                        sp.dma_start(bs[0:1], I["sgu_b_2"]).then_inc(loaded, 16)
                        sp.wait_ge(loaded, 80)

                    @block.vector
                    def _(v):
                        v.wait_ge(summed, 1)
                        v.tensor_scalar(mean, sp_[:, 0, 0:TOK], 1.0 / D, None, ALU.mult).then_inc(meaned, 1)
                        v.wait_ge(meaned, 1)
                        for q in range(4):
                            v.tensor_tensor(vv[:, 4 * q:4 * q + 4, :], vv[:, 4 * q:4 * q + 4, :],
                                            mean.rearrange("p (o t) -> p o t", o=1).to_broadcast([P, 4, TOK]),
                                            ALU.subtract).then_inc(centred, 1)
                        v.wait_ge(centred, 4)
                        inv_root(v, sp_[:, 1, 0:TOK], D, summed2, meaned2, rooted, inverted)
                        with v.Fori(0, 16) as g:
                            dv.did(v.scalar_tensor_tensor(vn, vv[:, at(g, 1), :].rearrange("p o t -> p (o t)"),
                                                          prm[:, at(g + rows["sgu_g"], 1)], rstd[:, :], ALU.mult, ALU.mult), "normed")
                            dv.wait(v, "normed", g)
                            dv.did(v.tensor_scalar(vn, vn, prm[:, at(g + rows["sgu_b"], 1)], None, ALU.add), "shifted")
                            ac.wait(v, "tok", g)
                            pe_.wait(v, "turned", g)
                            dv.did(v.tensor_tensor(tok[:, 2, :], sp_[:, 3, 0:P], tri128, ALU.mult), "w_turned")
                            pe_.wait(v, "mixed", g)
                            dv.did(v.tensor_tensor(u[:, at(g, 1), :].rearrange("p o t -> p (o t)"), sp_[:, 0, 0:TOK],
                                                   u[:, at(g, 1), :].rearrange("p o t -> p (o t)"), ALU.mult), "out")

                    @block.scalar
                    def _(act):
                        for q in range(4):
                            act.wait_ge(centred, q + 1)
                            act.activation(sq[:, 4 * q:4 * q + 4, :], vv[:, 4 * q:4 * q + 4, :], ACT.Square).then_inc(squared, 1)
                        act.wait_ge(meaned2, 1)
                        act.activation(rstd[:, :], variance[:, :], ACT.Sqrt).then_inc(rooted, 1)
                        act.wait_ge(loaded, 80)
                        with act.Fori(0, 16) as g:
                            dv.wait(act, "normed", g)
                            ac.did(act.activation(ws_st, ws[:, at(g, 1), :].rearrange("p o t -> p (o t)"), ACT.Copy), "w_staged")
                            pe_.wait(act, "turned", g)
                            ac.did(act.activation(tok[:, 0:2, :], sp_[:, 2, 0:256].rearrange("p (n s) -> p n s", n=2), ACT.Copy), "tok")

                    @block.tensor
                    def _(pe):
                        for c in range(DC):
                            m = pe.matmul(sp_[:, 0, 0:TOK], ones[:, :], vv[:, c, :], start=(c == 0), stop=(c == DC - 1))
                        m.then_inc(summed, 1)
                        for c in range(DC):
                            pe.wait_ge(squared, c // 4 + 1)
                            m = pe.matmul(sp_[:, 1, 0:TOK], ones[:, :], sq[:, c, :], start=(c == 0), stop=(c == DC - 1))
                        m.then_inc(summed2, 1)
                        pe.wait_ge(loaded, 80)
                        with pe.Fori(0, 16) as g:
                            dv.wait(pe, "shifted", g)
                            ac.wait(pe, "w_staged", g)
                            for t in range(2):
                                pe.transpose(sp_[:, 2, t * P:(t + 1) * P], vn[:, t * P:(t + 1) * P], ident[:, :])
                            pe_.did(pe.transpose(sp_[:, 3, 0:P], ws_st, ident[:, :]), "turned")
                            dv.wait(pe, "w_turned", g)
                            for t in range(2):
                                pe.matmul(sp_[:, 0, t * P:(t + 1) * P], ones[0:1, :], bs[0:1, at(g, 1), :].rearrange("p o t -> p (o t)"),
                                          start=True, stop=False, skip_group_check=True)
                                m = pe.matmul(sp_[:, 0, t * P:(t + 1) * P], tok[:, t, :], tok[:, 2, :],
                                              start=False, stop=True, skip_group_check=True)
                            pe_.did(m, "mixed")

        def merge2_stage():
            att, u, ga, gb = area(A0, DC), area(15888, DC), area(19984, DC), area(24080, DC)
            with ExitStack() as e:
                gated, added = local(e, "gated"), local(e, "added")
                with nc.Block() as block:
                    @block.vector
                    def _(v):
                        v.tensor_tensor(att, att, ga, ALU.mult).then_inc(gated, 1)
                        v.tensor_tensor(u, u, gb, ALU.mult).then_inc(gated, 1)
                        v.wait_ge(gated, 2)
                        v.tensor_tensor(att, att, u, ALU.add).then_inc(added, 1)

        def residual_evac(eng, i, b, ps):
            c = at(i * 8 + b * 4, 4)
            return eng.tensor_tensor(xt[:, c, :], ps, xt[:, c, :], ALU.add)

        def up_stage(name, half, ff, raw):
            s = S[name]
            def blocks_before(i, b):
                return i * 2 + (8 * half + b + 1)
            def rectify(act, i, b):
                block_done(act, s, i, b)
                act.activation(raw[:, b], gp[:, b], ACT.Relu).then_inc(pair_evacuated[b], 1)
                act.wait_ge(ff_squared, blocks_before(i, b))
                act.activation(ff[:, 0, at(i * 8 + b * 4, 4), :], raw[:, b], ACT.Copy).then_inc(ff_high_split, 1)
            def square(v, i, b):
                v.wait_ge(pair_evacuated[b], i + (s.block0 // 2 + 2))
                v.tensor_tensor(raw[:, b], raw[:, b], raw[:, b], ALU.mult).then_inc(ff_squared, 1)
                v.wait_ge(ff_high_split, blocks_before(i, b))
                v.tensor_tensor(ff[:, 1, at(i * 8 + b * 4, 4), :], raw[:, b],
                                ff[:, 0, at(i * 8 + b * 4, 4), :].bitcast(F32), ALU.subtract)
            with nc.Block() as block:
                @block.sync
                def _(sp):
                    load_section(sp, s)

                @block.tensor
                def _(pe):
                    multiply_section(pe, s, x_hi, x_lo)

                @block.scalar
                def _(act):
                    split_section(act, s, split_high, rectify)

                @block.vector
                def _(v):
                    split_section(v, s, split_low, square)

        def feed_forward(block_name):
            ff, raw = new_phase(("ff_parts", [P, 2, 32, TOK], F32R), ("ff_raw", [P, 2, 4, TOK], F32))
            xs = (lambda b, c: ff[:, 0, c, :], lambda b, c: ff[:, 1, c, :])
            for n in range(2):
                up_stage(f"up{block_name}_{n}", 2 * (block_name == "3") + n, ff, raw)
                gemm_stage(f"down{block_name}_{n}", residual_evac, "vector", x=xs)
            arena_box[0], = new_phase(("arena", [P, ARENA], F32))
        WINDOWS = (2, 4, 8, 16)
        negd = consts[:, 0:256]
        count = consts[:, 256:512]
        slopes = consts[:, 512:520]
        dist = consts[:, 520:776]

        def tables3_stage():
            disti = variance_t[:, :].bitcast(I32)
            with ExitStack() as e:
                made, done = local(e, "distances"), local(e, "tables")
                with nc.Block() as block:
                    @block.gpsimd
                    def _(pool):
                        pool.iota(disti, [[1, TOK]], base=-127, channel_multiplier=1).then_inc(made, 1)
                        for n in range(8):
                            pool.wait_ge(made, n + 1)
                            pool.memset(slopes[:, n:n + 1], 2.0 ** (-8.0 * (n + 1) / 8)).then_inc(made, 1)
                        pool.wait_ge(done, 10)
                        pool.affine_select(out=negd, in_=negd, compare_op=ALU.is_ge, fill=-1.0e33, base=-127,
                                           pattern=[[1, TOK]], channel_multiplier=1).then_inc(made, 1)

                    @block.vector
                    def _(v):
                        n = 0
                        def did(ins):
                            nonlocal n
                            n += 1
                            ins.then_inc(done, 1)
                            v.wait_ge(done, n)
                        m = variance[:, :].bitcast(I32)
                        f = rstd[:, :]
                        v.wait_ge(made, 9)
                        did(v.tensor_copy(dist, disti))
                        did(v.tensor_scalar(count, dist, 128.5, None, ALU.is_lt))
                        for mask in (3, 15):
                            did(v.tensor_scalar(m, disti, mask, None, ALU.bitwise_and))
                            did(v.tensor_scalar(f, m, 0, None, ALU.is_equal))
                            did(v.tensor_tensor(count, count, f, ALU.add))
                        did(v.tensor_scalar(f, count, 0.5, -1.0e33, ALU.is_lt, ALU.mult))
                        did(v.tensor_tensor(negd, f, dist, ALU.subtract))

        def pool_stage():
            u, d = area(A0, 32), area(16400, BC)
            w = arena[:, 18448:20496].rearrange("p (g k n) -> p g k n", g=4, k=2)
            yp = area(20496, BC)
            part = area(22544, 4)
            inv = area(23568, 4)
            with ExitStack() as e:
                loaded, made, summed, diffed, mixed, scaled = (
                    local(e, x) for x in ("pool_loaded", "counts_made", "window_sums", "diffed", "mixed", "scaled"))
                with nc.Block() as block:
                    @block.sync
                    def _(sp):
                        for g in range(4):
                            sp.dma_start(w[:, g], I["pool_w_3"][0, g].rearrange("(k p) n -> p k n", p=P)).then_inc(loaded, 16)
                        sp.wait_ge(loaded, 64)

                    @block.gpsimd
                    def _(pool):
                        n = 0
                        for g, win in enumerate(WINDOWS):
                            pool.memset(inv[:, g, win - 1:], 1.0 / win).then_inc(made, 1)
                            n += 1
                            pool.wait_ge(made, n)
                            for t in range(win - 1):
                                pool.memset(inv[:, g, t:t + 1], 1.0 / (t + 1)).then_inc(made, 1)
                                n += 1
                                pool.wait_ge(made, n)

                    @block.vector
                    def _(v):
                        n = 0
                        def did(ins):
                            nonlocal n
                            n += 1
                            ins.then_inc(summed, 1)
                            v.wait_ge(summed, n)
                        v.wait_ge(made, sum(WINDOWS))
                        for g, win in enumerate(WINDOWS):
                            src = u[:, 2 * g:2 * g + 2, :]
                            w0, k = src, 1
                            while k < win:
                                dst = part[:, 0:2, :] if k in (1, 4) else part[:, 2:4, :]
                                did(v.tensor_copy(dst[:, :, 0:k], w0[:, :, 0:k]))
                                did(v.tensor_tensor(dst[:, :, k:], w0[:, :, k:], w0[:, :, 0:TOK - k], ALU.add))
                                w0, k = dst, 2 * k
                            did(v.tensor_tensor(w0, w0, inv[:, g:g + 1, :].to_broadcast([P, 2, TOK]), ALU.mult))
                            ins = v.tensor_tensor(d[:, 2 * g:2 * g + 2, :], w0, src, ALU.subtract)
                            ins.then_inc(diffed, 1)
                            v.wait_ge(diffed, g + 1)

                    @block.tensor
                    def _(pe):
                        pe.wait_ge(loaded, 64)
                        for g in range(4):
                            pe.wait_ge(diffed, g + 1)
                            for j in range(2):
                                for k in range(2):
                                    m = pe.matmul(sp_[:, g, j * TOK:(j + 1) * TOK], w[:, g, k, j * P:(j + 1) * P], d[:, 2 * g + k, :],
                                                  start=(k == 0), stop=(k == 1), skip_group_check=True)
                            m.then_inc(mixed, 1)

                    @block.scalar
                    def _(act):
                        for g in range(4):
                            act.wait_ge(mixed, g + 1)
                            for j in range(2):
                                act.activation(yp[:, 2 * g + j, :], sp_[:, g, j * TOK:(j + 1) * TOK], ACT.Copy,
                                               scale=par("pscale", 2 * g + j)).then_inc(scaled, 1)

        def attention3_stage():
            def logits(v, dv, g, r, head, ps, sc):
                v.scalar_tensor_tensor(sc[:, 0:128], negd[:, 0:128], slopes[:, at(head, 1)], ps[:, 0:128], ALU.mult, ALU.add)
                dv.did(v.scalar_tensor_tensor(sc[:, 128:384], negd, slopes[:, at(head, 1)], ps[:, 128:384], ALU.mult, ALU.add), f"log{r}_0")
            def weigh(v, g, sc, small):
                v.scalar_tensor_tensor(sc[:, 0:128], sc[:, 0:128], 1.0, count[:, 0:128], ALU.mult, ALU.mult, accum_out=small[:, 4:5])
                v.scalar_tensor_tensor(sc[:, 128:384], sc[:, 128:384], 1.0, count, ALU.mult, ALU.mult, accum_out=small[:, 5:6]).then_inc(weighed, 1)
                v.wait_ge(weighed, g + 1)
            weighed = sem("weighed")
            in3 = area(A0, 32)
            attention_stage(in3[:, 8:16, :], lambda g: in3[:, at(g + 16, 1), :], lambda g: in3[:, at(g + 24, 1), :],
                            8, 1, 128 ** -0.5, logits, weigh, 1, 26640)

        def store_stage():
            rowsb = arena[:, A0:A0 + 4096].rearrange("p (t c) -> p t c", t=2)
            with ExitStack() as e:
                turned, copied, stored = local(e, "turned"), local(e, "copied"), local(e, "stored")
                with nc.Block() as block:
                    @block.tensor
                    def _(pe):
                        for g in range(8):
                            if g >= 4:
                                pe.wait_ge(copied, g - 3)
                            for n in range(4):
                                m = pe.transpose(sp_[:, g % 4, n * P:(n + 1) * P],
                                                 xt[:, (g % 4) * 4 + n, (g // 4) * P:(g // 4 + 1) * P], ident[:, :])
                            m.then_inc(turned, 1)

                    @block.vector
                    def _(v):
                        for g in range(8):
                            v.wait_ge(turned, g + 1)
                            v.tensor_copy(rowsb[:, g // 4, (g % 4) * 512:(g % 4 + 1) * 512], sp_[:, g % 4, :]).then_inc(copied, 1)

                    @block.sync
                    def _(sp):
                        for t in range(2):
                            sp.wait_ge(copied, 4 * t + 4)
                            sp.dma_start(out_dram[0, t * P:(t + 1) * P, :], rowsb[:, t, :]).then_inc(stored, 16)
                        sp.wait_ge(stored, 32)
        stages = []
        def copy_pad(dst):
            def evac(eng, i, b, ps):
                return eng.activation(dst[:, at(i * 8 + b * 4, 4), 1:TOK + 1], ps, ACT.Copy)
            return evac
        def pad_stage():
            with nc.Block() as block:
                @block.gpsimd
                def _(pool):
                    pool.memset(area(A0, 24, TOK + 1)[:, :, 0:1], 0.0)
        h1 = hp[:, :, 1:TOK + 1]
        arena_box[0], = new_phase(("arena", [P, ARENA], F32))
        stages += [("start", start_stage), ("masks", masks_stage),
                   ("norm", lambda: norm_stage(xt[:, :, :], DC, "pre", hp[:, :, 1:TOK + 1])),
                   ("lora", lora_stage), ("pad", pad_stage),
                   ("split1", lambda: split_stage((h1, 0))), ("rkv", lambda: gemm_stage("rkv", copy_pad(area(A0, 24, TOK + 1)))),
                   ("mix", mix_stage)]
        def evac_silu(dst):
            def evac(eng, i, b, ps):
                return eng.activation(dst[:, at(i * 8 + b * 4, 4), :], ps, ACT.Silu)
            return evac
        stages += [("zr", lambda: gemm_stage("zr", evac_silu(area(A0, 8)))),
                   ("qkv", lambda: gemm_stage("qkv", copy_to(area(A0 + 2048, 24)))),
                   ("za", lambda: gemm_stage("za", evac_silu(area(A0 + 8192, 8)))),
                   ("att1", attention1_stage), ("rwkv", rwkv_stage),
                   ("gates", lambda: gemm_stage("gates", gates_evac)),
                   ("splitb", lambda: split_stage((area(A0, BC), 0), (area(A0 + 2048, BC), 8))),
                   ("branch", branch_stage),
                   ("splito", lambda: split_stage((area(12304, DC), 0))),
                   ("out", lambda: gemm_stage("out", copy_to(area(4096, DC)))),
                   ("post", lambda: norm_stage(area(4096, DC), DC, "post", area(4096, DC), add_to=xt[:, :, :]))]
        def evac_as(dst, func):
            def evac(eng, i, b, ps):
                return eng.activation(dst[:, at(i * 8 + b * 4, 4), :], ps, func)
            return evac
        stages += [("norm1", lambda: norm_stage(xt[:, :, :], DC, "norm1", h)),
                   ("split2", lambda: split_stage((h, 0))), ("qkv2", lambda: gemm_stage("qkv2", copy_to(area(A0, 24)))),
                   ("index2", lambda: gemm_stage("index2", index_evac, tiles=(4, 2))), ("bias2", bias2_stage), ("select", select_stage),
                   ("att2", attention2_stage),
                   ("uv2", lambda: gemm_stage("uv2", evac_as(area(15888, 32), ACT.Gelu_apprx_tanh))),
                   ("sgu", sgu_stage),
                   ("gates2", lambda: gemm_stage("gates2", evac_as(area(19984, 32), ACT.Sigmoid))),
                   ("merge2", merge2_stage),
                   ("splito2", lambda: split_stage((area(A0, DC), 0))), ("out2", lambda: gemm_stage("out2", residual_evac, "vector")),
                   ("norm2", lambda: norm_stage(xt[:, :, :], DC, "norm2", h)),
                   ("split_ff2", lambda: split_stage((h, 0))), ("down2_1", lambda: feed_forward("2")),
                   ("final2", lambda: norm_stage(xt[:, :, :], DC, "final2", xt[:, :, :]))]
        stages += [("mix3", lambda: norm_stage(xt[:, :, :], DC, "mix3", h)),
                   ("split3", lambda: split_stage((h, 0))), ("in3", lambda: gemm_stage("in3", copy_to(area(A0, 32)))),
                   ("tables3", tables3_stage), ("pool", pool_stage), ("att3", attention3_stage),
                   ("pout", lambda: norm_stage(area(20496, BC), BC, "pout", area(4096, BC), scratch=26640)),
                   ("aout", lambda: norm_stage(area(A0 + 2048, BC), BC, "aout", area(6144, BC), scratch=26640)),
                   ("splito3", lambda: split_stage((h, 0))), ("out3", lambda: gemm_stage("out3", residual_evac, "vector")),
                   ("mlp3", lambda: norm_stage(xt[:, :, :], DC, "mlp3", h)),
                   ("split_ff3", lambda: split_stage((h, 0))), ("down3_1", lambda: feed_forward("3")),
                   ("final3", lambda: norm_stage(xt[:, :, :], DC, "final3", xt[:, :, :])), ("end", store_stage)]
        seen = 0
        for name, f in stages:
            f()
            if name in S:
                seen = order.index(S[name]) + 1
            if name == upto and seen < len(order):
                with nc.Block() as block:
                    @block.sync
                    def _(sp):
                        for k in range(SLOTS):
                            sp.wait_ge(unit_loaded[k], 16 * (order[seen].unit0 // 4 + 1))
                break


def kernel(**inputs):
    import concourse.bacc as bacc
    from concourse.bass_utils import run_bass_kernel_spmd

    nc = bacc.Bacc("TRN2", target_bir_lowering=False, num_devices=1)
    arrays, aps = {}, {}
    for name, a in inputs.items():
        arrays[name] = np.ascontiguousarray(a)
        aps[name] = nc.dram_tensor(name, arrays[name].shape, mybir.dt.from_np(arrays[name].dtype), kind="ExternalInput").ap()
    out = nc.dram_tensor("out", (1, TOK, D), F32, kind="ExternalOutput").ap()
    build_kernel(nc, aps, out)
    return run_bass_kernel_spmd(nc, [arrays], core_ids=[0]).results[0]["out"]
```
